# Optimizing a Trainium2 kernel written in Bass

```python
import jax, jax.numpy as jnp
from jax import lax
import numpy as np

D_MODEL = 1024
BATCH = 1
SEQ = 1024
DEPTH = 1

CHUNK = 64
Q_BLOCK = 128
SGU_CHUNK = 128
HEAD_DIM = 64
D_ATTN = D_MODEL // 2
N_ATTN_HEADS = D_ATTN // HEAD_DIM
D_SGU = D_MODEL // 2
SGU_GROUP_DIM = 64
N_SGU_GROUPS = D_SGU // SGU_GROUP_DIM
D_MIX = D_ATTN + D_SGU
D_IN = 3 * D_ATTN + N_ATTN_HEADS + 2 * D_SGU
D_FF = -(-8 * D_MODEL // (3 * 256)) * 256
EPS = 1e-6


def rms_norm(x, g):
    xf = x.astype(jnp.float32)
    y = xf * lax.rsqrt(jnp.mean(xf * xf, axis=-1, keepdims=True) + EPS)
    return (y * g.astype(jnp.float32)).astype(x.dtype)

def layer_norm(x, g, b):
    xf = x.astype(jnp.float32)
    mu = jnp.mean(xf, axis=-1, keepdims=True)
    xc = xf - mu
    y = xc * lax.rsqrt(jnp.mean(xc * xc, axis=-1, keepdims=True) + EPS)
    return (y * g.astype(jnp.float32) + b.astype(jnp.float32)).astype(x.dtype)

def forgetting_attention(q, k, v, log_f):
    B, S, H, Dh = q.shape
    nb = S // Q_BLOCK
    c_bhs = jnp.cumsum(log_f, axis=1).transpose(0, 2, 1)
    q_blocks = q.reshape(B, nb, Q_BLOCK, H, Dh).transpose(1, 0, 2, 3, 4)
    cq_blocks = c_bhs.reshape(B, H, nb, Q_BLOCK).transpose(2, 0, 1, 3)
    starts = jnp.arange(nb, dtype=jnp.int32) * Q_BLOCK
    key_pos = jnp.arange(S, dtype=jnp.int32)
    scale = Dh ** -0.5

    def one_block(args):
        qb, cqb, start = args
        s = jnp.einsum('bqhd,bkhd->bhqk', qb, k).astype(jnp.float32) * scale
        s = s + cqb[..., :, None] - c_bhs[..., None, :]
        q_pos = start + jnp.arange(Q_BLOCK, dtype=jnp.int32)
        causal = key_pos[None, :] <= q_pos[:, None]
        s = jnp.where(causal, s, -jnp.inf)
        p = jax.nn.softmax(s, axis=-1).astype(v.dtype)
        return jnp.einsum('bhqk,bkhd->bqhd', p, v)

    out = lax.map(one_block, (q_blocks, cq_blocks, starts))
    return out.transpose(1, 0, 2, 3, 4).reshape(B, S, H * Dh)

def spatial_gating(z, ln_g, ln_b, w_s, b_s):
    B, S, _ = z.shape
    zu, zv = jnp.split(z, 2, axis=-1)
    zv = layer_norm(zv, ln_g, ln_b)
    nc = S // SGU_CHUNK
    zv = zv.reshape(B, nc, SGU_CHUNK, N_SGU_GROUPS, SGU_GROUP_DIM)
    pos = jnp.arange(SGU_CHUNK, dtype=jnp.int32) // CHUNK
    mask = (pos[None, :] <= pos[:, None]).astype(w_s.dtype)
    w = w_s * mask[None]
    mixed = jnp.einsum('gij,bcjgd->bcigd', w, zv) + b_s.T[None, None, :, :, None]
    return zu * mixed.reshape(B, S, D_SGU)

def first_inputs(seed: int = 0) -> dict:
    key = jax.random.key(seed)
    ks = jax.random.split(key, 14)
    f32 = jnp.float32
    nrm = lambda k, shape, s: jax.random.normal(k, shape, f32) * s
    head_bias = jnp.linspace(1.0, 5.0, N_ATTN_HEADS, dtype=f32)
    return {
        'x': jax.random.normal(ks[0], (BATCH, SEQ, D_MODEL), f32),
        'mix_norm_g': 1.0 + nrm(ks[1], (DEPTH, D_MODEL), 0.05),
        'w_in': nrm(ks[2], (DEPTH, D_MODEL, D_IN), D_MODEL ** -0.5),
        'b_f': head_bias[None, :] + nrm(ks[3], (DEPTH, N_ATTN_HEADS), 0.1),
        'sgu_ln_g': 1.0 + nrm(ks[4], (DEPTH, D_SGU), 0.05),
        'sgu_ln_b': nrm(ks[5], (DEPTH, D_SGU), 0.02),
        'w_s': nrm(ks[6], (DEPTH, N_SGU_GROUPS, SGU_CHUNK, SGU_CHUNK), 0.5 * SGU_CHUNK ** -0.5),
        'b_s': 1.0 + nrm(ks[7], (DEPTH, N_SGU_GROUPS, SGU_CHUNK), 0.1),
        'out_norm_g': 1.0 + nrm(ks[8], (DEPTH, D_MIX), 0.05),
        'w_out': nrm(ks[9], (DEPTH, D_MIX, D_MODEL), D_MIX ** -0.5),
        'ffn_norm_g': 1.0 + nrm(ks[10], (DEPTH, D_MODEL), 0.05),
        'w_gate_up': nrm(ks[11], (DEPTH, D_MODEL, 2 * D_FF), D_MODEL ** -0.5),
        'w_down': nrm(ks[12], (DEPTH, D_FF, D_MODEL), D_FF ** -0.5),
        'final_norm_g': 1.0 + nrm(ks[13], (D_MODEL,), 0.05),
    }

def first_block(x, mix_norm_g, w_in, b_f, sgu_ln_g, sgu_ln_b, w_s, b_s, out_norm_g, w_out,
              ffn_norm_g, w_gate_up, w_down, final_norm_g):
    B, S, _ = x.shape
    for l in range(DEPTH):
        xn = rms_norm(x, mix_norm_g[l])
        h = xn @ w_in[l]
        q, k, v, f_logit, z = jnp.split(
            h, [D_ATTN, 2 * D_ATTN, 3 * D_ATTN, 3 * D_ATTN + N_ATTN_HEADS], axis=-1)
        q = q.reshape(B, S, N_ATTN_HEADS, HEAD_DIM)
        k = k.reshape(B, S, N_ATTN_HEADS, HEAD_DIM)
        v = v.reshape(B, S, N_ATTN_HEADS, HEAD_DIM)
        log_f = jax.nn.log_sigmoid(f_logit.astype(jnp.float32) + b_f[l].astype(jnp.float32))
        attn = forgetting_attention(q, k, v, log_f)
        sgu = spatial_gating(jax.nn.gelu(z, approximate=False),
                             sgu_ln_g[l], sgu_ln_b[l], w_s[l], b_s[l])
        merged = jnp.concatenate(
            [rms_norm(attn, out_norm_g[l, :D_ATTN]), rms_norm(sgu, out_norm_g[l, D_ATTN:])], axis=-1)
        x = x + merged @ w_out[l]
        xn = rms_norm(x, ffn_norm_g[l])
        gate, up = jnp.split(xn @ w_gate_up[l], 2, axis=-1)
        x = x + (jax.nn.silu(gate) * up) @ w_down[l]
    return rms_norm(x, final_norm_g)


D_MIX_2 = D_MODEL
SC_WIDTH = D_MIX_2 // 4
SC_GROUPS = 4
SC_KERNEL = 3
GDN_WIDTH = D_MIX_2 // 2
GDN_HEADS = 4
GDN_HEAD_DIM = GDN_WIDTH // GDN_HEADS
GDN_CONV = 4
GDN_CHUNK = 64
SB_WIDTH = D_MIX_2 - SC_WIDTH - GDN_WIDTH
SB_HEADS = 4
SB_HEAD_DIM = SB_WIDTH // SB_HEADS
SB_BLOCK = 128
D_FF_2 = 256 * ((8 * D_MODEL // 3 + 255) // 256)
FFN_CONV = 3
NORM_EPS = 1e-6
SPLIT_SIZES = (SC_WIDTH, SC_WIDTH, SC_WIDTH,
               GDN_WIDTH, GDN_WIDTH, GDN_WIDTH, GDN_WIDTH, GDN_HEADS, GDN_HEADS,
               SB_WIDTH, SB_WIDTH, SB_WIDTH)
D_IN_PROJ = 3 * SC_WIDTH + 4 * GDN_WIDTH + 2 * GDN_HEADS + 3 * SB_WIDTH


def rmsnorm(x, w):
    xf = x.astype(jnp.float32)
    y = xf * lax.rsqrt(jnp.mean(xf * xf, axis=-1, keepdims=True) + NORM_EPS) * w.astype(jnp.float32)
    return y.astype(x.dtype)

def l2norm(x):
    xf = x.astype(jnp.float32)
    return xf * lax.rsqrt(jnp.sum(xf * xf, axis=-1, keepdims=True) + NORM_EPS)

def causal_dwconv(x, w):
    K, C = w.shape
    return lax.conv_general_dilated(
        x, w[:, None, :].astype(x.dtype), window_strides=(1,), padding=[(K - 1, 0)],
        dimension_numbers=('NWC', 'WIO', 'NWC'), feature_group_count=C)

def split_columns(proj):
    points = [int(p) for p in np.cumsum(np.array(SPLIT_SIZES))[:-1]]
    return jnp.split(proj, points, axis=-1)

def gated_delta_rule_chunked(q, k, v, g, beta):
    f32 = jnp.float32
    Bsz, L, H, Dk = q.shape
    Dv = v.shape[-1]
    N = L // GDN_CHUNK

    def to_chunks(t):
        t = t.reshape((Bsz, N, GDN_CHUNK, H) + t.shape[3:])
        return jnp.moveaxis(t, 3, 1)

    q = to_chunks(q.astype(f32)) * (Dk ** -0.5)
    k = to_chunks(k.astype(f32))
    v = to_chunks(v.astype(f32))
    beta = to_chunks(beta.astype(f32))
    g = jnp.cumsum(to_chunks(g.astype(f32)), axis=-1)
    idx = jnp.arange(GDN_CHUNK)
    causal = idx[:, None] >= idx[None, :]
    strict = idx[:, None] > idx[None, :]
    decay = jnp.exp(jnp.where(causal, g[..., :, None] - g[..., None, :], -jnp.inf))
    k_beta = k * beta[..., None]
    lower = jnp.where(strict, jnp.einsum('bhncd,bhnsd->bhncs', k_beta, k) * decay, 0.0)
    lhs = lower + jnp.eye(GDN_CHUNK, dtype=f32)
    rhs = jnp.concatenate([v * beta[..., None], k_beta * jnp.exp(g)[..., None]], axis=-1)
    sol = lax.linalg.triangular_solve(lhs, rhs, left_side=True, lower=True, unit_diagonal=True)
    u, w = sol[..., :Dv], sol[..., Dv:]
    attn_intra = jnp.where(causal, jnp.einsum('bhncd,bhnsd->bhncs', q, k) * decay, 0.0)

    def step(S, inp):
        q_i, k_i, u_i, w_i, g_i, a_i = inp
        v_new = u_i - jnp.einsum('bhcd,bhde->bhce', w_i, S)
        o = jnp.einsum('bhcd,bhde->bhce', q_i * jnp.exp(g_i)[..., None], S) + \
            jnp.einsum('bhcs,bhse->bhce', a_i, v_new)
        g_last = g_i[..., -1]
        S = S * jnp.exp(g_last)[..., None, None] + \
            jnp.einsum('bhcd,bhce->bhde', k_i * jnp.exp(g_last[..., None] - g_i)[..., None], v_new)
        return S, o

    xs = tuple(jnp.moveaxis(t, 2, 0) for t in (q, k, u, w, g, attn_intra))
    S0 = jnp.zeros((Bsz, H, Dk, Dv), f32)
    _, outs = lax.scan(step, S0, xs)
    return outs.transpose(1, 0, 3, 2, 4).reshape(Bsz, L, H, Dv)

def stick_breaking_attention(q, k, v):
    L, D = q.shape[1], q.shape[-1]
    scale = D ** -0.5
    q_off = jnp.arange(SB_BLOCK)
    outs = []
    for blk in range(L // SB_BLOCK):
        start, end = blk * SB_BLOCK, (blk + 1) * SB_BLOCK
        z = jnp.einsum('bqhd,bkhd->bhqk', q[:, start:end], k[:, :end]).astype(jnp.float32) * scale
        strict = jnp.arange(end)[None, :] < (start + q_off)[:, None]
        log_beta = jax.nn.log_sigmoid(z)
        log_one_minus = jnp.where(strict, jax.nn.log_sigmoid(-z), 0.0)
        tail = lax.cumsum(log_one_minus, axis=3, reverse=True) - log_one_minus
        A = jnp.where(strict, jnp.exp(log_beta + tail), 0.0)
        outs.append(jnp.einsum('bhqk,bkhd->bqhd', A.astype(v.dtype), v[:, :end]))
    return jnp.concatenate(outs, axis=1)

def second_inputs(seed: int = 0) -> dict:
    key = jax.random.key(seed)
    ks = jax.random.split(key, 16)
    f32 = jnp.float32
    nrm = lambda k, shape: jax.random.normal(k, shape, f32)
    dt = jnp.exp(jax.random.uniform(ks[6], (DEPTH, GDN_HEADS), f32, np.log(1e-3), np.log(1e-1)))
    return {
        'x': nrm(ks[0], (BATCH, SEQ, D_MODEL)),
        'w_norm_mix': 1.0 + 0.02 * nrm(ks[1], (DEPTH, D_MODEL)),
        'w_mix_in': nrm(ks[2], (DEPTH, D_MODEL, D_IN_PROJ)) * D_MODEL ** -0.5,
        'w_sconv': nrm(ks[3], (DEPTH, SC_KERNEL, SC_WIDTH)) * SC_KERNEL ** -0.5,
        'w_gdn_conv': nrm(ks[4], (DEPTH, GDN_CONV, 3 * GDN_WIDTH)) * GDN_CONV ** -0.5,
        'gdn_a_log': jnp.log(jax.random.uniform(ks[5], (DEPTH, GDN_HEADS), f32, 1.0, 16.0)),
        'gdn_dt_bias': dt + jnp.log(-jnp.expm1(-dt)),
        'w_gdn_norm': 1.0 + 0.02 * nrm(ks[7], (DEPTH, GDN_HEAD_DIM)),
        'w_mix_out': nrm(ks[8], (DEPTH, D_MIX_2, D_MODEL)) * D_MIX_2 ** -0.5,
        'w_norm_ffn': 1.0 + 0.02 * nrm(ks[9], (DEPTH, D_MODEL)),
        'w_ffn_up': nrm(ks[10], (DEPTH, D_MODEL, 2 * D_FF_2)) * D_MODEL ** -0.5,
        'w_ffn_conv': nrm(ks[11], (DEPTH, FFN_CONV, 2 * D_FF_2)) * FFN_CONV ** -0.5,
        'w_ffn_down': nrm(ks[12], (DEPTH, D_FF_2, D_MODEL)) * D_FF_2 ** -0.5,
        'w_norm_final': 1.0 + 0.02 * nrm(ks[13], (D_MODEL,)),
    }

def second_block(x, w_norm_mix, w_mix_in, w_sconv, w_gdn_conv, gdn_a_log, gdn_dt_bias, w_gdn_norm,
              w_mix_out, w_norm_ffn, w_ffn_up, w_ffn_conv, w_ffn_down, w_norm_final):
    Bsz, L, _ = x.shape
    f32 = jnp.float32
    for l in range(DEPTH):
        h = rmsnorm(x, w_norm_mix[l])
        proj = h @ w_mix_in[l]
        (sc_b, sc_c, sc_h, gq, gk, gv, gz, ga, gb, sq, sk, sv) = split_columns(proj)

        y_sc = sc_b * causal_dwconv(sc_c * sc_h, w_sconv[l])

        qkv = jax.nn.silu(causal_dwconv(jnp.concatenate([gq, gk, gv], axis=-1), w_gdn_conv[l]))
        gq, gk, gv = jnp.split(qkv, 3, axis=-1)
        heads = lambda t: t.reshape(Bsz, L, GDN_HEADS, GDN_HEAD_DIM)
        beta = jax.nn.sigmoid(gb.astype(f32))
        g = -jnp.exp(gdn_a_log[l].astype(f32)) * jax.nn.softplus(ga.astype(f32) + gdn_dt_bias[l].astype(f32))
        o = gated_delta_rule_chunked(l2norm(heads(gq)), l2norm(heads(gk)), heads(gv), g, beta)
        o = rmsnorm(o, w_gdn_norm[l]) * jax.nn.silu(heads(gz).astype(f32))
        y_gdn = o.reshape(Bsz, L, GDN_WIDTH).astype(x.dtype)

        sb_heads = lambda t: t.reshape(Bsz, L, SB_HEADS, SB_HEAD_DIM)
        y_sb = stick_breaking_attention(sb_heads(sq), sb_heads(sk), sb_heads(sv)).reshape(Bsz, L, SB_WIDTH)

        x = x + jnp.concatenate([y_sc, y_gdn, y_sb], axis=-1) @ w_mix_out[l]

        h = rmsnorm(x, w_norm_ffn[l])
        u = causal_dwconv(h @ w_ffn_up[l], w_ffn_conv[l])
        gate, val = jnp.split(u, 2, axis=-1)
        x = x + (jax.nn.silu(gate) * val) @ w_ffn_down[l]
    return rmsnorm(x, w_norm_final)


def setup_inputs(seed=0):
    out = dict(first_inputs(seed))
    for name, value in second_inputs(seed + 1).items():
        if name != "x":
            out[name + "_2"] = value
    return out


def reference(
    x, mix_norm_g, w_in, b_f, sgu_ln_g, sgu_ln_b, w_s, b_s, out_norm_g, w_out, ffn_norm_g,
    w_gate_up, w_down, final_norm_g, w_norm_mix_2, w_mix_in_2, w_sconv_2, w_gdn_conv_2,
    gdn_a_log_2, gdn_dt_bias_2, w_gdn_norm_2, w_mix_out_2, w_norm_ffn_2, w_ffn_up_2,
    w_ffn_conv_2, w_ffn_down_2, w_norm_final_2,
):
    x = first_block(
        x, mix_norm_g, w_in, b_f, sgu_ln_g, sgu_ln_b, w_s, b_s, out_norm_g, w_out, ffn_norm_g,
        w_gate_up, w_down, final_norm_g,
    )
    return second_block(
        x, w_norm_mix_2, w_mix_in_2, w_sconv_2, w_gdn_conv_2, gdn_a_log_2, gdn_dt_bias_2,
        w_gdn_norm_2, w_mix_out_2, w_norm_ffn_2, w_ffn_up_2, w_ffn_conv_2, w_ffn_down_2,
        w_norm_final_2,
    )


_drawn_inputs = setup_inputs


def setup_inputs(seed=0):
    import zlib

    import numpy as np

    out = dict(_drawn_inputs(seed))
    spreads = {}
    factors = {'sgu_ln_g': 3.972,
     'sgu_ln_b': 8.0,
     'w_gdn_norm_2': 8.0,
     'w_norm_ffn_2': 4.312,
     'w_norm_final_2': 2.784}
    for name, (base, spread) in spreads.items():
        noise = np.random.default_rng([zlib.crc32(name.encode()), seed]).standard_normal(out[name].shape)
        drawn = base * np.exp(spread * noise) if base else spread * noise
        out[name] = __import__('jax').numpy.asarray(drawn.astype(out[name].dtype))
    for name, factor in factors.items():
        out[name] = (out[name] * factor).astype(out[name].dtype)
    return out
```

```python
from contextlib import ExitStack

import concourse.bass as bass
from concourse import mybir

ALU = mybir.AluOpType
ACT = mybir.ActivationFunctionType
AX = mybir.AxisListType.X
F32 = mybir.dt.float32
F32R = mybir.dt.float32r

P = 128
S = 1024
D = 1024
NT = S // P
KD = D // P
HALF = 512
NB = 8
EPS = 1e-6
NEG = -1e30
KB = 1024
BASE = 17 * KB
RING = 4
FF = 2816
FI = FF // 256
HA = 8
DH = 64
D_IN = 2568


class Machine:
    pass


def setup(nc, ctx, a):
    m = Machine()
    m.nc, m.ctx, m.a = nc, ctx, a
    m.at = lambda name, shape, off, dt=F32: nc.alloc_sbuf_tensor_at(name, shape, dt, offset=BASE + int(off * KB))
    m.psum = [ctx.enter_context(nc.psum_tensor(f"bank{b}", [P, HALF], F32)) for b in range(NB)]
    m.xt_hi = m.at("xt_hi", [P, KD, S], 32, F32R)
    m.xt_lo = m.at("xt_lo", [P, KD, S], 64, F32R)
    m.w_raw = m.at("w_raw", [P, RING, HALF], 96)
    m.w_hi = m.at("w_hi", [P, RING, HALF], 104, F32R)
    m.w_lo = m.at("w_lo", [P, RING, HALF], 112, F32R)
    m.ident = m.at("ident", [P, P], 200)
    m.causal = m.at("causal", [P, P], 200.5)
    m.sel = m.at("sel", [8, 8, P], 201)
    m.cols = m.at("cols", [P, 240], 205)
    m.zero = m.at("zero", [P, 1], 206)
    m.eps = m.at("eps", [P, 1], 206.0625)
    m.loaded = [ctx.enter_context(nc.semaphore(f"slice_loaded{u}")) for u in range(RING)]
    m.hi_done = ctx.enter_context(nc.semaphore("slice_hi_done"))
    m.split = ctx.enter_context(nc.semaphore("slice_split"))
    m.used = ctx.enter_context(nc.semaphore("slice_used"))
    m.slices = 0
    m.norms = m.turns = 0
    m.sem = lambda name: ctx.enter_context(nc.semaphore(name))
    m.bank_done = m.sem("bank_done")
    m.chunks = 0
    m.norm_square_a, m.norm_square_d = m.sem("norm_square_act"), m.sem("norm_square_dve")
    m.squares = {"act": 0, "dve": 0}
    m.norm_rstd = m.sem("norm_rstd")
    m.norm_scaled = m.sem("norm_scaled")
    m.norm_turned = m.sem("norm_turned")
    m.norm_hi = m.sem("norm_hi")
    m.norm_lo = m.sem("norm_lo")
    m.dve_step = m.sem("dve_step")
    m.act_step = m.sem("act_step")
    m.dve_steps = m.act_steps = 0
    return m


ROW = {"mix_norm_g": 0, "out_norm_g": 8, "ffn_norm_g": 16, "w_norm_mix_2": 24, "w_norm_ffn_2": 32,
       "b_s": 40, "w_sconv_2": 48, "w_gdn_conv_2": 54, "w_gdn_norm_2": 102}
ROWS1 = 103
COL_FFC = ROWS1


def load_slices(m, sp, base, first, count, source):
    with sp.Fori(1 if first == 0 else 0, count // RING) as j:
        for u in range(RING):
            sp.wait_ge(m.split, base + first + RING * j + u + 1 - RING)
            dst, src = source(j, u)
            sp.dma_start(dst, src).then_inc(m.loaded[u], 16)


def load_first(m, sp, base, source):
    for u in range(RING):
        if base:
            sp.wait_ge(m.split, base + u + 1 - RING)
        dst, src = source(u)
        sp.dma_start(dst, src).then_inc(m.loaded[u], 16)


def split_slices(m, pool, base, count, start=0):
    r0 = base // RING
    with pool.Fori(start // RING, count // RING) as j:
        for u in range(RING):
            split_slice(m, pool, base + RING * j + u, r0 + j, u, False)


def split_slice(m, pool, n, r, u, fresh):
    zeros = m.zero[:, 0:1].to_broadcast([P, HALF])
    if not fresh:
        pool.wait_ge(m.used, n + 1 - RING)
    pool.wait_ge(m.loaded[u], 16 * r + 16)
    pool.tensor_tensor(m.w_hi[:, u, :], m.w_raw[:, u, :], zeros, ALU.add).then_inc(m.hi_done, 1)
    pool.wait_ge(m.hi_done, n + 1)
    pool.tensor_tensor(m.w_lo[:, u, :], m.w_raw[:, u, :], m.w_hi[:, u, :].bitcast(F32),
                       ALU.subtract).then_inc(m.split, 1)


def split_first(m, pool, base):
    for u in range(RING):
        split_slice(m, pool, base + u, base // RING, u, base == 0)


def columns_of(m, w, col):
    return lambda u: (m.w_raw[:, u, :], w[u * P:(u + 1) * P, col:col + HALF])


def in_turn(m, eng, name):
    sem = m.dve_step if name == "dve" else m.act_step

    def step(ins):
        if name == "dve":
            m.dve_steps += 1
            n = m.dve_steps
        else:
            m.act_steps += 1
            n = m.act_steps
        ins.then_inc(sem, 1)
        eng.wait_ge(sem, n)

    return step


def chunk_products(m, pe, base, chunk, token_major, wait_bank=None):
    for k in range(KD):
        u = k % RING
        pe.wait_ge(m.split, base + k + 1)
        for b in range(NB):
            if k == 0 and wait_bank is not None:
                wait_bank(b)
            if token_major:
                col, tok = slice(0, HALF), slice(b * P, (b + 1) * P)
                pairs = [(m.xt_hi, m.w_hi), (m.xt_hi, m.w_lo), (m.xt_lo, m.w_hi)]
                pairs = [(x[:, k, tok], w[:, u, col]) for x, w in pairs]
            else:
                h, n = b // 4, b % 4
                col, tok = slice(n * P, (n + 1) * P), slice(h * HALF, (h + 1) * HALF)
                pairs = [(m.w_hi, m.xt_hi), (m.w_hi, m.xt_lo), (m.w_lo, m.xt_hi)]
                pairs = [(w[:, u, col], x[:, k, tok]) for w, x in pairs]
            for i, (lhs, rhs) in enumerate(pairs):
                mm = pe.matmul(m.psum[b][:, :], lhs, rhs, start=k == 0 and i == 0, stop=k == KD - 1 and i == 2)
            if b == NB - 1:
                mm.then_inc(m.used, 1)
            elif k == KD - 1:
                mm.then_inc(m.bank_done, 1)


def wait_chunk_bank(m, eng, base, chunk, b):
    if b == NB - 1:
        eng.wait_ge(m.used, base + KD)
    else:
        eng.wait_ge(m.bank_done, (NB - 1) * chunk + b + 1)


def square_sums(m, eng, name, src, halves, ss, junk, tiles):
    width = D // halves
    for t in tiles:
        for g in range(halves):
            x, out, acc = src(t, g * width, (g + 1) * width), junk[:, g * width:(g + 1) * width], ss[:, g * NT + t:g * NT + t + 1]
            sem = m.norm_square_a if name == "act" else m.norm_square_d
            n = m.squares[name]
            if n:
                eng.wait_ge(sem, n)
            if name == "act":
                ins = eng.activation(out, x, ACT.Square, accum_out=acc)
            else:
                ins = eng.tensor_tensor_reduce(out, x, x, 1.0, 0.0, ALU.mult, ALU.add, acc)
            ins.then_inc(sem, 1)
            m.squares[name] += 1


def inverse_rms(m, act, halves, ss, rstd, half, squares_d):
    act.wait_ge(m.norm_square_a, m.squares["act"])
    act.wait_ge(m.norm_square_d, squares_d)
    step = in_turn(m, act, "act")
    pick = lambda t: t[:, 0:halves * NT].rearrange("p (g t) -> p g t", t=NT)[:, :, 4 * half:4 * half + 4]
    step(act.activation(pick(rstd), pick(ss), ACT.Ln, scale=halves / D, bias=m.eps[:, 0:1]))
    act.activation(pick(rstd), pick(rstd), ACT.Exp, scale=-0.5).then_inc(m.norm_rstd, 1)


def norm_tiles(half, name):
    return (4 * half, 4 * half + 1) if name == "act" else (4 * half + 2, 4 * half + 3)


def norm_stage(m, src, dst, halves, gcol, scratch, first=None):
    nc = m.nc
    r, turns = m.norms, m.turns
    ss = m.at(f"ss{r}", [P, 16], scratch + 8)
    rstd = m.at(f"rstd{r}", [P, 16], scratch + 8.0625)
    junk_a, junk_d = m.at(f"junk_a{r}", [P, D], scratch), m.at(f"junk_d{r}", [P, D], scratch + 4)
    sq_d = m.squares["dve"]
    with nc.Block() as block:
        if first is not None:
            @block.sync
            def _(sp):
                load_first(m, sp, m.slices, first)

            @block.gpsimd
            def _(pool):
                split_first(m, pool, m.slices)

        @block.scalar
        def _(act):
            for half in range(2):
                square_sums(m, act, "act", src, halves, ss, junk_a, norm_tiles(half, "act"))
                inverse_rms(m, act, halves, ss, rstd, half, sq_d + 2 * halves * (half + 1))
            for i in range(2 * KD):
                h, k = i // KD, i % KD
                act.wait_ge(m.norm_turned, 16 * turns + i + 1)
                act.activation(m.xt_hi[:, k, h * HALF:(h + 1) * HALF], m.psum[i % NB][:, :], ACT.Identity,
                               scale=m.cols[:, gcol + k:gcol + k + 1]).then_inc(m.norm_hi, 1)

        @block.vector
        def _(dve):
            for half in range(2):
                square_sums(m, dve, "dve", src, halves, ss, junk_d, norm_tiles(half, "dve"))
            width = D // halves
            for t in range(NT):
                if t % 4 == 0:
                    dve.wait_ge(m.norm_rstd, 2 * r + t // 4 + 1)
                for g in range(halves):
                    ins = dve.tensor_scalar(dst(t, g * width, (g + 1) * width), src(t, g * width, (g + 1) * width),
                                            rstd[:, g * NT + t:g * NT + t + 1], None, ALU.mult)
                ins.then_inc(m.norm_scaled, 1)
            for i in range(2 * KD):
                h, k = i // KD, i % KD
                dve.wait_ge(m.norm_hi, 16 * turns + i + 1)
                tok = slice(h * HALF, (h + 1) * HALF)
                dve.scalar_tensor_tensor(m.xt_lo[:, k, tok], m.psum[i % NB][:, :],
                                         m.cols[:, gcol + k:gcol + k + 1], m.xt_hi[:, k, tok].bitcast(F32),
                                         ALU.mult, ALU.subtract).then_inc(m.norm_lo, 1)

        @block.tensor
        def _(pe):
            for i in range(2 * KD):
                h, k = i // KD, i % KD
                if k == 0:
                    pe.wait_ge(m.norm_scaled, NT * turns + 4 * (h + 1))
                if i >= NB:
                    pe.wait_ge(m.norm_lo, 16 * turns + i + 1 - NB)
                for j in range(4):
                    mm = pe.transpose(m.psum[i % NB][:, j * P:(j + 1) * P],
                                      dst(4 * h + j, k * P, (k + 1) * P), m.ident[:, :])
                mm.then_inc(m.norm_turned, 1)
    m.norms += 1
    m.turns += 1


def start_stage(m, x_sb, w_s_raw, w_sT):
    nc, a = m.nc, m.a
    rows = m.at("vector_rows", [P, 3, P], 176)
    in_x, in_rows = m.sem("in_x"), m.sem("in_rows")
    made, masked, turned, cols_done = m.sem("made"), m.sem("masked"), m.sem("vec_turned"), m.sem("cols_done")
    in_ws = m.sem("in_ws")
    with nc.Block() as block:
        @block.sync
        def _(sp):
            for t in range(NT):
                sp.dma_start(x_sb[:, t, :], a["x"][0, t * P:(t + 1) * P, :]).then_inc(in_x, 16)
            sp.wait_ge(made, 7)
            for name in ("mix_norm_g", "out_norm_g", "ffn_norm_g", "w_norm_mix_2", "w_norm_ffn_2", "b_s",
                         "w_sconv_2", "w_gdn_conv_2", "w_gdn_norm_2"):
                v = a[name]
                flat = v.rearrange("a b -> (a b)") if len(v.shape) == 2 else v.rearrange("a b c -> (a b c)")
                n = flat.shape[0] // P
                sp.dma_start(rows[ROW[name]:ROW[name] + n, 0, :],
                             flat.rearrange("(r p) -> r p", p=P)).then_inc(in_rows, 16)
            f = a["w_ffn_conv_2"].rearrange("a b c -> (a b c)").rearrange("(r p) -> r p", p=P)
            sp.dma_start(rows[0:88, 1, :], f[0:88, :]).then_inc(in_rows, 16)
            sp.dma_start(rows[0:44, 2, :], f[88:132, :]).then_inc(in_rows, 16)
            sp.dma_start(w_s_raw[:, :, :], a["w_s"].rearrange("a g i j -> i (a g) j")).then_inc(in_ws, 16)
            sp.wait_ge(in_x, 16 * NT)

        @block.gpsimd
        def _(pool):
            pool.memset(m.ident[:, :], 0.0).then_inc(made, 1)
            pool.memset(m.causal[:, :], 0.0).then_inc(made, 1)
            pool.memset(m.sel[:, :, :], 0.0).then_inc(made, 1)
            pool.memset(m.zero[:, :], 0.0).then_inc(made, 1)
            pool.memset(m.eps[:, :], EPS).then_inc(made, 1)
            pool.memset(rows[:, :, :], 0.0).then_inc(made, 1)
            pool.memset(m.cols[:, :], 0.0).then_inc(made, 1)
            pool.wait_ge(made, 7)
            pool.affine_select(out=m.ident[:, :], in_=m.ident[:, :], compare_op=ALU.not_equal, fill=1.0,
                               base=0, pattern=[[-1, P]], channel_multiplier=1).then_inc(masked, 1)
            pool.affine_select(out=m.causal[:, :], in_=m.causal[:, :], compare_op=ALU.is_ge, fill=NEG,
                               base=0, pattern=[[-1, P]], channel_multiplier=1).then_inc(masked, 1)
            pool.affine_select(out=m.sel[:, :, :], in_=m.sel[:, :, :], compare_op=ALU.not_equal, fill=1.0,
                               base=0, pattern=[[-1, 8], [0, P]], channel_multiplier=1).then_inc(masked, 1)
            pool.wait_ge(masked, 3)

        @block.tensor
        def _(pe):
            pe.wait_ge(masked, 3)
            pe.wait_ge(in_rows, 16 * 11)
            for j in range(3):
                mm = pe.transpose(m.psum[0][:, j * P:(j + 1) * P], rows[:, j, :], m.ident[:, :])
            mm.then_inc(turned, 1)
            pe.wait_ge(in_ws, 16)
            for g in range(8):
                mm = pe.transpose(m.psum[1 + g // 4][:, (g % 4) * P:(g % 4 + 1) * P], w_s_raw[:, g, :], m.ident[:, :])
            mm.then_inc(turned, 1)

        @block.vector
        def _(dve):
            dve.wait_ge(turned, 1)
            dve.wait_ge(made, 7)
            dve.tensor_copy(m.cols[:, 0:ROWS1], m.psum[0][:, 0:ROWS1]).then_inc(cols_done, 1)
            dve.tensor_copy(m.cols[:, COL_FFC:COL_FFC + 88], m.psum[0][:, P:P + 88]).then_inc(cols_done, 1)
            dve.tensor_copy(m.cols[:, COL_FFC + 88:COL_FFC + 132], m.psum[0][:, 2 * P:2 * P + 44]).then_inc(cols_done, 1)
            dve.wait_ge(turned, 2)
            for c in range(2):
                dve.tensor_copy(w_sT[:, 4 * c:4 * c + 4, :],
                                m.psum[1 + c][:, :].rearrange("p (g i) -> p g i", g=4)).then_inc(cols_done, 1)
            dve.wait_ge(cols_done, 5)
            dve.memset(w_sT[64:P, :, 0:64], 0.0).then_inc(cols_done, 1)
            dve.wait_ge(cols_done, 6)


def proj1_stage(m, zu, zv, v, q, k_, sp_f, csum):
    nc, a = m.nc, m.a
    base, c0 = m.slices, m.chunks
    w = a["w_in"][0]
    lng, lnb = m.at("ln_g", [P, 512], 0), m.at("ln_b", [P, 512], 2)
    wf = m.at("w_f", [P, KD, 8], 12)
    wf_hi, wf_lo = m.at("w_f_hi", [P, KD, 8], 12.25, F32R), m.at("w_f_lo", [P, KD, 8], 12.5, F32R)
    bf = m.at("b_f_col", [8, 1], 12.75)
    stats, mv, ln_r = m.at("ln_stats", [P, NT, 6], 13), m.at("ln_mv", [P, NT, 2], 13.25), m.at("ln_rstd", [P, NT], 13.5)
    in_small, evac, f_split, f_done = m.sem("in_small"), m.sem("p1_evac"), m.sem("f_split"), m.sem("f_done")
    sp_done, lnr, stat_done, f_evac = m.sem("softplus_done"), m.sem("ln_rstd_done"), m.sem("ln_stat"), m.sem("f_evac")
    cols = [1544, 1544 + 512, 1024, 0, 512]

    with nc.Block() as block:
        @block.sync
        def _(sp):
            sp.dma_start(wf[:, :, :], w[:, 1536:1544].rearrange("(k p) n -> p k n", p=P)).then_inc(in_small, 16)
            sp.dma_start(bf[:, :], a["b_f"].rearrange("a h -> h a")).then_inc(in_small, 16)
            sp.dma_start(lng[:, :], a["sgu_ln_g"].to_broadcast([P, 512])).then_inc(in_small, 16)
            sp.dma_start(lnb[:, :], a["sgu_ln_b"].to_broadcast([P, 512])).then_inc(in_small, 16)
            for c, col in enumerate(cols):
                load_slices(m, sp, base, 8 * c, 8, lambda j, u: (
                    m.w_raw[:, u, :], w[bass.ds((j * RING + u) * P, P), col:col + HALF]))
            sp.wait_ge(in_small, 64)

        @block.gpsimd
        def _(pool):
            pool.wait_ge(in_small, 64)
            pool.tensor_tensor(wf_hi[:, :, :], wf[:, :, :], m.zero[:, 0:1].unsqueeze(2).to_broadcast([P, KD, 8]), ALU.add).then_inc(f_split, 1)
            pool.wait_ge(f_split, 1)
            pool.tensor_tensor(wf_lo[:, :, :], wf[:, :, :], wf_hi[:, :, :].bitcast(F32), ALU.subtract).then_inc(f_split, 1)
            split_slices(m, pool, base, 40, RING)

        @block.tensor
        def _(pe):
            pe.wait_ge(f_split, 2)
            for h in range(2):
                tok = slice(h * HALF, (h + 1) * HALF)
                for k in range(KD):
                    pe.matmul(m.psum[h][0:8, :], wf_hi[:, k, :], m.xt_hi[:, k, tok], start=k == 0, stop=False)
                    pe.matmul(m.psum[h][0:8, :], wf_hi[:, k, :], m.xt_lo[:, k, tok], start=False, stop=False)
                    mm = pe.matmul(m.psum[h][0:8, :], wf_lo[:, k, :], m.xt_hi[:, k, tok], start=False, stop=k == KD - 1)
                mm.then_inc(f_done, 1)
            for c in range(5):
                def wait_bank(b):
                    if c == 0 and b < 2:
                        pe.wait_ge(f_evac, b + 1)
                    if c >= 1:
                        pe.wait_ge(evac, 8 * (c - 1) + b + 1)
                chunk_products(m, pe, base + 8 * c, c0 + c, c < 3, wait_bank)

        @block.scalar
        def _(act):
            act.wait_ge(in_small, 64)
            for h in range(2):
                act.wait_ge(f_done, h + 1)
                act.activation(sp_f[:, 0, h * HALF:(h + 1) * HALF], m.psum[h][0:8, :], ACT.Identity,
                               bias=bf[:, 0:1]).then_inc(f_evac, 1)
            act.wait_ge(f_evac, 2)
            step = in_turn(m, act, "act")
            step(act.activation(sp_f[:, 1, :], sp_f[:, 0, :], ACT.Abs))
            step(act.activation(sp_f[:, 1, :], sp_f[:, 1, :], ACT.Exp, scale=-1.0))
            act.activation(sp_f[:, 1, :], sp_f[:, 1, :], ACT.Ln, bias=1.0).then_inc(sp_done, 1)
            for c in range(3):
                for b in range(NB):
                    wait_chunk_bank(m, act, base + 8 * c, c0 + c, b)
                    if c == 2:
                        ins = act.activation(v[:, b, :], m.psum[b][:, :], ACT.Copy)
                    else:
                        ins = act.activation((zu, zv)[c][:, b, :], m.psum[b][:, :], ACT.Gelu)
                    ins.then_inc(evac, 1)
            act.wait_ge(stat_done, NT)
            step(act.activation(ln_r[:, :], mv[:, :, 1], ACT.Ln, bias=m.eps[:, 0:1]))
            act.activation(ln_r[:, :], ln_r[:, :], ACT.Exp, scale=-0.5).then_inc(lnr, 1)

        @block.vector
        def _(dve):
            step = in_turn(m, dve, "dve")
            dve.wait_ge(f_evac, 2)
            step(dve.tensor_scalar(sp_f[:, 2, :], sp_f[:, 0, :], -1.0, 0.0, ALU.mult, ALU.max))
            dve.wait_ge(sp_done, 1)
            step(dve.tensor_tensor(sp_f[:, 1, :], sp_f[:, 1, :], sp_f[:, 2, :], ALU.add))
            step(dve.memset(sp_f[:, 2, :], 1.0))
            step(dve.tensor_tensor_scan(csum[:, :], sp_f[:, 2, :], sp_f[:, 1, :], 0.0, ALU.mult, ALU.add))
            for t in range(NT):
                dve.wait_ge(evac, 8 + t + 1)
                step(dve.bn_stats(stats[:, t, :], zv[:, t, :]))
                dve.bn_aggr(mv[:, t, :], stats[:, t, :]).then_inc(stat_done, 1)
            dve.wait_ge(lnr, 1)
            for t in range(NT):
                step(dve.tensor_scalar(zv[:, t, :], zv[:, t, :], mv[:, t, 0:1], ln_r[:, t:t + 1],
                                       ALU.subtract, ALU.mult))
                step(dve.tensor_tensor(zv[:, t, :], zv[:, t, :], lng[:, :], ALU.mult))
                step(dve.tensor_tensor(zv[:, t, :], zv[:, t, :], lnb[:, :], ALU.add))
            for c in range(2):
                for b in range(NB):
                    wait_chunk_bank(m, dve, base + 8 * (3 + c), c0 + 3 + c, b)
                    h, n = b // 4, b % 4
                    dve.tensor_scalar((q, k_)[c][:, n, h * HALF:(h + 1) * HALF], m.psum[b][:, :],
                                      (DH ** -0.5, 1.0)[c], None, ALU.mult).then_inc(evac, 1)
    m.slices += 40
    m.chunks += 5


def mix1_stage(m, attn, gated, zu, zv, v, q, k_, csum, w_sT):
    nc = m.nc
    cb, cbd = m.at("c_rows", [P, S], 32), m.at("c_rows_masked", [P, NT, P], 36)
    sc = m.at("scores", [P, 3, S], 64)
    pt = m.at("probs_t", [P, 2, NT, P], 48)
    nm, ls, rl, m0 = (m.at(n, [P, 64], 56 + i / 4) for i, n in enumerate(("neg_max", "sums", "inv_sums", "max0")))
    mx = m.at("row_max", [P, 64], 57)
    units = [(h, i) for h in range(HA) for i in (7, 0, 6, 1, 5, 2, 4, 3)]
    NU = len(units)
    sgu, sgu_out = m.sem("sgu"), m.sem("sgu_out")
    qk, scored, expd, turned = m.sem("qk"), m.sem("scored"), m.sem("probs"), m.sem("probs_turned")
    pta, ptd, pv, outd = m.sem("probs_t_act"), m.sem("probs_t_dve"), m.sem("pv"), m.sem("attn_out")
    cbp, cbs, mxs, nms = m.sem("c_bcast"), m.sem("c_rows_done"), m.sem("max_done"), m.sem("neg_max_done")

    def bank1(u):
        return sum(1 for x in units[:u + 1] if x[1] >= 4)

    with nc.Block() as block:
        @block.tensor
        def _(pe):
            for g in range(8):
                pe.matmul(m.psum[g][:, :], w_sT[:, g, :], zv[:, :, g * 64:(g + 1) * 64],
                          start=True, stop=True).then_inc(sgu, 1)

            def scores(u):
                h, i = units[u]
                if u % NT == 0:
                    if u:
                        pe.wait_ge(cbs, 2 * h)
                    else:
                        pe.wait_ge(sgu_out, 8)
                    for c in range(2):
                        if c:
                            pe.wait_ge(cbs, 2 * h + 1)
                        pe.matmul(m.psum[7][:, :], m.sel[0:8, h, :], csum[:, c * HALF:(c + 1) * HALF],
                                  start=True, stop=True).then_inc(cbp, 1)
                r, n = 64 * (h % 2), (i + 1) * P
                if u >= 2:
                    pe.wait_ge(scored, u - 1)
                for c in range(0, n, HALF):
                    e = min(n, c + HALF)
                    mm = pe.matmul(m.psum[2 * (u % 2) + c // HALF][:, 0:e - c], q[r:r + 64, h // 2, i * P:(i + 1) * P],
                                   k_[r:r + 64, h // 2, c:e], start=True, stop=True)
                mm.then_inc(qk, 1)

            def turn(u):
                h, i = units[u]
                pe.wait_ge(expd, u + 1)
                if u:
                    pe.wait_ge(pta, u)
                    if bank1(u - 1):
                        pe.wait_ge(ptd, bank1(u - 1))
                for j in range(i + 1):
                    mm = pe.transpose(m.psum[4 + j // 4][:, (j % 4) * P:(j % 4 + 1) * P],
                                      sc[:, u % 3, j * P:(j + 1) * P], m.ident[:, :])
                mm.then_inc(turned, 1)

            def values(u):
                h, i = units[u]
                pe.wait_ge(pta, u + 1)
                if i >= 4:
                    pe.wait_ge(ptd, bank1(u))
                if u:
                    pe.wait_ge(outd, u)
                for j in range(i + 1):
                    mm = pe.matmul(m.psum[6][:, 64 * (u % 2):64 * (u % 2) + 64], pt[:, u % 2, j, :],
                                   v[:, j, h * DH:(h + 1) * DH], start=j == 0, stop=j == i)
                mm.then_inc(pv, 1)

            scores(0)
            scores(1)
            for u in range(NU):
                if u + 2 < NU:
                    scores(u + 2)
                turn(u)
                if u:
                    values(u - 1)
            values(NU - 1)

        @block.vector
        def _(dve):
            for g in range(8):
                dve.wait_ge(sgu, g + 1)
                dve.scalar_tensor_tensor(gated[:, :, g * 64:(g + 1) * 64],
                                         m.psum[g][:, :].rearrange("p (c d) -> p c d", c=NT),
                                         m.cols[:, ROW["b_s"] + g:ROW["b_s"] + g + 1],
                                         zu[:, :, g * 64:(g + 1) * 64], ALU.add, ALU.mult).then_inc(sgu_out, 1)

            def score(u):
                h, i = units[u]
                if u % NT == 0:
                    for c in range(2):
                        dve.wait_ge(cbp, 2 * h + c + 1)
                        dve.tensor_copy(cb[:, c * HALF:(c + 1) * HALF], m.psum[7][:, :]).then_inc(cbs, 1)
                    dve.wait_ge(cbs, 2 * h + 2)
                    dve.tensor_tensor(cbd[:, :, :], cb[:, :].rearrange("p (t n) -> p t n", n=P),
                                      m.causal[:, :].unsqueeze(1).to_broadcast([P, NT, P]), ALU.add).then_inc(m.dve_step, 1)
                    m.dve_steps += 1
                    dve.wait_ge(m.dve_step, m.dve_steps)
                s = u % 2
                dve.wait_ge(qk, u + 1)
                if u >= 3:
                    dve.wait_ge(turned, u - 2)
                c0, d0 = i // 4, (i % 4) * P
                first = m0 if i else mx
                ins = dve.tensor_tensor_reduce(sc[:, u % 3, i * P:(i + 1) * P], m.psum[2 * s + c0][:, d0:d0 + P],
                                               cbd[:, i, :], 1.0, NEG * 10, ALU.add, ALU.max, first[:, u:u + 1])
                ins.then_inc(mxs, 1)
                nmx[0] += 1
                dve.wait_ge(mxs, nmx[0])
                parts = [(c, min(i * P, c + HALF)) for c in range(0, i * P, HALF)]
                for n, (c, e) in enumerate(parts):
                    src = m0 if n == 0 else mx2
                    dst = mx if n == len(parts) - 1 else mx2
                    ins = dve.tensor_tensor_reduce(sc[:, u % 3, c:e], m.psum[2 * s + c // HALF][:, 0:e - c],
                                                   cb[:, c:e], 1.0, src[:, u:u + 1], ALU.add, ALU.max, dst[:, u:u + 1])
                    ins.then_inc(mxs, 1)
                    nmx[0] += 1
                    dve.wait_ge(mxs, nmx[0])
                dve.tensor_scalar(nm[:, u:u + 1], mx[:, u:u + 1], -1.0, None, ALU.mult).then_inc(scored, 1)

            def second_bank(u):
                h, i = units[u]
                if i >= 4:
                    dve.wait_ge(turned, u + 1)
                    if u >= 2:
                        dve.wait_ge(pv, u - 1)
                    dve.tensor_copy(pt[:, u % 2, 4:i + 1, :],
                                    m.psum[5][:, 0:(i - 3) * P].rearrange("p (j n) -> p j n", n=P)).then_inc(ptd, 1)

            def out(u):
                h, i = units[u]
                dve.wait_ge(expd, u + 1)
                step(dve.reciprocal(rl[:, u:u + 1], ls[:, u:u + 1]))
                dve.wait_ge(pv, u + 1)
                dve.tensor_scalar(attn[:, i, h * DH:(h + 1) * DH], m.psum[6][:, 64 * (u % 2):64 * (u % 2) + 64],
                                  rl[:, u:u + 1], None, ALU.mult).then_inc(outd, 1)

            step = in_turn(m, dve, "dve")
            nmx = [0]
            mx2 = m.at("max1", [P, 64], 57.25)
            score(0)
            score(1)
            for u in range(NU):
                if u + 2 < NU:
                    score(u + 2)
                second_bank(u)
                if u:
                    out(u - 1)
            out(NU - 1)

        @block.scalar
        def _(act):
            def turned_probs(u):
                h, i = units[u]
                act.wait_ge(turned, u + 1)
                if u >= 2:
                    act.wait_ge(pv, u - 1)
                n = min(i + 1, 4)
                act.activation(pt[:, u % 2, 0:n, :], m.psum[4][:, 0:n * P].rearrange("p (j n) -> p j n", n=P),
                               ACT.Copy).then_inc(pta, 1)

            for u in range(NU):
                h, i = units[u]
                act.wait_ge(scored, u + 1)
                act.activation(sc[:, u % 3, 0:(i + 1) * P], sc[:, u % 3, 0:(i + 1) * P], ACT.Exp,
                               bias=nm[:, u:u + 1], accum_out=ls[:, u:u + 1]).then_inc(expd, 1)
                if u:
                    turned_probs(u - 1)
            turned_probs(NU - 1)


def out_proj_stage(m, w, x_sb, load_x=None):
    nc = m.nc
    base, c0 = m.slices, m.chunks
    n = m.chunks
    evac = m.sem(f"out_evac{n}")
    in_x = m.sem(f"out_x{n}") if load_x is not None else None
    with nc.Block() as block:
        @block.sync
        def _(sp):
            for c in range(2):
                load_slices(m, sp, base, 8 * c, 8, lambda j, u: (
                    m.w_raw[:, u, :], w[bass.ds((j * RING + u) * P, P), c * HALF:(c + 1) * HALF]))
                if c == 0 and load_x is not None:
                    for t in range(NT):
                        sp.dma_start(x_sb[:, t, :], load_x[t * P:(t + 1) * P, :]).then_inc(in_x, 16)

        @block.gpsimd
        def _(pool):
            split_slices(m, pool, base, 16, RING)

        @block.tensor
        def _(pe):
            for c in range(2):
                chunk_products(m, pe, base + 8 * c, c0 + c, True,
                               (lambda b: pe.wait_ge(evac, 8 * (c - 1) + b + 1)) if c else None)

        @block.vector
        def _(dve):
            if load_x is not None:
                dve.wait_ge(in_x, 16 * NT)
            for c in range(2):
                for b in range(NB):
                    wait_chunk_bank(m, dve, base + 8 * c, c0 + c, b)
                    xs = x_sb[:, b, c * HALF:(c + 1) * HALF]
                    dve.tensor_tensor(xs, m.psum[b][:, :], xs, ALU.add).then_inc(evac, 1)
    m.slices += 16
    m.chunks += 2


def up_first(m, w_up):
    v = w_up.rearrange("k (s n) -> k s n", s=2)
    return lambda u: (m.w_raw[:, u, :].rearrange("p (s n) -> p s n", s=2), v[u * P:(u + 1) * P, :, 0:256])


def ffn_stage(m, w_up, w_down, x_sb, conv):
    nc = m.nc
    base, c0, tag = m.slices, m.chunks, "_conv" if conv else ""
    PAD = 2
    raw = m.at("hidden_raw" + tag, [P, 4, PAD + S], 152)
    hid_hi = m.at("hidden_hi" + tag, [P, 2, S], 169, F32R)
    hid_lo = m.at("hidden_lo" + tag, [P, 2, S], 177, F32R)
    mix = m.at("hidden" + tag, [P, 4, S], 0)
    up_v = w_up.rearrange("k (s n) -> k s n", s=2)
    ev_a, ev_d, dn_done, dn_ev = (m.sem(n + tag) for n in ("gate_read", "up_read", "down_done", "down_read"))
    hid, hid_a, acted, sig, tap = (m.sem(n + tag) for n in ("hidden_done", "hidden_hi_done", "hidden_prod", "silu_done", "tap_done"))
    GU, DN = 8, 4

    with nc.Block() as block:
        @block.sync
        def _(sp):
            def up_slices(first, i, start=0):
                for k in range(start, GU):
                    u, n = k % RING, first + k
                    sp.wait_ge(m.split, n + 1 - RING)
                    sp.dma_start(m.w_raw[:, u, :].rearrange("p (s n) -> p s n", s=2),
                                 up_v[k * P:(k + 1) * P, :, bass.ds(i * 256, 256)]).then_inc(m.loaded[u], 16)

            def down_slices(first, i):
                for u in range(DN):
                    sp.wait_ge(m.split, first + u + 1 - RING)
                    sp.dma_start(m.w_raw[:, u, :], w_down[bass.ds(i * 256 + (u % 2) * P, P),
                                                          (u // 2) * HALF:(u // 2 + 1) * HALF]).then_inc(m.loaded[u], 16)

            up_slices(base, 0, RING)
            with sp.Fori(0, FI - 1) as i:
                up_slices(base + GU + 12 * i, i + 1)
                down_slices(base + 2 * GU + 12 * i, i)
            down_slices(base + GU + 12 * (FI - 1), FI - 1)

        @block.gpsimd
        def _(pool):
            split_slices(m, pool, base, 12 * FI, RING)

        @block.tensor
        def _(pe):
            def up(first, wait_bank):
                for k in range(KD):
                    u = k % RING
                    pe.wait_ge(m.split, first + k + 1)
                    for b in range(NB):
                        if k == 0 and wait_bank is not None:
                            wait_bank(b)
                        h, j, s = b // 4, (b // 2) % 2, b % 2
                        col, tok = slice((2 * s + j) * P, (2 * s + j + 1) * P), slice(h * HALF, (h + 1) * HALF)
                        pe.matmul(m.psum[b][:, :], m.w_hi[:, u, col], m.xt_hi[:, k, tok], start=k == 0, stop=False)
                        pe.matmul(m.psum[b][:, :], m.w_hi[:, u, col], m.xt_lo[:, k, tok], start=False, stop=False)
                        mm = pe.matmul(m.psum[b][:, :], m.w_lo[:, u, col], m.xt_hi[:, k, tok],
                                       start=False, stop=k == KD - 1)
                        if b == NB - 1:
                            mm.then_inc(m.used, 1)
                        elif k == KD - 1:
                            mm.then_inc(m.bank_done, 1)

            def down(first, i, last):
                for nh in range(2):
                    for t in range(NT):
                        if nh == 0:
                            if t == 0:
                                pe.wait_ge(m.split, first + 2)
                            if t in (0, 4):
                                pe.wait_ge(hid, 4 * i + 2 * (t // 4) + 2)
                            if not last:
                                pe.wait_ge(ev_d if t % 2 else ev_a, 4 * (i + 1) + t // 2 + 1)
                        else:
                            if t == 0:
                                pe.wait_ge(m.split, first + 4)
                            pe.wait_ge(dn_ev, 16 * i + t + 2)
                        for j in range(2):
                            u, tok = 2 * nh + j, slice(t * P, (t + 1) * P)
                            pe.matmul(m.psum[t][:, :], hid_hi[:, j, tok], m.w_hi[:, u, :], start=j == 0, stop=False)
                            pe.matmul(m.psum[t][:, :], hid_lo[:, j, tok], m.w_hi[:, u, :], start=False, stop=False)
                            mm = pe.matmul(m.psum[t][:, :], hid_hi[:, j, tok], m.w_lo[:, u, :], start=False, stop=j == 1)
                            if t == NT - 1 and j == 0:
                                mm.then_inc(m.used, 1)
                        mm.then_inc(m.used if t == NT - 1 else dn_done, 1)

            up(base, None)
            with pe.Fori(0, FI - 1) as i:
                def wait_bank(b):
                    pe.wait_ge(ev_d if b % 2 else ev_a, 4 * i + b // 2 + 1)
                    pe.wait_ge(dn_ev, 16 * i + 1)
                up(base + GU + 12 * i, wait_bank)
                down(base + 2 * GU + 12 * i, i, False)
            down(base + GU + 12 * (FI - 1), FI - 1, True)

        def bank_full(eng, first, i, b):
            if b == NB - 1:
                eng.wait_ge(m.used, first + GU)
            else:
                eng.wait_ge(m.bank_done, 7 * (c0 + i) + b + 1)

        def weights_of(i, c, tap_):
            return m.cols[:, bass.ds(COL_FFC + 44 * tap_ + 22 * (c // 2) + c % 2 + 2 * i, 1)]

        @block.scalar
        def _(act):
            def read_gate(first, i):
                for q_ in range(4):
                    h, j = q_ // 2, q_ % 2
                    bank_full(act, first, i, 2 * q_)
                    act.activation(raw[:, j, PAD + h * HALF:PAD + (h + 1) * HALF], m.psum[2 * q_][:, :],
                                   ACT.Copy if conv else ACT.Silu).then_inc(ev_a, 1)

            def finish(i):
                if conv:
                    act.wait_ge(ev_a, 4 * i + 4)
                    act.wait_ge(ev_d, 4 * i + 4)
                    for c in range(4):
                        act.activation(mix[:, c, :], raw[:, c, PAD:PAD + S], ACT.Identity,
                                       scale=weights_of(i, c, 2)).then_inc(tap, 1)
                    for c in range(2):
                        act.wait_ge(acted, 4 * i + c + 1)
                        act.activation(mix[:, c, :], mix[:, c, :], ACT.Silu).then_inc(sig, 1)
                for q_ in range(4):
                    h, j = q_ // 2, q_ % 2
                    tok = slice(h * HALF, (h + 1) * HALF)
                    act.wait_ge(hid_a, 4 * i + q_ + 1)
                    act.activation(hid_hi[:, j, tok], mix[:, j, tok], ACT.Copy).then_inc(sig2, 1)

            sig2 = m.sem("hidden_rounded" + tag)
            m.sig2 = sig2
            read_gate(base, 0)
            finish(0)
            with act.Fori(1, FI) as i:
                act.wait_ge(hid, 4 * i)
                read_gate(base + GU + 12 * (i - 1), i)
                finish(i)

        @block.vector
        def _(dve):
            sig2 = m.sig2
            dve.memset(raw[:, :, 0:PAD], 0.0).then_inc(dn_ev, 1)
            dve.wait_ge(dn_ev, 1)

            def read_up(first, i):
                for q_ in range(4):
                    h, j = q_ // 2, q_ % 2
                    bank_full(dve, first, i, 2 * q_ + 1)
                    dve.tensor_copy(raw[:, 2 + j, PAD + h * HALF:PAD + (h + 1) * HALF],
                                    m.psum[2 * q_ + 1][:, :]).then_inc(ev_d, 1)

            def finish(i):
                if conv:
                    for n, c in enumerate((0, 1, 2, 3)):
                        dve.wait_ge(tap, 4 * i + n + 1)
                        for back in (1, 2):
                            ins = dve.scalar_tensor_tensor(mix[:, c, :], raw[:, c, PAD - back:PAD - back + S],
                                                           weights_of(i, c, 2 - back), mix[:, c, :],
                                                           ALU.mult, ALU.add)
                            if back == 1:
                                ins.then_inc(mid, 1)
                                dve.wait_ge(mid, 4 * i + n + 1)
                        ins.then_inc(acted, 1)
                    dve.wait_ge(acted, 4 * i + 4)
                    dve.wait_ge(sig, 2 * i + 2)
                else:
                    dve.wait_ge(ev_a, 4 * i + 4)
                    dve.wait_ge(ev_d, 4 * i + 4)
                for q_ in range(4):
                    h, j = q_ // 2, q_ % 2
                    tok = slice(h * HALF, (h + 1) * HALF)
                    pad = slice(PAD + h * HALF, PAD + (h + 1) * HALF)
                    g_, u_ = (mix[:, j, tok], mix[:, 2 + j, tok]) if conv else (raw[:, j, pad], raw[:, 2 + j, pad])
                    dve.tensor_tensor(mix[:, j, tok], g_, u_, ALU.mult).then_inc(hid_a, 1)
                for q_ in range(4):
                    h, j = q_ // 2, q_ % 2
                    tok = slice(h * HALF, (h + 1) * HALF)
                    dve.wait_ge(sig2, 4 * i + q_ + 1)
                    dve.tensor_tensor(hid_lo[:, j, tok], mix[:, j, tok], hid_hi[:, j, tok].bitcast(F32),
                                      ALU.subtract).then_inc(hid, 1)

            def read_down(first, i):
                for nh in range(2):
                    for t in range(NT):
                        if t == NT - 1:
                            dve.wait_ge(m.used, first + 2 * nh + 2)
                        else:
                            dve.wait_ge(dn_done, 14 * i + 7 * nh + t + 1)
                        xs = x_sb[:, t, nh * HALF:(nh + 1) * HALF]
                        dve.tensor_tensor(xs, m.psum[t][:, :], xs, ALU.add).then_inc(dn_ev, 1)

            mid = m.sem("tap_mid" + tag)
            read_up(base, 0)
            finish(0)
            with dve.Fori(0, FI - 1) as i:
                read_up(base + GU + 12 * i, i + 1)
                read_down(base + 2 * GU + 12 * i, i)
                finish(i + 1)
            read_down(base + GU + 12 * (FI - 1), FI - 1)
    m.slices += 12 * FI
    m.chunks += FI


HG = 4


def proj2_stage(m, sc, qkv, gz, sqk, sv, ab):
    nc, a = m.nc, m.a
    base, c0 = m.slices, m.chunks
    w = a["w_mix_in_2"][0]
    wf = m.at("w_ab", [P, KD, 8], 196)
    wf_hi, wf_lo = m.at("w_ab_hi", [P, KD, 8], 196.25, F32R), m.at("w_ab_lo", [P, KD, 8], 196.5, F32R)
    conv = m.at("conv", [P, 2, S], 184)
    in_small, evac, f_split, f_done, f_evac = (m.sem(n) for n in ("in_ab", "p2_evac", "ab_split", "ab_done", "ab_evac"))
    prod, last_tap, older, acted, sdone = (m.sem(n) for n in ("sc_prod", "last_tap", "older_taps", "conv_act", "sc_done"))
    two = [m.sem(f"piece_loaded{u}") for u in range(RING)]
    pieces = [[(0, 512)], [(512, 512)], [(1024, 512)], [(1536, 512)], [(2048, 256), (3336, 256)],
              [(2304, 512)], [(2824, 512)]]
    NC = len(pieces)
    jobs = {1: [("s", 0), ("s", 1), ("g", 0), ("g", 1)], 2: [("g", i) for i in range(2, 6)],
            3: [("g", i) for i in range(6, 10)], 4: [("g", 10), ("g", 11)]}
    order = [job for c in range(NC) for job in jobs.get(c, [])]

    def place(c, n):
        i = 4 * c + n
        if i < 6:
            return sc[:, i, :]
        if c < 5 and i < 18:
            return qkv[:, i - 6, :]
        return sv[:, n - 2, :] if c == 4 else sqk[:, n, :]

    with nc.Block() as block:
        @block.sync
        def _(sp):
            sp.dma_start(wf[:, :, :], w[:, 2816:2824].rearrange("(k p) n -> p k n", p=P)).then_inc(in_small, 16)
            for c in range(NC):
                if len(pieces[c]) == 1:
                    col = pieces[c][0][0]
                    load_slices(m, sp, base, 8 * c, 8, lambda j, u: (
                        m.w_raw[:, u, :], w[bass.ds((j * RING + u) * P, P), col:col + HALF]))
                else:
                    for k in range(KD):
                        u = k % RING
                        sp.wait_ge(m.split, base + 8 * c + k + 1 - RING)
                        (c1, n1), (c2, n2) = pieces[c]
                        sp.dma_start(m.w_raw[:, u, 0:n1], w[k * P:(k + 1) * P, c1:c1 + n1]).then_inc(two[u], 16)
                        sp.dma_start(m.w_raw[:, u, n1:HALF], w[k * P:(k + 1) * P, c2:c2 + n2]).then_inc(m.loaded[u], 16)
            sp.wait_ge(in_small, 16)

        @block.gpsimd
        def _(pool):
            pool.wait_ge(in_small, 16)
            pool.tensor_tensor(wf_hi[:, :, :], wf[:, :, :], m.zero[:, 0:1].unsqueeze(2).to_broadcast([P, KD, 8]),
                               ALU.add).then_inc(f_split, 1)
            pool.wait_ge(f_split, 1)
            pool.tensor_tensor(wf_lo[:, :, :], wf[:, :, :], wf_hi[:, :, :].bitcast(F32), ALU.subtract).then_inc(f_split, 1)
            split_slices(m, pool, base, 32, RING)
            for k in range(KD):
                pool.wait_ge(two[k % RING], 16 * (k // RING + 1))
                if k % RING == RING - 1:
                    split_slices(m, pool, base + 32 + k - RING + 1, RING)
            split_slices(m, pool, base + 40, 16)

        @block.tensor
        def _(pe):
            pe.wait_ge(f_split, 2)
            for h in range(2):
                tok = slice(h * HALF, (h + 1) * HALF)
                for k in range(KD):
                    pe.matmul(m.psum[h][0:8, :], wf_hi[:, k, :], m.xt_hi[:, k, tok], start=k == 0, stop=False)
                    pe.matmul(m.psum[h][0:8, :], wf_hi[:, k, :], m.xt_lo[:, k, tok], start=False, stop=False)
                    mm = pe.matmul(m.psum[h][0:8, :], wf_lo[:, k, :], m.xt_hi[:, k, tok], start=False, stop=k == KD - 1)
                mm.then_inc(f_done, 1)
            for c in range(NC):
                def wait_bank(b):
                    if c == 0 and b < 2:
                        pe.wait_ge(f_evac, b + 1)
                    if c >= 1:
                        pe.wait_ge(evac, 8 * (c - 1) + b + 1)
                chunk_products(m, pe, base + 8 * c, c0 + c, c == 5, wait_bank)

        def source(job):
            kind, i = job
            return sc[:, 2 + i, :] if kind == "s" else qkv[:, i, :]

        def tap(job, n):
            kind, i = job
            col = ROW["w_sconv_2"] + 2 * (2 - n) + i if kind == "s" else ROW["w_gdn_conv_2"] + 12 * (3 - n) + i
            return m.cols[:, col:col + 1]

        @block.scalar
        def _(act):
            for h in range(2):
                act.wait_ge(f_done, h + 1)
                act.activation(ab[:, h * HALF:(h + 1) * HALF], m.psum[h][0:8, :], ACT.Copy).then_inc(f_evac, 1)

            def finish(x):
                act.wait_ge(older, x + 1)
                if order[x][0] == "g":
                    act.activation(source(order[x]), conv[:, x % 2, :], ACT.Silu).then_inc(acted, 1)

            x = 0
            for c in range(NC):
                for b in range(NB):
                    wait_chunk_bank(m, act, base + 8 * c, c0 + c, b)
                    h, n = b // 4, b % 4
                    if c == 5:
                        dst = gz[:, b, :]
                    else:
                        dst = place(c, n)[:, h * HALF:(h + 1) * HALF]
                    if c == 6 and b == 0:
                        act.wait_ge(sdone, 2)
                    act.activation(dst, m.psum[b][:, :], ACT.Copy,
                                   scale=SBD ** -0.5 if c == 6 and n < 2 else 1.0).then_inc(evac, 1)
                for job in jobs.get(c, []):
                    act.wait_ge(evac, 8 * (c + 1))
                    if job[0] == "s":
                        act.wait_ge(prod, job[1] + 1)
                    if x >= 2:
                        if order[x - 2][0] == "g":
                            act.wait_ge(acted, sum(o[0] == "g" for o in order[:x - 1]))
                        else:
                            act.wait_ge(sdone, order[x - 2][1] + 1)
                    n = 0
                    act.activation(conv[:, x % 2, :], source(job), ACT.Identity, scale=tap(job, 0)).then_inc(last_tap, 1)
                    if x:
                        finish(x - 1)
                    x += 1
                if c == 4:
                    finish(x - 1)

        @block.vector
        def _(dve):
            step = in_turn(m, dve, "dve")
            for i in range(2):
                dve.wait_ge(evac, 16)
                dve.tensor_tensor(sc[:, 2 + i, :], sc[:, 2 + i, :], sc[:, 4 + i, :], ALU.mult).then_inc(prod, 1)
            dve.wait_ge(prod, 2)
            for x, job in enumerate(order):
                dve.wait_ge(last_tap, x + 1)
                taps = 2 if job[0] == "s" else 3
                for n in range(1, taps + 1):
                    y = conv[:, x % 2, n:S]
                    ins = dve.scalar_tensor_tensor(y, source(job)[:, 0:S - n], tap(job, n), y, ALU.mult, ALU.add)
                    if n < taps:
                        step(ins)
                ins.then_inc(older, 1)
                if job[0] == "s":
                    dve.wait_ge(older, x + 1)
                    y = sc[:, job[1], :]
                    dve.tensor_tensor(y, y, conv[:, x % 2, :], ALU.mult).then_inc(sdone, 1)
    m.slices += 8 * NC
    m.chunks += NC


SBD = 64


def nth(events, h, name):
    return len(events) * h + events.index(name) + 1


def delta_stage(m, q_, k_, v_, ab, t_at):
    nc, a = m.nc, m.a
    at = m.at
    a_t, kd, elast = t_at["a_t"], t_at["kd"], t_at["elast"]
    X, XT, LT, T1, ke, vb = (at(n, [P, NT, P], 64 + 4 * i) for i, n in enumerate(("X", "XT", "LT", "T1", "ke", "vb")))
    LM = [at("LM0", [P, NT, P], 88), at("LM1", [P, NT, P], 92)]
    Gb, GBb, Qb, Kb = (at(n, [P, NT, P], 96 + 4 * i) for i, n in enumerate(("Gb", "GBb", "Qb", "Kb")))
    masks = at("masks", [P, 3, P], 112)
    lev = at("levels", [P, 7, P], 113.5)
    ones = at("ones", [P, P], 117)
    small = at("small", [P, 12, NT], 117.5)
    eps128 = at("eps128", [P, 1], 118)
    col8 = at("col8", [8, 4], 118.0625)
    gct, gbt = at("gct", [P, NT, 8], 118.125), at("gbt", [P, NT, 8], 118.375)
    gc, gcb = at("gc", [8, S], 196), ab
    r1, r2, r3 = (at(n, [8, S], 64 + 4 * i) for i, n in enumerate(("r1", "r2", "r3")))
    made, rows_in, rows, turned = m.sem("delta_masks"), m.sem("delta_in"), m.sem("delta_rows"), m.sem("delta_cols")
    pe_s, dve_s, act_s, pool_s = m.sem("delta_pe"), m.sem("delta_dve"), m.sem("delta_act"), m.sem("delta_pool")
    LEV = range(1, 7)
    MADE = 30
    PE_EV = ["g", "gb", "ssq", "ssk", "kt", "vt", "kk", "kq"] + [
        f"{n}{j}{g}" for j in LEV for g in (0, 1) for n in (("t", "x", "xt") if j < 6 else ("t", "xt"))] + ["w0", "w1", "u0", "u1"]
    DVE_EV = ["gcopy", "gbcopy", "ktcopy", "ssc", "r", "b", "ea", "elt", "el", "ke", "vb", "kd", "LT", "X1", "a_t", "qe"] + [
        f"{n}{j}{g}" for j in LEV for g in (0, 1) for n in (("x", "xt") if j < 6 else ("xt",))] + ["w0", "w1"]
    ACT_EV = ["sqq", "sqk", "lnq", "lnk", "sqt", "lns", "ex", "er1", "ea", "elt", "el"] + [
        f"t{j}{g}" for j in LEV for g in (0, 1)] + ["u0", "u1"]
    POOL_EV = [f"m{j}" for j in LEV]

    def pe_at(e, h, n):
        e.wait_ge(pe_s, nth(PE_EV, h, n))

    def dve_at(e, h, n):
        e.wait_ge(dve_s, nth(DVE_EV, h, n))

    def act_at(e, h, n):
        e.wait_ge(act_s, nth(ACT_EV, h, n))

    def tiles(bank):
        return bank[:, :].rearrange("p (c n) -> p c n", n=P)

    def half(t, g):
        return t[:, 4 * g:4 * g + 4, :]

    def flat(t, c):
        return t[:, :, :].rearrange("p c n -> p (c n)")[:, c * HALF:(c + 1) * HALF]

    with nc.Block() as block:
        @block.sync
        def _(sp):
            sp.wait_ge(made, 1)
            sp.dma_start(col8[0:4, 0:1], a["gdn_dt_bias_2"].rearrange("a h -> h a")).then_inc(rows_in, 16)
            sp.dma_start(col8[0:4, 1:2], a["gdn_a_log_2"].rearrange("a h -> h a")).then_inc(rows_in, 16)
            sp.wait_ge(rows_in, 32)

        @block.gpsimd
        def _(pool):
            pool.memset(col8[:, :], 0.0).then_inc(made, 1)
            pool.memset(masks[:, :, :], 0.0).then_inc(made, 1)
            pool.memset(lev[:, :, :], 0.0).then_inc(made, 1)
            pool.memset(ones[:, :], 1.0).then_inc(made, 1)
            pool.memset(eps128[:, :], EPS * P).then_inc(made, 1)
            pool.wait_ge(made, 5)
            n = 5
            for i, b in ((0, 0), (1, -1)):
                pool.affine_select(out=masks[:, i, :], in_=masks[:, i, :], compare_op=ALU.is_ge, fill=NEG,
                                   base=b, pattern=[[1, P]], channel_multiplier=-1).then_inc(made, 1)
                n += 1
            pool.memset(masks[:, 2, :], NEG).then_inc(made, 1)
            n += 1
            pool.wait_ge(made, n)
            v = masks[:, 2, :].rearrange("p (b e) -> p b e", e=2)
            pool.affine_select(out=v[:, :, 0], in_=v[:, :, 0], compare_op=ALU.not_equal, fill=0.0,
                               base=-1, pattern=[[-2, 64]], channel_multiplier=1).then_inc(made, 1)
            n += 1
            for j in range(7):
                b = 1 << j
                v = lev[:, j, :].rearrange("p (k e r) -> p k e r", e=2, r=b)[:, :, 1, :]
                pool.memset(v, 1.0).then_inc(made, 1)
                n += 1
                pool.wait_ge(made, n)
                pool.affine_select(out=v, in_=v, compare_op=ALU.is_ge, fill=0.0, base=0,
                                   pattern=[[-2 * b, 64 // b], [0, b]], channel_multiplier=1).then_inc(made, 1)
                n += 1
                pool.wait_ge(made, n)
                pool.affine_select(out=v, in_=v, compare_op=ALU.is_ge, fill=0.0, base=b - 1,
                                   pattern=[[2 * b, 64 // b], [0, b]], channel_multiplier=-1).then_inc(made, 1)
                n += 1
            pool.wait_ge(made, n)
            assert n == MADE
            for h in range(HG):
                dve_at(pool, h, "LT")
                for j in LEV:
                    if j > 2:
                        pe_at(pool, h, f"t{j - 2}1")
                    elif h:
                        pe_at(pool, h - 1, f"t{j + 4}1")
                    pool.tensor_tensor(LM[j % 2][:, :, :], LT[:, :, :],
                                       lev[:, j, :].unsqueeze(1).to_broadcast([P, NT, P]), ALU.mult).then_inc(pool_s, 1)

        @block.scalar
        def _(act):
            step = in_turn(m, act, "act")
            act.wait_ge(rows_in, 32)
            act.wait_ge(made, MADE)
            step(act.activation(r1[:, :], ab[:, :], ACT.Identity, bias=col8[:, 0:1]))
            step(act.activation(r2[:, :], r1[:, :], ACT.Abs))
            step(act.activation(r2[:, :], r2[:, :], ACT.Exp, scale=-1.0))
            act.activation(r2[:, :], r2[:, :], ACT.Ln, bias=1.0).then_inc(rows, 1)
            act.activation(col8[:, 2:3], col8[:, 1:2], ACT.Exp).then_inc(rows, 1)
            for h in range(HG):
                if h:
                    pe_at(act, h - 1, "u1")
                else:
                    act.wait_ge(rows, 3)
                act.activation(X[:, :, :].rearrange("p c n -> p (c n)"), q_[:, h, :], ACT.Square).then_inc(act_s, 1)
                act.activation(XT[:, :, :].rearrange("p c n -> p (c n)"), k_[:, h, :], ACT.Square).then_inc(act_s, 1)
                for i, (dst, ev) in enumerate(((Qb, "ssq"), (Kb, "ssk"))):
                    pe_at(act, h, ev)
                    for c in range(2):
                        ins = act.activation(flat(dst, c), m.psum[4 + 2 * i + c][:, :], ACT.Ln,
                                             scale=float(P) if i == 0 else 1.0,
                                             bias=(eps128 if i == 0 else m.eps)[:, 0:1])
                    ins.then_inc(act_s, 1)
                dve_at(act, h, "ktcopy")
                act.activation(T1[:, :, :], kd[:, h, :, :], ACT.Square).then_inc(act_s, 1)
                dve_at(act, h, "ssc")
                act.activation(small[:, 1, :], small[:, 0, :], ACT.Ln, bias=m.eps[:, 0:1]).then_inc(act_s, 1)
                dve_at(act, h, "b")
                act.activation(small[:, 8:12, :], small[:, 4:8, :], ACT.Exp).then_inc(act_s, 1)
                act.activation(Gb[:, :, :], Qb[:, :, :], ACT.Exp).then_inc(act_s, 1)
                for t, ev in ((Qb, "ea"), (GBb, "elt"), (Kb, "el")):
                    dve_at(act, h, ev)
                    act.activation(t[:, :, :], t[:, :, :], ACT.Exp).then_inc(act_s, 1)
                for j in LEV:
                    for g in (0, 1):
                        pe_at(act, h, f"t{j}{g}")
                        act.activation(half(T1, g), tiles(m.psum[g]), ACT.Copy).then_inc(act_s, 1)
                for g in (0, 1):
                    pe_at(act, h, f"u{g}")
                    act.activation(v_[:, h, g * HALF:(g + 1) * HALF], m.psum[6 + g][:, :], ACT.Copy).then_inc(act_s, 1)

        @block.vector
        def _(dve):
            step = in_turn(m, dve, "dve")
            dve.wait_ge(rows, 2)
            step(dve.tensor_scalar(r3[:, :], r1[:, :], 0.0, None, ALU.max))
            step(dve.tensor_tensor(r3[:, :], r3[:, :], r2[:, :], ALU.add))
            step(dve.tensor_scalar(r3[:, :], r3[:, :], col8[:, 2:3], -1.0, ALU.mult, ALU.mult))
            step(dve.tensor_scalar(r1[:, :], r1[:, :], -1.0, 0.0, ALU.mult, ALU.max))
            step(dve.tensor_tensor(r1[:, :], r1[:, :], r2[:, :], ALU.add))
            step(dve.tensor_scalar(gcb[:, :], r1[:, :], -1.0, None, ALU.mult))
            step(dve.memset(r2[:, :], 1.0))
            step(dve.memset(r2[:, :].rearrange("p (c n) -> p c n", n=P)[:, :, 0:1], 0.0))
            dve.tensor_tensor_scan(gc[:, :], r2[:, :], r3[:, :], 0.0, ALU.mult, ALU.add).then_inc(rows, 1)
            dve.wait_ge(turned, 1)
            step(dve.tensor_copy(gct[:, :, :], m.psum[0][:, 0:64].rearrange("p (c n) -> p c n", n=8)))
            step(dve.tensor_copy(gbt[:, :, 4:8], m.psum[0][:, 64:128].rearrange("p (c n) -> p c n", n=8)[:, :, 4:8]))
            m.dve_steps_cols = m.dve_steps
            step(dve.tensor_tensor(gbt[:, :, 0:4], gbt[:, :, 4:8], gct[:, :, 0:4], ALU.add))
            dve.wait_ge(made, MADE)
            for h in range(HG):
                for i, (dst, ev) in enumerate(((Gb, "g"), (GBb, "gb"))):
                    pe_at(dve, h, ev)
                    for c in range(2):
                        ins = dve.tensor_copy(flat(dst, c), m.psum[2 * i + c][:, :])
                    ins.then_inc(dve_s, 1)
                pe_at(dve, h, "kt")
                for c in range(2):
                    ins = dve.tensor_copy(kd[:, h, 4 * c:4 * c + 4, :], tiles(m.psum[c]))
                ins.then_inc(dve_s, 1)
                act_at(dve, h, "sqt")
                dve.tensor_reduce(small[:, 0, :], T1[:, :, :], AX, ALU.add).then_inc(dve_s, 1)
                act_at(dve, h, "lnk")
                dve_at(dve, h, "gbcopy")
                step(dve.tensor_copy(small[:, 7, :], Gb[:, :, P - 1]))
                step(dve.scalar_tensor_tensor(Qb[:, :, :], Qb[:, :, :], -0.5, Gb[:, :, :], ALU.mult, ALU.add))
                step(dve.tensor_tensor(GBb[:, :, :], GBb[:, :, :], Gb[:, :, :], ALU.add))
                step(dve.scalar_tensor_tensor(GBb[:, :, :], Kb[:, :, :], -0.5, GBb[:, :, :], ALU.mult, ALU.add))
                dve.scalar_tensor_tensor(Kb[:, :, :], Kb[:, :, :], -0.5, Gb[:, :, :], ALU.mult, ALU.subtract).then_inc(dve_s, 1)
                act_at(dve, h, "lns")
                dve_at(dve, h, "r")
                step(dve.scalar_tensor_tensor(small[:, 2, :], small[:, 1, :], -0.5, gct[:, :, h], ALU.mult, ALU.subtract))
                step(dve.scalar_tensor_tensor(small[:, 4, :], small[:, 1, :], -0.5, gbt[:, :, h], ALU.mult, ALU.add))
                step(dve.tensor_tensor(small[:, 5, :], small[:, 2, :], small[:, 7, :], ALU.add))
                dve.tensor_tensor(small[:, 6, :], gbt[:, :, h], gct[:, :, h], ALU.subtract).then_inc(dve_s, 1)
                act_at(dve, h, "er1")
                dve_at(dve, h, "b")
                for i, (t, bias) in enumerate(((Qb, 2), (GBb, 2), (Kb, 4))):
                    for c in range(NT):
                        ins = dve.scalar_tensor_tensor(t[:, c, :], t[:, c, :], small[:, bias, c:c + 1], masks[:, i, :],
                                                       ALU.add, ALU.add)
                    ins.then_inc(dve_s, 1)
                dve.tensor_tensor(ke[:, :, :], kd[:, h, :, :], small[:, 8, :].unsqueeze(2).to_broadcast([P, NT, P]),
                                  ALU.mult).then_inc(dve_s, 1)
                pe_at(dve, h, "vt")
                for c in range(2):
                    ins = dve.tensor_tensor(half(vb, c), tiles(m.psum[2 + c]),
                                            small[:, 10, 4 * c:4 * c + 4].unsqueeze(2).to_broadcast([P, 4, P]), ALU.mult)
                ins.then_inc(dve_s, 1)
                dve_at(dve, h, "ke")
                dve.tensor_tensor(kd[:, h, :, :], kd[:, h, :, :], small[:, 9, :].unsqueeze(2).to_broadcast([P, NT, P]),
                                  ALU.mult).then_inc(dve_s, 1)
                step(dve.tensor_copy(elast[:, h, :], small[:, 11, :]))
                pe_at(dve, h, "kk")
                act_at(dve, h, "el")
                for c in range(2):
                    ins = dve.tensor_tensor(half(LT, c), tiles(m.psum[4 + c]), half(GBb, c), ALU.mult)
                ins.then_inc(dve_s, 1)
                for c in range(2):
                    step(dve.tensor_tensor(half(X, c), tiles(m.psum[4 + c]), half(Kb, c), ALU.mult))
                eye = m.ident[:, :].unsqueeze(1).to_broadcast([P, NT, P])
                dve_at(dve, h, "LT")
                step(dve.tensor_tensor(X[:, :, :], eye, X[:, :, :], ALU.subtract))
                step(dve.tensor_tensor(XT[:, :, :], LT[:, :, :], lev[:, 0, :].unsqueeze(1).to_broadcast([P, NT, P]), ALU.mult))
                dve.tensor_tensor(XT[:, :, :], eye, XT[:, :, :], ALU.subtract).then_inc(dve_s, 1)
                pe_at(dve, h, "kq")
                for c in range(2):
                    ins = dve.tensor_tensor(a_t[:, h, 4 * c:4 * c + 4, :], tiles(m.psum[6 + c]), half(Qb, c), ALU.mult)
                ins.then_inc(dve_s, 1)
                dve.tensor_tensor(q_[:, h, :], q_[:, h, :], Gb[:, :, :].rearrange("p c n -> p (c n)"), ALU.mult).then_inc(dve_s, 1)
                dve_at(dve, h, "qe")
                for j in LEV:
                    for g in (0, 1):
                        if j < 6:
                            pe_at(dve, h, f"x{j}{g}")
                            dve.tensor_tensor(half(X, g), half(X, g), tiles(m.psum[2 + g]), ALU.subtract).then_inc(dve_s, 1)
                        pe_at(dve, h, f"xt{j}{g}")
                        dve.tensor_tensor(half(XT, g), half(XT, g), tiles(m.psum[4 + g]), ALU.subtract).then_inc(dve_s, 1)
                for g in (0, 1):
                    pe_at(dve, h, f"w{g}")
                    dve.tensor_copy(k_[:, h, g * HALF:(g + 1) * HALF], m.psum[g][:, :]).then_inc(dve_s, 1)

        @block.tensor
        def _(pe):
            pe.wait_ge(made, MADE)
            pe.wait_ge(rows, 3)
            for c in range(NT):
                pe.transpose(m.psum[0][:, 8 * c:8 * c + 8], gc[:, c * P:(c + 1) * P], m.ident[0:8, 0:8])
            for c in range(NT):
                mm = pe.transpose(m.psum[0][:, 64 + 8 * c:72 + 8 * c], gcb[:, c * P:(c + 1) * P], m.ident[0:8, 0:8])
            mm.then_inc(turned, 1)
            pe.wait_ge(m.dve_step, m.dve_steps_cols)
            for h in range(HG):
                if h:
                    act_at(pe, h - 1, "u1")
                    dve_at(pe, h - 1, "w1")
                for i, (rows_, r) in enumerate(((gc, h), (gcb, 4 + h))):
                    for c in range(2):
                        mm = pe.matmul(m.psum[2 * i + c][:, :], m.sel[0:8, r, :], rows_[:, c * HALF:(c + 1) * HALF],
                                       start=True, stop=True)
                    mm.then_inc(pe_s, 1)
                for i, (t, ev) in enumerate(((X, "sqq"), (XT, "sqk"))):
                    act_at(pe, h, ev)
                    for c in range(2):
                        mm = pe.matmul(m.psum[4 + 2 * i + c][:, :], ones[:, :], flat(t, c), start=True, stop=True)
                    mm.then_inc(pe_s, 1)
                for i, (t, ev) in enumerate(((k_, "gcopy"), (v_, "gbcopy"))):
                    dve_at(pe, h, ev)
                    for c in range(NT):
                        mm = pe.transpose(m.psum[2 * i + c // 4][:, (c % 4) * P:(c % 4 + 1) * P],
                                          t[:, h, c * P:(c + 1) * P], m.ident[:, :])
                    mm.then_inc(pe_s, 1)
                for i, (t, ev) in enumerate(((k_, "lnq"), (q_, "lnk"))):
                    act_at(pe, h, ev)
                    for c in range(NT):
                        tok = slice(c * P, (c + 1) * P)
                        mm = pe.matmul(m.psum[4 + 2 * i + c // 4][:, (c % 4) * P:(c % 4 + 1) * P],
                                       k_[:, h, tok], t[:, h, tok], start=True, stop=True)
                    mm.then_inc(pe_s, 1)

                def products(bank, g, lhs, rhs):
                    for c in range(4 * g, 4 * g + 4):
                        mm = pe.matmul(m.psum[bank][:, (c % 4) * P:(c % 4 + 1) * P], lhs(c), rhs(c), start=True, stop=True)
                    mm.then_inc(pe_s, 1)

                dve_at(pe, h, "X1")
                dve_at(pe, h, "vb")
                for j in LEV:
                    pe.wait_ge(pool_s, 6 * h + j)
                    for g in (0, 1):
                        if j > 1:
                            dve_at(pe, h, f"xt{j - 1}{g}")
                        products(g, g, lambda c: LM[j % 2][:, c, :], lambda c: X[:, c, :])
                        act_at(pe, h, f"t{j}{g}")
                        if j < 6:
                            products(2 + g, g, lambda c: XT[:, c, :], lambda c: T1[:, c, :])
                        products(4 + g, g, lambda c: T1[:, c, :], lambda c: XT[:, c, :])
                for g in (0, 1):
                    dve_at(pe, h, f"xt6{g}")
                    products(g, g, lambda c: ke[:, c, :], lambda c: XT[:, c, :])
                for g in (0, 1):
                    if g == 0:
                        dve_at(pe, h, "a_t")
                    products(6 + g, g, lambda c: XT[:, c, :], lambda c: vb[:, c, :])


def scan_stage(m, q_, k_, v_, t_at, gz):
    nc = m.nc
    a_t, kd, elast = t_at["a_t"], t_at["kd"], t_at["elast"]
    state, vn = m.at("state", [P, HG, P], 64), m.at("v_new", [P, HG, P], 66)
    o = m.at("delta_out", [P, NT, HG, P], 68)
    sq = m.at("delta_sq", [P, NT, HG, P], 84)
    ss, rs = m.at("delta_ss", [P, NT * HG], 100), m.at("delta_rs", [P, NT * HG], 100.25)
    pe_s, dve_s, act_s = m.sem("scan_pe"), m.sem("scan_dve"), m.sem("scan_out")
    gate = m.sem("scan_gate")
    with nc.Block() as block:
        @block.tensor
        def _(pe):
            for c in range(NT):
                tok = slice(c * P, (c + 1) * P)
                for h in range(HG):
                    if c:
                        pe.wait_ge(dve_s, 8 * c - 4 + h + 1)
                    else:
                        pe.wait_ge(gate, 1)
                    pe.matmul(m.psum[h][:, 0:P], k_[:, h, tok], state[:, h, :], start=True, stop=True).then_inc(pe_s, 1)
                for h in range(HG):
                    if c:
                        pe.wait_ge(act_s, 4 * (c - 1) + h + 1)
                    pe.matmul(m.psum[4 + h][:, 0:P], q_[:, h, tok], state[:, h, :], start=True, stop=False)
                    pe.wait_ge(dve_s, 8 * c + h + 1)
                    pe.matmul(m.psum[4 + h][:, 0:P], a_t[:, h, c, :], vn[:, h, :], start=False, stop=True).then_inc(pe_s, 1)
                for h in range(HG):
                    pe.matmul(m.psum[h][:, 0:P], kd[:, h, c, :], vn[:, h, :], start=True, stop=True).then_inc(pe_s, 1)

        @block.vector
        def _(dve):
            step = in_turn(m, dve, "dve")
            dve.memset(state[:, :, :], 0.0).then_inc(gate, 1)
            dve.wait_ge(gate, 1)
            for c in range(NT):
                for h in range(HG):
                    dve.wait_ge(pe_s, 12 * c + h + 1)
                    dve.tensor_tensor(vn[:, h, :], v_[:, h, c * P:(c + 1) * P], m.psum[h][:, 0:P],
                                      ALU.subtract).then_inc(dve_s, 1)
                for h in range(HG):
                    dve.wait_ge(pe_s, 12 * c + 8 + h + 1)
                    if c:
                        dve.wait_ge(dve_s, 8 * c - 4 + h + 1)
                    dve.scalar_tensor_tensor(state[:, h, :], state[:, h, :], elast[:, h, c:c + 1], m.psum[h][:, 0:P],
                                             ALU.mult, ALU.add).then_inc(dve_s, 1)
            dve.wait_ge(gate, 2)
            dve.tensor_reduce(ss[:, :], sq[:, :, :, :].rearrange("p c h n -> p (c h) n"), AX, ALU.add).then_inc(gate, 1)
            dve.wait_ge(gate, 5)
            of = o[:, :, :, :].rearrange("p c h n -> p (c h) n")
            step(dve.tensor_tensor(of, of, rs[:, :].unsqueeze(2).to_broadcast([P, NT * HG, P]), ALU.mult))
            step(dve.tensor_tensor(gz[:, :, :], gz[:, :, :], o[:, :, :, :].rearrange("p c h n -> p c (h n)"), ALU.mult))

        @block.scalar
        def _(act):
            for c in range(NT):
                for h in range(HG):
                    act.wait_ge(pe_s, 12 * c + 4 + h + 1)
                    act.activation(o[:, c, h, :], m.psum[4 + h][:, 0:P], ACT.Copy).then_inc(act_s, 1)
            act.wait_ge(act_s, 32)
            act.wait_ge(gate, 1)
            act.activation(sq[:, :, :, :], o[:, :, :, :], ACT.Square).then_inc(gate, 1)
            act.wait_ge(gate, 3)
            act.activation(rs[:, :], ss[:, :], ACT.Ln, scale=1.0 / P, bias=m.eps[:, 0:1]).then_inc(gate, 1)
            act.wait_ge(gate, 4)
            act.activation(gz[:, :, :], gz[:, :, :], ACT.Silu).then_inc(m.act_step, 1)
            m.act_steps += 1
            act.wait_ge(m.act_step, m.act_steps)
            act.activation(rs[:, :], rs[:, :], ACT.Exp, scale=-0.5).then_inc(gate, 1)


def stick_stage(m, sqk, sv, y):
    nc = m.nc
    svt = m.at("sv_t", [P, NT, 4, SBD], 64)
    tri, allm, keep, mneg = (m.at(n, [P, P], 72 + i / 2) for i, n in enumerate(("tri", "minus_ones", "keep", "not_before")))
    zc, sp, acc, A = (m.at(n, [P, 4, HALF], 76 + 8 * i) for i, n in enumerate(("z_capped", "softplus", "later", "weights")))
    made, pe_s, dve_s, act_s, dma = m.sem("sb_made"), m.sem("sb_pe"), m.sem("sb_dve"), m.sem("sb_act"), m.sem("sb_t")
    rounds = [(g, b) for g in range(2) for b in range(4 * g + 3, -1, -1)]
    DN = 16
    evo, extra, values_in = m.sem("sb_out"), m.sem("sb_later"), m.sem("sb_values")

    def cols(g, b):
        return max(0, b - 4 * g) * P

    with nc.Block() as block:
        @block.gpsimd
        def _(pool):
            pool.memset(tri[:, :], -1.0).then_inc(made, 1)
            pool.memset(allm[:, :], -1.0).then_inc(made, 1)
            pool.memset(keep[:, :], 1.0).then_inc(made, 1)
            pool.memset(mneg[:, :], 0.0).then_inc(made, 1)
            pool.wait_ge(made, 4)
            pool.affine_select(out=tri[:, :], in_=tri[:, :], compare_op=ALU.is_ge, fill=0.0, base=0,
                               pattern=[[-1, P]], channel_multiplier=1).then_inc(made, 1)
            pool.affine_select(out=keep[:, :], in_=keep[:, :], compare_op=ALU.is_gt, fill=0.0, base=0,
                               pattern=[[1, P]], channel_multiplier=-1).then_inc(made, 1)
            pool.affine_select(out=mneg[:, :], in_=mneg[:, :], compare_op=ALU.is_gt, fill=NEG, base=0,
                               pattern=[[1, P]], channel_multiplier=-1).then_inc(made, 1)
            pool.wait_ge(made, 7)

        @block.tensor
        def _(pe):
            for n in range(2):
                for t in range(NT):
                    mm = pe.transpose(m.psum[2 * n + t // 4][:, (t % 4) * P:(t % 4 + 1) * P],
                                      sv[:, n, t * P:(t + 1) * P], m.ident[:, :])
                mm.then_inc(dma, 1)
            pe.wait_ge(made, 7)
            pe.wait_ge(values_in, 2)
            for r, (g, b) in enumerate(rounds):
                c0, key = cols(g, b), slice(b * P, (b + 1) * P)
                first, last = b == 4 * g + 3, b == 0
                for h in range(4):
                    p0 = 64 * (h % 2)
                    if r:
                        pe.wait_ge(act_s, 12 * (r - 1) + 8 + h + 1)
                    pe.matmul(m.psum[h][:, c0:HALF], sqk[p0:p0 + 64, 2 + h // 2, key],
                              sqk[p0:p0 + 64, h // 2, g * HALF + c0:(g + 1) * HALF], start=True, stop=True).then_inc(pe_s, 1)
                for h in range(4):
                    pe.wait_ge(dve_s, DN * r + 2 * (h + 1) + 4)
                    mm = pe.matmul(m.psum[h][:, c0:HALF], tri[:, :], sp[:, h, c0:HALF], start=False, stop=False,
                                   skip_group_check=True)
                    if b >= 4 * g:
                        mm = pe.matmul(m.psum[h][:, c0:c0 + P], m.ident[:, :], mneg[:, :], start=False, stop=False,
                                       skip_group_check=True)
                    if not first:
                        c1 = c0 + P if b >= 4 * g else c0
                        mm = pe.matmul(m.psum[h][:, c1:HALF], allm[:, :], acc[:, h, c1:HALF], start=False, stop=True,
                                       skip_group_check=True)
                    mm.then_inc(pe_s, 1)
                for h in range(4):
                    p0 = 64 * (h % 2)
                    pe.wait_ge(act_s, 12 * r + 8 + h + 1)
                    if first and g:
                        pe.wait_ge(evo, h + 1)
                    pe.matmul(m.psum[4 + h][p0:p0 + 64, c0:HALF], svt[:, b, h, :], A[:, h, c0:HALF],
                              start=first, stop=last, skip_group_check=True).then_inc(pe_s, 1)

        @block.vector
        def _(dve):
            for n in range(2):
                dve.wait_ge(dma, n + 1)
                for c in range(2):
                    ins = dve.tensor_copy(svt[:, 4 * c:4 * c + 4, 2 * n:2 * n + 2, :],
                                          m.psum[2 * n + c][:, :].rearrange("p (t h d) -> p t h d", t=4, h=2))
                ins.then_inc(values_in, 1)
            dve.wait_ge(made, 7)
            for r, (g, b) in enumerate(rounds):
                c0 = cols(g, b)
                first = b == 4 * g + 3
                base = DN * r
                for h in range(4):
                    dve.wait_ge(pe_s, 12 * r + h + 1)
                    if r:
                        dve.wait_ge(act_s, 12 * (r - 1) + h + 1)
                    dve.tensor_scalar(zc[:, h, c0:HALF], m.psum[h][:, c0:HALF], 40.0, None, ALU.min).then_inc(dve_s, 1)
                for h in range(4):
                    dve.wait_ge(act_s, 12 * r + 4 + h + 1)
                    dve.tensor_tensor(sp[:, h, c0:HALF], sp[:, h, c0:HALF], m.psum[h][:, c0:HALF], ALU.max).then_inc(dve_s, 1)
                    dve.wait_ge(dve_s, base + 4 + 2 * h + 1)
                    if b >= 4 * g:
                        dve.tensor_tensor(sp[:, h, c0:c0 + P], sp[:, h, c0:c0 + P], keep[:, :], ALU.mult).then_inc(dve_s, 1)
                    else:
                        dve.tensor_copy(zc[:, h, 0:1], sp[:, h, 0:1]).then_inc(dve_s, 1)
                for h in range(4):
                    dve.wait_ge(pe_s, 12 * r + 4 + h + 1)
                    if first:
                        dve.wait_ge(dve_s, base + 4 + 2 * h + 2)
                        dve.tensor_copy(acc[:, h, c0:HALF], sp[:, h, c0:HALF]).then_inc(dve_s, 1)
                    elif b >= 4 * g:
                        dve.wait_ge(dve_s, base + 4 + 2 * h + 2)
                        dve.tensor_tensor(acc[:, h, c0 + P:HALF], acc[:, h, c0 + P:HALF], sp[:, h, c0 + P:HALF], ALU.add)\
                           .then_inc(extra, 1)
                        dve.tensor_copy(acc[:, h, c0:c0 + P], sp[:, h, c0:c0 + P]).then_inc(dve_s, 1)
                    else:
                        dve.tensor_tensor(acc[:, h, :], acc[:, h, :], sp[:, h, :], ALU.add).then_inc(dve_s, 1)
                if b == 0:
                    for h in range(4):
                        p0 = 64 * (h % 2)
                        dve.wait_ge(pe_s, 12 * r + 8 + h + 1)
                        dve.tensor_copy(y[p0:p0 + 64, h // 2, g * HALF:(g + 1) * HALF],
                                        m.psum[4 + h][p0:p0 + 64, :]).then_inc(evo, 1)

        @block.scalar
        def _(act):
            for r, (g, b) in enumerate(rounds):
                c0 = cols(g, b)
                for h in range(4):
                    act.wait_ge(dve_s, DN * r + h + 1)
                    act.activation(zc[:, h, c0:HALF], zc[:, h, c0:HALF], ACT.Exp).then_inc(act_s, 1)
                for h in range(4):
                    act.wait_ge(act_s, 12 * r + h + 1)
                    if r:
                        act.wait_ge(dve_s, DN * (r - 1) + 12 + h + 1)
                    act.activation(sp[:, h, c0:HALF], zc[:, h, c0:HALF], ACT.Ln, bias=1.0).then_inc(act_s, 1)
                for h in range(4):
                    act.wait_ge(pe_s, 12 * r + 4 + h + 1)
                    if r:
                        act.wait_ge(pe_s, 12 * (r - 1) + 8 + h + 1)
                    act.activation(A[:, h, c0:HALF], m.psum[h][:, c0:HALF], ACT.Exp).then_inc(act_s, 1)


def gather_stage(m, sc, gz, y_sb, first):
    nc = m.nc
    hi, lo, turned = m.sem("gather_hi"), m.sem("gather_lo"), m.sem("gather_turned")
    gn = ROW["w_gdn_norm_2"]
    direct = [(0, sc[:, 0, :]), (1, sc[:, 1, :]), (6, y_sb[:, 0, :]), (7, y_sb[:, 1, :])]
    with nc.Block() as block:
        @block.sync
        def _(sp):
            load_first(m, sp, m.slices, first)

        @block.gpsimd
        def _(pool):
            split_first(m, pool, m.slices)

        @block.tensor
        def _(pe):
            for i in range(8):
                h, k = i // 4, i % 4
                for j in range(4):
                    mm = pe.transpose(m.psum[i][:, j * P:(j + 1) * P], gz[:, 4 * h + j, k * P:(k + 1) * P], m.ident[:, :])
                mm.then_inc(turned, 1)

        @block.scalar
        def _(act):
            for k, src in direct:
                act.activation(m.xt_hi[:, k, :], src, ACT.Copy).then_inc(hi, 1)
            for i in range(8):
                h, k = i // 4, i % 4
                act.wait_ge(turned, i + 1)
                act.activation(m.xt_hi[:, 2 + k, h * HALF:(h + 1) * HALF], m.psum[i][:, :], ACT.Identity,
                               scale=m.cols[:, gn:gn + 1]).then_inc(hi, 1)

        @block.vector
        def _(dve):
            for n, (k, src) in enumerate(direct):
                dve.wait_ge(hi, n + 1)
                dve.tensor_tensor(m.xt_lo[:, k, :], src, m.xt_hi[:, k, :].bitcast(F32), ALU.subtract).then_inc(lo, 1)
            for i in range(8):
                h, k = i // 4, i % 4
                tok = slice(h * HALF, (h + 1) * HALF)
                dve.wait_ge(hi, 4 + i + 1)
                dve.scalar_tensor_tensor(m.xt_lo[:, 2 + k, tok], m.psum[i][:, :], m.cols[:, gn:gn + 1],
                                         m.xt_hi[:, 2 + k, tok].bitcast(F32), ALU.mult, ALU.subtract).then_inc(lo, 1)


def whole_norm_stage(m, x_sb, gain, out):
    nc = m.nc
    r = m.norms
    ss, rstd = m.at(f"ss_whole{r}", [P, 16], 60), m.at(f"rstd_whole{r}", [P, 16], 60.125)
    junk_a, junk_d = m.at(f"junk_whole_a{r}", [P, D], 48), m.at(f"junk_whole_d{r}", [P, D], 52)
    g = m.at(f"gain_whole{r}", [P, D], 56)
    sq_d = m.squares["dve"]
    in_g, done, stored = (m.sem(f"{n}{r}") for n in ("in_gain", "normed", "stored"))
    with nc.Block() as block:
        @block.sync
        def _(sp):
            sp.dma_start(g[:, :], gain.rearrange("(a n) -> a n", a=1).to_broadcast([P, D])).then_inc(in_g, 16)
            for t in range(NT):
                sp.wait_ge(done, t + 1)
                sp.dma_start(out[t * P:(t + 1) * P, :], x_sb[:, t, :]).then_inc(stored, 16)
            sp.wait_ge(stored, 16 * NT)

        @block.scalar
        def _(act):
            for half in range(2):
                square_sums(m, act, "act", whole(x_sb), 1, ss, junk_a, norm_tiles(half, "act"))
                inverse_rms(m, act, 1, ss, rstd, half, sq_d + 2 * (half + 1))

        @block.vector
        def _(dve):
            for half in range(2):
                square_sums(m, dve, "dve", whole(x_sb), 1, ss, junk_d, norm_tiles(half, "dve"))
            dve.wait_ge(in_g, 16)
            for t in range(NT):
                if t % 4 == 0:
                    dve.wait_ge(m.norm_rstd, 2 * r + t // 4 + 1)
                dve.scalar_tensor_tensor(x_sb[:, t, :], x_sb[:, t, :], rstd[:, t:t + 1], g[:, :],
                                         ALU.mult, ALU.mult).then_inc(done, 1)
    m.norms += 1


def by_tile(ap):
    return ap.rearrange("(t p) n -> p t n", p=P)


def whole(tile):
    return lambda t, c0, c1: tile[:, t, c0:c1]


def program(m, out):
    a = m.a
    x_sb = m.at("x_sb", [P, NT, D], 120)
    spare = m.at("spare", [P, NT, D], 0)
    w_s_raw = m.at("w_s_raw", [P, 8, P], 184)
    w_sT = m.at("w_sT", [P, 8, P], 16)
    start_stage(m, x_sb, w_s_raw, w_sT)
    spare1 = m.at("x_scaled", [P, NT, D], 152)
    norm_stage(m, whole(x_sb), whole(spare1), 1, ROW["mix_norm_g"], 6,
               columns_of(m, a["w_in"][0], 1544))
    zu, zv = m.at("zu", [P, NT, 512], 120), m.at("zv", [P, NT, 512], 136)
    v = m.at("v", [P, NT, 512], 152)
    q, k_ = m.at("q", [P, 4, S], 168), m.at("k", [P, 4, S], 184)
    sp_f, csum = m.at("sp_f", [8, 3, S], 20), m.at("csum", [8, S], 4)
    proj1_stage(m, zu, zv, v, q, k_, sp_f, csum)
    mix1_stage(m, zv, zu, zu, zv, v, q, k_, csum, w_sT)

    def merged(t, c0, c1):
        return zv[:, t, c0:c1] if c1 <= 512 else zu[:, t, c0 - 512:c1 - 512]

    norm_stage(m, merged, merged, 2, ROW["out_norm_g"], 6, columns_of(m, a["w_out"][0], 0))
    out_proj_stage(m, a["w_out"][0], x_sb, a["x"][0])
    norm_stage(m, whole(x_sb), whole(spare), 1, ROW["ffn_norm_g"], 152, up_first(m, a["w_gate_up"][0]))
    ffn_stage(m, a["w_gate_up"][0], a["w_down"][0], x_sb, False)

    x_dram = m.nc.dram_tensor("x_between", [S, D], F32, kind="Internal").ap()
    whole_norm_stage(m, x_sb, a["final_norm_g"], x_dram)
    norm_stage(m, whole(x_sb), whole(spare), 1, ROW["w_norm_mix_2"], 152,
               columns_of(m, a["w_mix_in_2"][0], 0))
    sc = m.at("sc", [P, 6, S], 0)
    qkv = m.at("qkv", [P, 12, S], 120)
    gz = m.at("gz", [P, NT, 512], 168)
    sqk, sv = m.at("sqk", [P, 4, S], 8), m.at("sv", [P, 2, S], 24)
    ab = m.at("ab", [8, S], 192)
    proj2_stage(m, sc, qkv, gz, sqk, sv, ab)
    t_at = {"a_t": m.at("a_t", [P, HG, NT, P], 32), "kd": m.at("kd", [P, HG, NT, P], 48),
            "elast": m.at("elast", [P, HG, NT], 118.75)}
    heads = [qkv[:, 4 * i:4 * i + 4, :] for i in range(3)]
    delta_stage(m, *heads, ab, t_at)
    scan_stage(m, *heads, t_at, gz)
    y_sb = m.at("y_sb", [P, 2, S], 184)
    stick_stage(m, sqk, sv, y_sb)
    gather_stage(m, sc, gz, y_sb, columns_of(m, a["w_mix_out_2"][0], 0))
    out_proj_stage(m, a["w_mix_out_2"][0], x_sb, x_dram)
    norm_stage(m, whole(x_sb), whole(spare), 1, ROW["w_norm_ffn_2"], 152, up_first(m, a["w_ffn_up_2"][0]))
    ffn_stage(m, a["w_ffn_up_2"][0], a["w_ffn_down_2"][0], x_sb, True)
    whole_norm_stage(m, x_sb, a["w_norm_final_2"], out)


def build(nc, out, **arrays):
    with ExitStack() as ctx:
        program(setup(nc, ctx, arrays), out.rearrange("a t n -> (a t) n"))


_INS = ["x", "mix_norm_g", "w_in", "b_f", "sgu_ln_g", "sgu_ln_b", "w_s", "b_s", "out_norm_g", "w_out", "ffn_norm_g",
        "w_gate_up", "w_down", "final_norm_g", "w_norm_mix_2", "w_mix_in_2", "w_sconv_2", "w_gdn_conv_2",
        "gdn_a_log_2", "gdn_dt_bias_2", "w_gdn_norm_2", "w_mix_out_2", "w_norm_ffn_2", "w_ffn_up_2",
        "w_ffn_conv_2", "w_ffn_down_2", "w_norm_final_2"]


def kernel(**inputs):
    import numpy as _np
    import concourse.bacc as _bacc
    from concourse import mybir as _mybir
    from concourse.bass_utils import run_bass_kernel_spmd as _run

    nc = _bacc.Bacc("TRN2", target_bir_lowering=False, num_devices=1)
    arrays, args = {}, {}
    for name in _INS:
        arr = _np.ascontiguousarray(inputs[name])
        arrays[f"in_{name}_dram"] = arr
        args[name] = nc.dram_tensor(f"in_{name}_dram", arr.shape, _mybir.dt.from_np(arr.dtype), kind="ExternalInput").ap()
    out = nc.dram_tensor("out_0_dram", (1, S, D), _mybir.dt.float32, kind="ExternalOutput").ap()
    build(nc, out, **args)
    r = _run(nc, [arrays], core_ids=[0])
    return r.results[0]["out_0_dram"]
```

```python
from contextlib import ExitStack

import concourse.bass as bass
from concourse import mybir

ALU = mybir.AluOpType
ACT = mybir.ActivationFunctionType
AX = mybir.AxisListType.X
F32 = mybir.dt.float32
F32R = mybir.dt.float32r

P = 128
S = 1024
D = 1024
NT = S // P
KD = D // P
HALF = 512
NB = 8
EPS = 1e-6
NEG = -1e30
KB = 1024
BASE = 17 * KB
RING = 4
FF = 2816
FI = FF // 256
HA = 8
DH = 64
D_IN = 2568


class Machine:
    pass


def setup(nc, ctx, a):
    m = Machine()
    m.nc, m.ctx, m.a = nc, ctx, a
    m.at = lambda name, shape, off, dt=F32: nc.alloc_sbuf_tensor_at(name, shape, dt, offset=BASE + int(off * KB))
    m.psum = [ctx.enter_context(nc.psum_tensor(f"bank{b}", [P, HALF], F32)) for b in range(NB)]
    m.xt_hi = m.at("xt_hi", [P, KD, S], 32, F32R)
    m.xt_lo = m.at("xt_lo", [P, KD, S], 64, F32R)
    m.w_raw = m.at("w_raw", [P, RING, HALF], 96)
    m.w_hi = m.at("w_hi", [P, RING, HALF], 104, F32R)
    m.w_lo = m.at("w_lo", [P, RING, HALF], 112, F32R)
    m.ident = m.at("ident", [P, P], 200)
    m.causal = m.at("causal", [P, P], 200.5)
    m.sel = m.at("sel", [8, 8, P], 201)
    m.cols = m.at("cols", [P, 240], 205)
    m.zero = m.at("zero", [P, 1], 206)
    m.eps = m.at("eps", [P, 1], 206.0625)
    m.loaded = [ctx.enter_context(nc.semaphore(f"slice_loaded{u}")) for u in range(RING)]
    m.hi_done = ctx.enter_context(nc.semaphore("slice_hi_done"))
    m.split = ctx.enter_context(nc.semaphore("slice_split"))
    m.used = ctx.enter_context(nc.semaphore("slice_used"))
    m.slices = 0
    m.norms = m.turns = 0
    m.sem = lambda name: ctx.enter_context(nc.semaphore(name))
    m.bank_done = m.sem("bank_done")
    m.chunks = 0
    m.norm_square_a, m.norm_square_d = m.sem("norm_square_act"), m.sem("norm_square_dve")
    m.squares = {"act": 0, "dve": 0}
    m.norm_rstd = m.sem("norm_rstd")
    m.norm_scaled = m.sem("norm_scaled")
    m.norm_turned = m.sem("norm_turned")
    m.norm_hi = m.sem("norm_hi")
    m.norm_lo = m.sem("norm_lo")
    m.dve_step = m.sem("dve_step")
    m.act_step = m.sem("act_step")
    m.dve_steps = m.act_steps = 0
    return m


ROW = {"mix_norm_g": 0, "out_norm_g": 8, "ffn_norm_g": 16, "w_norm_mix_2": 24, "w_norm_ffn_2": 32,
       "b_s": 40, "w_sconv_2": 48, "w_gdn_conv_2": 54, "w_gdn_norm_2": 102}
ROWS1 = 103
COL_FFC = ROWS1


def load_slices(m, sp, base, first, count, source):
    with sp.Fori(1 if first == 0 else 0, count // RING) as j:
        for u in range(RING):
            sp.wait_ge(m.split, base + first + RING * j + u + 1 - RING)
            dst, src = source(j, u)
            sp.dma_start(dst, src).then_inc(m.loaded[u], 16)


def load_first(m, sp, base, source):
    for u in range(RING):
        if base:
            sp.wait_ge(m.split, base + u + 1 - RING)
        dst, src = source(u)
        sp.dma_start(dst, src).then_inc(m.loaded[u], 16)


def split_slices(m, pool, base, count, start=0):
    r0 = base // RING
    with pool.Fori(start // RING, count // RING) as j:
        for u in range(RING):
            split_slice(m, pool, base + RING * j + u, r0 + j, u, False)


def split_slice(m, pool, n, r, u, fresh):
    zeros = m.zero[:, 0:1].to_broadcast([P, HALF])
    if not fresh:
        pool.wait_ge(m.used, n + 1 - RING)
    pool.wait_ge(m.loaded[u], 16 * r + 16)
    pool.tensor_tensor(m.w_hi[:, u, :], m.w_raw[:, u, :], zeros, ALU.add).then_inc(m.hi_done, 1)
    pool.wait_ge(m.hi_done, n + 1)
    pool.tensor_tensor(m.w_lo[:, u, :], m.w_raw[:, u, :], m.w_hi[:, u, :].bitcast(F32),
                       ALU.subtract).then_inc(m.split, 1)


def split_first(m, pool, base):
    for u in range(RING):
        split_slice(m, pool, base + u, base // RING, u, base == 0)


def columns_of(m, w, col):
    return lambda u: (m.w_raw[:, u, :], w[u * P:(u + 1) * P, col:col + HALF])


def in_turn(m, eng, name):
    sem = m.dve_step if name == "dve" else m.act_step

    def step(ins):
        if name == "dve":
            m.dve_steps += 1
            n = m.dve_steps
        else:
            m.act_steps += 1
            n = m.act_steps
        ins.then_inc(sem, 1)
        eng.wait_ge(sem, n)

    return step


def chunk_products(m, pe, base, chunk, token_major, wait_bank=None):
    for k in range(KD):
        u = k % RING
        pe.wait_ge(m.split, base + k + 1)
        for b in range(NB):
            if k == 0 and wait_bank is not None:
                wait_bank(b)
            if token_major:
                col, tok = slice(0, HALF), slice(b * P, (b + 1) * P)
                pairs = [(m.xt_hi, m.w_hi), (m.xt_hi, m.w_lo), (m.xt_lo, m.w_hi)]
                pairs = [(x[:, k, tok], w[:, u, col]) for x, w in pairs]
            else:
                h, n = b // 4, b % 4
                col, tok = slice(n * P, (n + 1) * P), slice(h * HALF, (h + 1) * HALF)
                pairs = [(m.w_hi, m.xt_hi), (m.w_hi, m.xt_lo), (m.w_lo, m.xt_hi)]
                pairs = [(w[:, u, col], x[:, k, tok]) for w, x in pairs]
            for i, (lhs, rhs) in enumerate(pairs):
                mm = pe.matmul(m.psum[b][:, :], lhs, rhs, start=k == 0 and i == 0, stop=k == KD - 1 and i == 2)
            if b == NB - 1:
                mm.then_inc(m.used, 1)
            elif k == KD - 1:
                mm.then_inc(m.bank_done, 1)


def wait_chunk_bank(m, eng, base, chunk, b):
    if b == NB - 1:
        eng.wait_ge(m.used, base + KD)
    else:
        eng.wait_ge(m.bank_done, (NB - 1) * chunk + b + 1)


def square_sums(m, eng, name, src, halves, ss, junk, tiles):
    width = D // halves
    for t in tiles:
        for g in range(halves):
            x, out, acc = src(t, g * width, (g + 1) * width), junk[:, g * width:(g + 1) * width], ss[:, g * NT + t:g * NT + t + 1]
            sem = m.norm_square_a if name == "act" else m.norm_square_d
            n = m.squares[name]
            if n:
                eng.wait_ge(sem, n)
            if name == "act":
                ins = eng.activation(out, x, ACT.Square, accum_out=acc)
            else:
                ins = eng.tensor_tensor_reduce(out, x, x, 1.0, 0.0, ALU.mult, ALU.add, acc)
            ins.then_inc(sem, 1)
            m.squares[name] += 1


def inverse_rms(m, act, halves, ss, rstd, half, squares_d):
    act.wait_ge(m.norm_square_a, m.squares["act"])
    act.wait_ge(m.norm_square_d, squares_d)
    step = in_turn(m, act, "act")
    pick = lambda t: t[:, 0:halves * NT].rearrange("p (g t) -> p g t", t=NT)[:, :, 4 * half:4 * half + 4]
    step(act.activation(pick(rstd), pick(ss), ACT.Ln, scale=halves / D, bias=m.eps[:, 0:1]))
    act.activation(pick(rstd), pick(rstd), ACT.Exp, scale=-0.5).then_inc(m.norm_rstd, 1)


def norm_tiles(half, name):
    return (4 * half, 4 * half + 1) if name == "act" else (4 * half + 2, 4 * half + 3)


def norm_stage(m, src, dst, halves, gcol, scratch, first=None):
    nc = m.nc
    r, turns = m.norms, m.turns
    ss = m.at(f"ss{r}", [P, 16], scratch + 8)
    rstd = m.at(f"rstd{r}", [P, 16], scratch + 8.0625)
    junk_a, junk_d = m.at(f"junk_a{r}", [P, D], scratch), m.at(f"junk_d{r}", [P, D], scratch + 4)
    sq_d = m.squares["dve"]
    with nc.Block() as block:
        if first is not None:
            @block.sync
            def _(sp):
                load_first(m, sp, m.slices, first)

            @block.gpsimd
            def _(pool):
                split_first(m, pool, m.slices)

        @block.scalar
        def _(act):
            for half in range(2):
                square_sums(m, act, "act", src, halves, ss, junk_a, norm_tiles(half, "act"))
                inverse_rms(m, act, halves, ss, rstd, half, sq_d + 2 * halves * (half + 1))
            for i in range(2 * KD):
                h, k = i // KD, i % KD
                act.wait_ge(m.norm_turned, 16 * turns + i + 1)
                act.activation(m.xt_hi[:, k, h * HALF:(h + 1) * HALF], m.psum[i % NB][:, :], ACT.Identity,
                               scale=m.cols[:, gcol + k:gcol + k + 1]).then_inc(m.norm_hi, 1)

        @block.vector
        def _(dve):
            for half in range(2):
                square_sums(m, dve, "dve", src, halves, ss, junk_d, norm_tiles(half, "dve"))
            width = D // halves
            for t in range(NT):
                if t % 4 == 0:
                    dve.wait_ge(m.norm_rstd, 2 * r + t // 4 + 1)
                for g in range(halves):
                    ins = dve.tensor_scalar(dst(t, g * width, (g + 1) * width), src(t, g * width, (g + 1) * width),
                                            rstd[:, g * NT + t:g * NT + t + 1], None, ALU.mult)
                ins.then_inc(m.norm_scaled, 1)
            for i in range(2 * KD):
                h, k = i // KD, i % KD
                dve.wait_ge(m.norm_hi, 16 * turns + i + 1)
                tok = slice(h * HALF, (h + 1) * HALF)
                dve.scalar_tensor_tensor(m.xt_lo[:, k, tok], m.psum[i % NB][:, :],
                                         m.cols[:, gcol + k:gcol + k + 1], m.xt_hi[:, k, tok].bitcast(F32),
                                         ALU.mult, ALU.subtract).then_inc(m.norm_lo, 1)

        @block.tensor
        def _(pe):
            for i in range(2 * KD):
                h, k = i // KD, i % KD
                if k == 0:
                    pe.wait_ge(m.norm_scaled, NT * turns + 4 * (h + 1))
                if i >= NB:
                    pe.wait_ge(m.norm_lo, 16 * turns + i + 1 - NB)
                for j in range(4):
                    mm = pe.transpose(m.psum[i % NB][:, j * P:(j + 1) * P],
                                      dst(4 * h + j, k * P, (k + 1) * P), m.ident[:, :])
                mm.then_inc(m.norm_turned, 1)
    m.norms += 1
    m.turns += 1


def start_stage(m, x_sb, w_s_raw, w_sT):
    nc, a = m.nc, m.a
    rows = m.at("vector_rows", [P, 3, P], 176)
    in_x, in_rows = m.sem("in_x"), m.sem("in_rows")
    made, masked, turned, cols_done = m.sem("made"), m.sem("masked"), m.sem("vec_turned"), m.sem("cols_done")
    in_ws = m.sem("in_ws")
    with nc.Block() as block:
        @block.sync
        def _(sp):
            for t in range(NT):
                sp.dma_start(x_sb[:, t, :], a["x"][0, t * P:(t + 1) * P, :]).then_inc(in_x, 16)
            sp.wait_ge(made, 7)
            for name in ("mix_norm_g", "out_norm_g", "ffn_norm_g", "w_norm_mix_2", "w_norm_ffn_2", "b_s",
                         "w_sconv_2", "w_gdn_conv_2", "w_gdn_norm_2"):
                v = a[name]
                flat = v.rearrange("a b -> (a b)") if len(v.shape) == 2 else v.rearrange("a b c -> (a b c)")
                n = flat.shape[0] // P
                sp.dma_start(rows[ROW[name]:ROW[name] + n, 0, :],
                             flat.rearrange("(r p) -> r p", p=P)).then_inc(in_rows, 16)
            f = a["w_ffn_conv_2"].rearrange("a b c -> (a b c)").rearrange("(r p) -> r p", p=P)
            sp.dma_start(rows[0:88, 1, :], f[0:88, :]).then_inc(in_rows, 16)
            sp.dma_start(rows[0:44, 2, :], f[88:132, :]).then_inc(in_rows, 16)
            sp.dma_start(w_s_raw[:, :, :], a["w_s"].rearrange("a g i j -> i (a g) j")).then_inc(in_ws, 16)
            sp.wait_ge(in_x, 16 * NT)

        @block.gpsimd
        def _(pool):
            pool.memset(m.ident[:, :], 0.0).then_inc(made, 1)
            pool.memset(m.causal[:, :], 0.0).then_inc(made, 1)
            pool.memset(m.sel[:, :, :], 0.0).then_inc(made, 1)
            pool.memset(m.zero[:, :], 0.0).then_inc(made, 1)
            pool.memset(m.eps[:, :], EPS).then_inc(made, 1)
            pool.memset(rows[:, :, :], 0.0).then_inc(made, 1)
            pool.memset(m.cols[:, :], 0.0).then_inc(made, 1)
            pool.wait_ge(made, 7)
            pool.affine_select(out=m.ident[:, :], in_=m.ident[:, :], compare_op=ALU.not_equal, fill=1.0,
                               base=0, pattern=[[-1, P]], channel_multiplier=1).then_inc(masked, 1)
            pool.affine_select(out=m.causal[:, :], in_=m.causal[:, :], compare_op=ALU.is_ge, fill=NEG,
                               base=0, pattern=[[-1, P]], channel_multiplier=1).then_inc(masked, 1)
            pool.affine_select(out=m.sel[:, :, :], in_=m.sel[:, :, :], compare_op=ALU.not_equal, fill=1.0,
                               base=0, pattern=[[-1, 8], [0, P]], channel_multiplier=1).then_inc(masked, 1)
            pool.wait_ge(masked, 3)

        @block.tensor
        def _(pe):
            pe.wait_ge(masked, 3)
            pe.wait_ge(in_rows, 16 * 11)
            for j in range(3):
                mm = pe.transpose(m.psum[0][:, j * P:(j + 1) * P], rows[:, j, :], m.ident[:, :])
            mm.then_inc(turned, 1)
            pe.wait_ge(in_ws, 16)
            for g in range(8):
                mm = pe.transpose(m.psum[1 + g // 4][:, (g % 4) * P:(g % 4 + 1) * P], w_s_raw[:, g, :], m.ident[:, :])
            mm.then_inc(turned, 1)

        @block.vector
        def _(dve):
            dve.wait_ge(turned, 1)
            dve.wait_ge(made, 7)
            dve.tensor_copy(m.cols[:, 0:ROWS1], m.psum[0][:, 0:ROWS1]).then_inc(cols_done, 1)
            dve.tensor_copy(m.cols[:, COL_FFC:COL_FFC + 88], m.psum[0][:, P:P + 88]).then_inc(cols_done, 1)
            dve.tensor_copy(m.cols[:, COL_FFC + 88:COL_FFC + 132], m.psum[0][:, 2 * P:2 * P + 44]).then_inc(cols_done, 1)
            dve.wait_ge(turned, 2)
            for c in range(2):
                dve.tensor_copy(w_sT[:, 4 * c:4 * c + 4, :],
                                m.psum[1 + c][:, :].rearrange("p (g i) -> p g i", g=4)).then_inc(cols_done, 1)
            dve.wait_ge(cols_done, 5)
            dve.memset(w_sT[64:P, :, 0:64], 0.0).then_inc(cols_done, 1)
            dve.wait_ge(cols_done, 6)


def proj1_stage(m, zu, zv, v, q, k_, sp_f, csum):
    nc, a = m.nc, m.a
    base, c0 = m.slices, m.chunks
    w = a["w_in"][0]
    lng, lnb = m.at("ln_g", [P, 512], 0), m.at("ln_b", [P, 512], 2)
    wf = m.at("w_f", [P, KD, 8], 12)
    wf_hi, wf_lo = m.at("w_f_hi", [P, KD, 8], 12.25, F32R), m.at("w_f_lo", [P, KD, 8], 12.5, F32R)
    bf = m.at("b_f_col", [8, 1], 12.75)
    stats, mv, ln_r = m.at("ln_stats", [P, NT, 6], 13), m.at("ln_mv", [P, NT, 2], 13.25), m.at("ln_rstd", [P, NT], 13.5)
    in_small, evac, f_split, f_done = m.sem("in_small"), m.sem("p1_evac"), m.sem("f_split"), m.sem("f_done")
    sp_done, lnr, stat_done, f_evac = m.sem("softplus_done"), m.sem("ln_rstd_done"), m.sem("ln_stat"), m.sem("f_evac")
    cols = [1544, 1544 + 512, 1024, 0, 512]

    with nc.Block() as block:
        @block.sync
        def _(sp):
            sp.dma_start(wf[:, :, :], w[:, 1536:1544].rearrange("(k p) n -> p k n", p=P)).then_inc(in_small, 16)
            sp.dma_start(bf[:, :], a["b_f"].rearrange("a h -> h a")).then_inc(in_small, 16)
            sp.dma_start(lng[:, :], a["sgu_ln_g"].to_broadcast([P, 512])).then_inc(in_small, 16)
            sp.dma_start(lnb[:, :], a["sgu_ln_b"].to_broadcast([P, 512])).then_inc(in_small, 16)
            for c, col in enumerate(cols):
                load_slices(m, sp, base, 8 * c, 8, lambda j, u: (
                    m.w_raw[:, u, :], w[bass.ds((j * RING + u) * P, P), col:col + HALF]))
            sp.wait_ge(in_small, 64)

        @block.gpsimd
        def _(pool):
            pool.wait_ge(in_small, 64)
            pool.tensor_tensor(wf_hi[:, :, :], wf[:, :, :], m.zero[:, 0:1].unsqueeze(2).to_broadcast([P, KD, 8]), ALU.add).then_inc(f_split, 1)
            pool.wait_ge(f_split, 1)
            pool.tensor_tensor(wf_lo[:, :, :], wf[:, :, :], wf_hi[:, :, :].bitcast(F32), ALU.subtract).then_inc(f_split, 1)
            split_slices(m, pool, base, 40, RING)

        @block.tensor
        def _(pe):
            pe.wait_ge(f_split, 2)
            for h in range(2):
                tok = slice(h * HALF, (h + 1) * HALF)
                for k in range(KD):
                    pe.matmul(m.psum[h][0:8, :], wf_hi[:, k, :], m.xt_hi[:, k, tok], start=k == 0, stop=False)
                    pe.matmul(m.psum[h][0:8, :], wf_hi[:, k, :], m.xt_lo[:, k, tok], start=False, stop=False)
                    mm = pe.matmul(m.psum[h][0:8, :], wf_lo[:, k, :], m.xt_hi[:, k, tok], start=False, stop=k == KD - 1)
                mm.then_inc(f_done, 1)
            for c in range(5):
                def wait_bank(b):
                    if c == 0 and b < 2:
                        pe.wait_ge(f_evac, b + 1)
                    if c >= 1:
                        pe.wait_ge(evac, 8 * (c - 1) + b + 1)
                chunk_products(m, pe, base + 8 * c, c0 + c, c < 3, wait_bank)

        @block.scalar
        def _(act):
            act.wait_ge(in_small, 64)
            for h in range(2):
                act.wait_ge(f_done, h + 1)
                act.activation(sp_f[:, 0, h * HALF:(h + 1) * HALF], m.psum[h][0:8, :], ACT.Identity,
                               bias=bf[:, 0:1]).then_inc(f_evac, 1)
            act.wait_ge(f_evac, 2)
            step = in_turn(m, act, "act")
            step(act.activation(sp_f[:, 1, :], sp_f[:, 0, :], ACT.Abs))
            step(act.activation(sp_f[:, 1, :], sp_f[:, 1, :], ACT.Exp, scale=-1.0))
            act.activation(sp_f[:, 1, :], sp_f[:, 1, :], ACT.Ln, bias=1.0).then_inc(sp_done, 1)
            for c in range(3):
                for b in range(NB):
                    wait_chunk_bank(m, act, base + 8 * c, c0 + c, b)
                    if c == 2:
                        ins = act.activation(v[:, b, :], m.psum[b][:, :], ACT.Copy)
                    else:
                        ins = act.activation((zu, zv)[c][:, b, :], m.psum[b][:, :], ACT.Gelu)
                    ins.then_inc(evac, 1)
            act.wait_ge(stat_done, NT)
            step(act.activation(ln_r[:, :], mv[:, :, 1], ACT.Ln, bias=m.eps[:, 0:1]))
            act.activation(ln_r[:, :], ln_r[:, :], ACT.Exp, scale=-0.5).then_inc(lnr, 1)

        @block.vector
        def _(dve):
            step = in_turn(m, dve, "dve")
            dve.wait_ge(f_evac, 2)
            step(dve.tensor_scalar(sp_f[:, 2, :], sp_f[:, 0, :], -1.0, 0.0, ALU.mult, ALU.max))
            dve.wait_ge(sp_done, 1)
            step(dve.tensor_tensor(sp_f[:, 1, :], sp_f[:, 1, :], sp_f[:, 2, :], ALU.add))
            step(dve.memset(sp_f[:, 2, :], 1.0))
            step(dve.tensor_tensor_scan(csum[:, :], sp_f[:, 2, :], sp_f[:, 1, :], 0.0, ALU.mult, ALU.add))
            for t in range(NT):
                dve.wait_ge(evac, 8 + t + 1)
                step(dve.bn_stats(stats[:, t, :], zv[:, t, :]))
                dve.bn_aggr(mv[:, t, :], stats[:, t, :]).then_inc(stat_done, 1)
            dve.wait_ge(lnr, 1)
            for t in range(NT):
                step(dve.tensor_scalar(zv[:, t, :], zv[:, t, :], mv[:, t, 0:1], ln_r[:, t:t + 1],
                                       ALU.subtract, ALU.mult))
                step(dve.tensor_tensor(zv[:, t, :], zv[:, t, :], lng[:, :], ALU.mult))
                step(dve.tensor_tensor(zv[:, t, :], zv[:, t, :], lnb[:, :], ALU.add))
            for c in range(2):
                for b in range(NB):
                    wait_chunk_bank(m, dve, base + 8 * (3 + c), c0 + 3 + c, b)
                    h, n = b // 4, b % 4
                    dve.tensor_scalar((q, k_)[c][:, n, h * HALF:(h + 1) * HALF], m.psum[b][:, :],
                                      (DH ** -0.5, 1.0)[c], None, ALU.mult).then_inc(evac, 1)
    m.slices += 40
    m.chunks += 5


def mix1_stage(m, attn, gated, zu, zv, v, q, k_, csum, w_sT):
    nc = m.nc
    cb, cbd = m.at("c_rows", [P, S], 32), m.at("c_rows_masked", [P, NT, P], 36)
    sc = m.at("scores", [P, 3, S], 64)
    pt = m.at("probs_t", [P, 2, NT, P], 48)
    nm, ls, rl, m0 = (m.at(n, [P, 64], 56 + i / 4) for i, n in enumerate(("neg_max", "sums", "inv_sums", "max0")))
    mx = m.at("row_max", [P, 64], 57)
    units = [(h, i) for h in range(HA) for i in (7, 0, 6, 1, 5, 2, 4, 3)]
    NU = len(units)
    sgu, sgu_out = m.sem("sgu"), m.sem("sgu_out")
    qk, scored, expd, turned = m.sem("qk"), m.sem("scored"), m.sem("probs"), m.sem("probs_turned")
    pta, ptd, pv, outd = m.sem("probs_t_act"), m.sem("probs_t_dve"), m.sem("pv"), m.sem("attn_out")
    cbp, cbs, mxs, nms = m.sem("c_bcast"), m.sem("c_rows_done"), m.sem("max_done"), m.sem("neg_max_done")

    def bank1(u):
        return sum(1 for x in units[:u + 1] if x[1] >= 4)

    with nc.Block() as block:
        @block.tensor
        def _(pe):
            for g in range(8):
                pe.matmul(m.psum[g][:, :], w_sT[:, g, :], zv[:, :, g * 64:(g + 1) * 64],
                          start=True, stop=True).then_inc(sgu, 1)

            def scores(u):
                h, i = units[u]
                if u % NT == 0:
                    if u:
                        pe.wait_ge(cbs, 2 * h)
                    else:
                        pe.wait_ge(sgu_out, 8)
                    for c in range(2):
                        if c:
                            pe.wait_ge(cbs, 2 * h + 1)
                        pe.matmul(m.psum[7][:, :], m.sel[0:8, h, :], csum[:, c * HALF:(c + 1) * HALF],
                                  start=True, stop=True).then_inc(cbp, 1)
                r, n = 64 * (h % 2), (i + 1) * P
                if u >= 2:
                    pe.wait_ge(scored, u - 1)
                for c in range(0, n, HALF):
                    e = min(n, c + HALF)
                    mm = pe.matmul(m.psum[2 * (u % 2) + c // HALF][:, 0:e - c], q[r:r + 64, h // 2, i * P:(i + 1) * P],
                                   k_[r:r + 64, h // 2, c:e], start=True, stop=True)
                mm.then_inc(qk, 1)

            def turn(u):
                h, i = units[u]
                pe.wait_ge(expd, u + 1)
                if u:
                    pe.wait_ge(pta, u)
                    if bank1(u - 1):
                        pe.wait_ge(ptd, bank1(u - 1))
                for j in range(i + 1):
                    mm = pe.transpose(m.psum[4 + j // 4][:, (j % 4) * P:(j % 4 + 1) * P],
                                      sc[:, u % 3, j * P:(j + 1) * P], m.ident[:, :])
                mm.then_inc(turned, 1)

            def values(u):
                h, i = units[u]
                pe.wait_ge(pta, u + 1)
                if i >= 4:
                    pe.wait_ge(ptd, bank1(u))
                if u:
                    pe.wait_ge(outd, u)
                for j in range(i + 1):
                    mm = pe.matmul(m.psum[6][:, 64 * (u % 2):64 * (u % 2) + 64], pt[:, u % 2, j, :],
                                   v[:, j, h * DH:(h + 1) * DH], start=j == 0, stop=j == i)
                mm.then_inc(pv, 1)

            scores(0)
            scores(1)
            for u in range(NU):
                if u + 2 < NU:
                    scores(u + 2)
                turn(u)
                if u:
                    values(u - 1)
            values(NU - 1)

        @block.vector
        def _(dve):
            for g in range(8):
                dve.wait_ge(sgu, g + 1)
                dve.scalar_tensor_tensor(gated[:, :, g * 64:(g + 1) * 64],
                                         m.psum[g][:, :].rearrange("p (c d) -> p c d", c=NT),
                                         m.cols[:, ROW["b_s"] + g:ROW["b_s"] + g + 1],
                                         zu[:, :, g * 64:(g + 1) * 64], ALU.add, ALU.mult).then_inc(sgu_out, 1)

            def score(u):
                h, i = units[u]
                if u % NT == 0:
                    for c in range(2):
                        dve.wait_ge(cbp, 2 * h + c + 1)
                        dve.tensor_copy(cb[:, c * HALF:(c + 1) * HALF], m.psum[7][:, :]).then_inc(cbs, 1)
                    dve.wait_ge(cbs, 2 * h + 2)
                    dve.tensor_tensor(cbd[:, :, :], cb[:, :].rearrange("p (t n) -> p t n", n=P),
                                      m.causal[:, :].unsqueeze(1).to_broadcast([P, NT, P]), ALU.add).then_inc(m.dve_step, 1)
                    m.dve_steps += 1
                    dve.wait_ge(m.dve_step, m.dve_steps)
                s = u % 2
                dve.wait_ge(qk, u + 1)
                if u >= 3:
                    dve.wait_ge(turned, u - 2)
                c0, d0 = i // 4, (i % 4) * P
                first = m0 if i else mx
                ins = dve.tensor_tensor_reduce(sc[:, u % 3, i * P:(i + 1) * P], m.psum[2 * s + c0][:, d0:d0 + P],
                                               cbd[:, i, :], 1.0, NEG * 10, ALU.add, ALU.max, first[:, u:u + 1])
                ins.then_inc(mxs, 1)
                nmx[0] += 1
                dve.wait_ge(mxs, nmx[0])
                parts = [(c, min(i * P, c + HALF)) for c in range(0, i * P, HALF)]
                for n, (c, e) in enumerate(parts):
                    src = m0 if n == 0 else mx2
                    dst = mx if n == len(parts) - 1 else mx2
                    ins = dve.tensor_tensor_reduce(sc[:, u % 3, c:e], m.psum[2 * s + c // HALF][:, 0:e - c],
                                                   cb[:, c:e], 1.0, src[:, u:u + 1], ALU.add, ALU.max, dst[:, u:u + 1])
                    ins.then_inc(mxs, 1)
                    nmx[0] += 1
                    dve.wait_ge(mxs, nmx[0])
                dve.tensor_scalar(nm[:, u:u + 1], mx[:, u:u + 1], -1.0, None, ALU.mult).then_inc(scored, 1)

            def out(u):
                h, i = units[u]
                dve.wait_ge(m.dve_step, inverse[u])
                dve.wait_ge(pv, u + 1)
                dve.tensor_scalar(attn[:, i, h * DH:(h + 1) * DH], m.psum[6][:, 64 * (u % 2):64 * (u % 2) + 64],
                                  rl[:, u:u + 1], None, ALU.mult).then_inc(outd, 1)

            step = in_turn(m, dve, "dve")
            nmx = [0]
            inverse = {}
            mx2 = m.at("max1", [P, 64], 57.25)
            score(0)
            score(1)
            for u in range(NU):
                if u:
                    dve.wait_ge(expd, u)
                    dve.reciprocal(rl[:, u - 1:u], ls[:, u - 1:u]).then_inc(m.dve_step, 1)
                    m.dve_steps += 1
                    inverse[u - 1] = m.dve_steps
                if u + 2 < NU:
                    score(u + 2)
                if u:
                    out(u - 1)
            dve.wait_ge(expd, NU)
            dve.reciprocal(rl[:, NU - 1:NU], ls[:, NU - 1:NU]).then_inc(m.dve_step, 1)
            m.dve_steps += 1
            inverse[NU - 1] = m.dve_steps
            out(NU - 1)

        @block.scalar
        def _(act):
            def turned_probs(u):
                h, i = units[u]
                act.wait_ge(turned, u + 1)
                if u >= 2:
                    act.wait_ge(pv, u - 1)
                n = min(i + 1, 4)
                act.activation(pt[:, u % 2, 0:n, :], m.psum[4][:, 0:n * P].rearrange("p (j n) -> p j n", n=P),
                               ACT.Copy).then_inc(pta, 1)

            def second_bank(u):
                h, i = units[u]
                if i >= 4:
                    act.wait_ge(turned, u + 1)
                    if u >= 2:
                        act.wait_ge(pv, u - 1)
                    act.activation(pt[:, u % 2, 4:i + 1, :],
                                    m.psum[5][:, 0:(i - 3) * P].rearrange("p (j n) -> p j n", n=P), ACT.Copy).then_inc(ptd, 1)

            for u in range(NU):
                h, i = units[u]
                act.wait_ge(scored, u + 1)
                act.activation(sc[:, u % 3, 0:(i + 1) * P], sc[:, u % 3, 0:(i + 1) * P], ACT.Exp,
                               bias=nm[:, u:u + 1], accum_out=ls[:, u:u + 1]).then_inc(expd, 1)
                if u:
                    turned_probs(u - 1)
                    second_bank(u - 1)
            turned_probs(NU - 1)
            second_bank(NU - 1)


def out_proj_stage(m, w, x_sb, load_x=None):
    nc = m.nc
    base, c0 = m.slices, m.chunks
    n = m.chunks
    evac = m.sem(f"out_evac{n}")
    in_x = m.sem(f"out_x{n}") if load_x is not None else None
    with nc.Block() as block:
        @block.sync
        def _(sp):
            for c in range(2):
                load_slices(m, sp, base, 8 * c, 8, lambda j, u: (
                    m.w_raw[:, u, :], w[bass.ds((j * RING + u) * P, P), c * HALF:(c + 1) * HALF]))
                if c == 0 and load_x is not None:
                    for t in range(NT):
                        sp.dma_start(x_sb[:, t, :], load_x[t * P:(t + 1) * P, :]).then_inc(in_x, 16)

        @block.gpsimd
        def _(pool):
            split_slices(m, pool, base, 16, RING)

        @block.tensor
        def _(pe):
            for c in range(2):
                chunk_products(m, pe, base + 8 * c, c0 + c, True,
                               (lambda b: pe.wait_ge(evac, 8 * (c - 1) + b + 1)) if c else None)

        @block.vector
        def _(dve):
            if load_x is not None:
                dve.wait_ge(in_x, 16 * NT)
            for c in range(2):
                for b in range(NB):
                    wait_chunk_bank(m, dve, base + 8 * c, c0 + c, b)
                    xs = x_sb[:, b, c * HALF:(c + 1) * HALF]
                    dve.tensor_tensor(xs, m.psum[b][:, :], xs, ALU.add).then_inc(evac, 1)
    m.slices += 16
    m.chunks += 2


def up_first(m, w_up):
    v = w_up.rearrange("k (s n) -> k s n", s=2)
    return lambda u: (m.w_raw[:, u, :].rearrange("p (s n) -> p s n", s=2), v[u * P:(u + 1) * P, :, 0:256])


def ffn_stage(m, w_up, w_down, x_sb, conv):
    nc = m.nc
    base, c0, tag = m.slices, m.chunks, "_conv" if conv else ""
    PAD = 2
    raw = m.at("hidden_raw" + tag, [P, 4, PAD + S], 152)
    hid_hi = m.at("hidden_hi" + tag, [P, 2, S], 169, F32R)
    hid_lo = m.at("hidden_lo" + tag, [P, 2, S], 177, F32R)
    mix = m.at("hidden" + tag, [P, 4, S], 0)
    up_v = w_up.rearrange("k (s n) -> k s n", s=2)
    ev_a, ev_d, dn_done, dn_ev = (m.sem(n + tag) for n in ("gate_read", "up_read", "down_done", "down_read"))
    hid, hid_a, acted, sig, tap = (m.sem(n + tag) for n in ("hidden_done", "hidden_hi_done", "hidden_prod", "silu_done", "tap_done"))
    GU, DN = 8, 4

    with nc.Block() as block:
        @block.sync
        def _(sp):
            def up_slices(first, i, start=0):
                for k in range(start, GU):
                    u, n = k % RING, first + k
                    sp.wait_ge(m.split, n + 1 - RING)
                    sp.dma_start(m.w_raw[:, u, :].rearrange("p (s n) -> p s n", s=2),
                                 up_v[k * P:(k + 1) * P, :, bass.ds(i * 256, 256)]).then_inc(m.loaded[u], 16)

            def down_slices(first, i):
                for u in range(DN):
                    sp.wait_ge(m.split, first + u + 1 - RING)
                    sp.dma_start(m.w_raw[:, u, :], w_down[bass.ds(i * 256 + (u % 2) * P, P),
                                                          (u // 2) * HALF:(u // 2 + 1) * HALF]).then_inc(m.loaded[u], 16)

            up_slices(base, 0, RING)
            with sp.Fori(0, FI - 1) as i:
                up_slices(base + GU + 12 * i, i + 1)
                down_slices(base + 2 * GU + 12 * i, i)
            down_slices(base + GU + 12 * (FI - 1), FI - 1)

        @block.gpsimd
        def _(pool):
            split_slices(m, pool, base, 12 * FI, RING)

        @block.tensor
        def _(pe):
            def up(first, wait_bank):
                for k in range(KD):
                    u = k % RING
                    pe.wait_ge(m.split, first + k + 1)
                    for b in range(NB):
                        if k == 0 and wait_bank is not None:
                            wait_bank(b)
                        h, j, s = b // 4, (b // 2) % 2, b % 2
                        col, tok = slice((2 * s + j) * P, (2 * s + j + 1) * P), slice(h * HALF, (h + 1) * HALF)
                        pe.matmul(m.psum[b][:, :], m.w_hi[:, u, col], m.xt_hi[:, k, tok], start=k == 0, stop=False)
                        pe.matmul(m.psum[b][:, :], m.w_hi[:, u, col], m.xt_lo[:, k, tok], start=False, stop=False)
                        mm = pe.matmul(m.psum[b][:, :], m.w_lo[:, u, col], m.xt_hi[:, k, tok],
                                       start=False, stop=k == KD - 1)
                        if b == NB - 1:
                            mm.then_inc(m.used, 1)
                        elif k == KD - 1:
                            mm.then_inc(m.bank_done, 1)

            def down(first, i, last):
                for nh in range(2):
                    for t in range(NT):
                        if nh == 0:
                            if t == 0:
                                pe.wait_ge(m.split, first + 2)
                            if t in (0, 4):
                                pe.wait_ge(hid, 4 * i + 2 * (t // 4) + 2)
                            if not last:
                                pe.wait_ge(ev_d if t % 2 else ev_a, 4 * (i + 1) + t // 2 + 1)
                        else:
                            if t == 0:
                                pe.wait_ge(m.split, first + 4)
                            pe.wait_ge(dn_ev, 16 * i + t + 2)
                        for j in range(2):
                            u, tok = 2 * nh + j, slice(t * P, (t + 1) * P)
                            pe.matmul(m.psum[t][:, :], hid_hi[:, j, tok], m.w_hi[:, u, :], start=j == 0, stop=False)
                            pe.matmul(m.psum[t][:, :], hid_lo[:, j, tok], m.w_hi[:, u, :], start=False, stop=False)
                            mm = pe.matmul(m.psum[t][:, :], hid_hi[:, j, tok], m.w_lo[:, u, :], start=False, stop=j == 1)
                            if t == NT - 1 and j == 0:
                                mm.then_inc(m.used, 1)
                        mm.then_inc(m.used if t == NT - 1 else dn_done, 1)

            up(base, None)
            with pe.Fori(0, FI - 1) as i:
                def wait_bank(b):
                    pe.wait_ge(ev_d if b % 2 else ev_a, 4 * i + b // 2 + 1)
                    pe.wait_ge(dn_ev, 16 * i + 1)
                up(base + GU + 12 * i, wait_bank)
                down(base + 2 * GU + 12 * i, i, False)
            down(base + GU + 12 * (FI - 1), FI - 1, True)

        def bank_full(eng, first, i, b):
            if b == NB - 1:
                eng.wait_ge(m.used, first + GU)
            else:
                eng.wait_ge(m.bank_done, 7 * (c0 + i) + b + 1)

        def weights_of(i, c, tap_):
            return m.cols[:, bass.ds(COL_FFC + 44 * tap_ + 22 * (c // 2) + c % 2 + 2 * i, 1)]

        @block.scalar
        def _(act):
            def read_gate(first, i):
                for q_ in range(4):
                    h, j = q_ // 2, q_ % 2
                    bank_full(act, first, i, 2 * q_)
                    act.activation(raw[:, j, PAD + h * HALF:PAD + (h + 1) * HALF], m.psum[2 * q_][:, :],
                                   ACT.Copy if conv else ACT.Silu).then_inc(ev_a, 1)

            def finish(i):
                if conv:
                    act.wait_ge(ev_a, 4 * i + 4)
                    act.wait_ge(ev_d, 4 * i + 4)
                    for c in range(4):
                        act.activation(mix[:, c, :], raw[:, c, PAD:PAD + S], ACT.Identity,
                                       scale=weights_of(i, c, 2)).then_inc(tap, 1)
                    for c in range(2):
                        act.wait_ge(acted, 4 * i + c + 1)
                        act.activation(mix[:, c, :], mix[:, c, :], ACT.Silu).then_inc(sig, 1)
                for q_ in range(4):
                    h, j = q_ // 2, q_ % 2
                    tok = slice(h * HALF, (h + 1) * HALF)
                    act.wait_ge(hid_a, 4 * i + q_ + 1)
                    act.activation(hid_hi[:, j, tok], mix[:, j, tok], ACT.Copy).then_inc(sig2, 1)

            sig2 = m.sem("hidden_rounded" + tag)
            m.sig2 = sig2
            read_gate(base, 0)
            finish(0)
            with act.Fori(1, FI) as i:
                act.wait_ge(hid, 4 * i)
                read_gate(base + GU + 12 * (i - 1), i)
                finish(i)

        @block.vector
        def _(dve):
            sig2 = m.sig2
            dve.memset(raw[:, :, 0:PAD], 0.0).then_inc(dn_ev, 1)
            dve.wait_ge(dn_ev, 1)

            def read_up(first, i):
                for q_ in range(4):
                    h, j = q_ // 2, q_ % 2
                    bank_full(dve, first, i, 2 * q_ + 1)
                    dve.tensor_copy(raw[:, 2 + j, PAD + h * HALF:PAD + (h + 1) * HALF],
                                    m.psum[2 * q_ + 1][:, :]).then_inc(ev_d, 1)

            def finish(i):
                if conv:
                    for n, c in enumerate((0, 1, 2, 3)):
                        dve.wait_ge(tap, 4 * i + n + 1)
                        for back in (1, 2):
                            ins = dve.scalar_tensor_tensor(mix[:, c, :], raw[:, c, PAD - back:PAD - back + S],
                                                           weights_of(i, c, 2 - back), mix[:, c, :],
                                                           ALU.mult, ALU.add)
                            if back == 1:
                                ins.then_inc(mid, 1)
                                dve.wait_ge(mid, 4 * i + n + 1)
                        ins.then_inc(acted, 1)
                    dve.wait_ge(acted, 4 * i + 4)
                    dve.wait_ge(sig, 2 * i + 2)
                else:
                    dve.wait_ge(ev_a, 4 * i + 4)
                    dve.wait_ge(ev_d, 4 * i + 4)
                for q_ in range(4):
                    h, j = q_ // 2, q_ % 2
                    tok = slice(h * HALF, (h + 1) * HALF)
                    pad = slice(PAD + h * HALF, PAD + (h + 1) * HALF)
                    g_, u_ = (mix[:, j, tok], mix[:, 2 + j, tok]) if conv else (raw[:, j, pad], raw[:, 2 + j, pad])
                    dve.tensor_tensor(mix[:, j, tok], g_, u_, ALU.mult).then_inc(hid_a, 1)
                for q_ in range(4):
                    h, j = q_ // 2, q_ % 2
                    tok = slice(h * HALF, (h + 1) * HALF)
                    dve.wait_ge(sig2, 4 * i + q_ + 1)
                    dve.tensor_tensor(hid_lo[:, j, tok], mix[:, j, tok], hid_hi[:, j, tok].bitcast(F32),
                                      ALU.subtract).then_inc(hid, 1)

            def read_down(first, i):
                for nh in range(2):
                    for t in range(NT):
                        if t == NT - 1:
                            dve.wait_ge(m.used, first + 2 * nh + 2)
                        else:
                            dve.wait_ge(dn_done, 14 * i + 7 * nh + t + 1)
                        xs = x_sb[:, t, nh * HALF:(nh + 1) * HALF]
                        dve.tensor_tensor(xs, m.psum[t][:, :], xs, ALU.add).then_inc(dn_ev, 1)

            mid = m.sem("tap_mid" + tag)
            read_up(base, 0)
            finish(0)
            with dve.Fori(0, FI - 1) as i:
                read_up(base + GU + 12 * i, i + 1)
                read_down(base + 2 * GU + 12 * i, i)
                finish(i + 1)
            read_down(base + GU + 12 * (FI - 1), FI - 1)
    m.slices += 12 * FI
    m.chunks += FI


HG = 4


def proj2_stage(m, sc, qkv, gz, sqk, sv, ab):
    nc, a = m.nc, m.a
    base, c0 = m.slices, m.chunks
    w = a["w_mix_in_2"][0]
    wf = m.at("w_ab", [P, KD, 8], 196)
    wf_hi, wf_lo = m.at("w_ab_hi", [P, KD, 8], 196.25, F32R), m.at("w_ab_lo", [P, KD, 8], 196.5, F32R)
    conv = m.at("conv", [P, 2, S], 184)
    in_small, evac, f_split, f_done, f_evac = (m.sem(n) for n in ("in_ab", "p2_evac", "ab_split", "ab_done", "ab_evac"))
    prod, last_tap, older, acted, sdone = (m.sem(n) for n in ("sc_prod", "last_tap", "older_taps", "conv_act", "sc_done"))
    two = [m.sem(f"piece_loaded{u}") for u in range(RING)]
    pieces = [[(0, 512)], [(512, 512)], [(1024, 512)], [(1536, 512)], [(2048, 256), (3336, 256)],
              [(2304, 512)], [(2824, 512)]]
    NC = len(pieces)
    jobs = {1: [("s", 0), ("s", 1), ("g", 0), ("g", 1)], 2: [("g", i) for i in range(2, 6)],
            3: [("g", i) for i in range(6, 10)], 4: [("g", 10), ("g", 11)]}
    order = [job for c in range(NC) for job in jobs.get(c, [])]

    def place(c, n):
        i = 4 * c + n
        if i < 6:
            return sc[:, i, :]
        if c < 5 and i < 18:
            return qkv[:, i - 6, :]
        return sv[:, n - 2, :] if c == 4 else sqk[:, n, :]

    with nc.Block() as block:
        @block.sync
        def _(sp):
            sp.dma_start(wf[:, :, :], w[:, 2816:2824].rearrange("(k p) n -> p k n", p=P)).then_inc(in_small, 16)
            for c in range(NC):
                if len(pieces[c]) == 1:
                    col = pieces[c][0][0]
                    load_slices(m, sp, base, 8 * c, 8, lambda j, u: (
                        m.w_raw[:, u, :], w[bass.ds((j * RING + u) * P, P), col:col + HALF]))
                else:
                    for k in range(KD):
                        u = k % RING
                        sp.wait_ge(m.split, base + 8 * c + k + 1 - RING)
                        (c1, n1), (c2, n2) = pieces[c]
                        sp.dma_start(m.w_raw[:, u, 0:n1], w[k * P:(k + 1) * P, c1:c1 + n1]).then_inc(two[u], 16)
                        sp.dma_start(m.w_raw[:, u, n1:HALF], w[k * P:(k + 1) * P, c2:c2 + n2]).then_inc(m.loaded[u], 16)
            sp.wait_ge(in_small, 16)

        @block.gpsimd
        def _(pool):
            pool.wait_ge(in_small, 16)
            pool.tensor_tensor(wf_hi[:, :, :], wf[:, :, :], m.zero[:, 0:1].unsqueeze(2).to_broadcast([P, KD, 8]),
                               ALU.add).then_inc(f_split, 1)
            pool.wait_ge(f_split, 1)
            pool.tensor_tensor(wf_lo[:, :, :], wf[:, :, :], wf_hi[:, :, :].bitcast(F32), ALU.subtract).then_inc(f_split, 1)
            split_slices(m, pool, base, 32, RING)
            for k in range(KD):
                pool.wait_ge(two[k % RING], 16 * (k // RING + 1))
                if k % RING == RING - 1:
                    split_slices(m, pool, base + 32 + k - RING + 1, RING)
            split_slices(m, pool, base + 40, 16)

        @block.tensor
        def _(pe):
            pe.wait_ge(f_split, 2)
            for h in range(2):
                tok = slice(h * HALF, (h + 1) * HALF)
                for k in range(KD):
                    pe.matmul(m.psum[h][0:8, :], wf_hi[:, k, :], m.xt_hi[:, k, tok], start=k == 0, stop=False)
                    pe.matmul(m.psum[h][0:8, :], wf_hi[:, k, :], m.xt_lo[:, k, tok], start=False, stop=False)
                    mm = pe.matmul(m.psum[h][0:8, :], wf_lo[:, k, :], m.xt_hi[:, k, tok], start=False, stop=k == KD - 1)
                mm.then_inc(f_done, 1)
            for c in range(NC):
                def wait_bank(b):
                    if c == 0 and b < 2:
                        pe.wait_ge(f_evac, b + 1)
                    if c >= 1:
                        pe.wait_ge(evac, 8 * (c - 1) + b + 1)
                chunk_products(m, pe, base + 8 * c, c0 + c, c == 5, wait_bank)

        def source(job):
            kind, i = job
            return sc[:, 2 + i, :] if kind == "s" else qkv[:, i, :]

        def tap(job, n):
            kind, i = job
            col = ROW["w_sconv_2"] + 2 * (2 - n) + i if kind == "s" else ROW["w_gdn_conv_2"] + 12 * (3 - n) + i
            return m.cols[:, col:col + 1]

        @block.scalar
        def _(act):
            for h in range(2):
                act.wait_ge(f_done, h + 1)
                act.activation(ab[:, h * HALF:(h + 1) * HALF], m.psum[h][0:8, :], ACT.Copy).then_inc(f_evac, 1)

            def finish(x):
                act.wait_ge(older, x + 1)
                if order[x][0] == "g":
                    act.activation(source(order[x]), conv[:, x % 2, :], ACT.Silu).then_inc(acted, 1)

            x = 0
            for c in range(NC):
                for b in range(NB):
                    wait_chunk_bank(m, act, base + 8 * c, c0 + c, b)
                    h, n = b // 4, b % 4
                    if c == 5:
                        dst = gz[:, b, :]
                    else:
                        dst = place(c, n)[:, h * HALF:(h + 1) * HALF]
                    if c == 6 and b == 0:
                        act.wait_ge(sdone, 2)
                    act.activation(dst, m.psum[b][:, :], ACT.Copy,
                                   scale=SBD ** -0.5 if c == 6 and n < 2 else 1.0).then_inc(evac, 1)
                for job in jobs.get(c, []):
                    act.wait_ge(evac, 8 * (c + 1))
                    if job[0] == "s":
                        act.wait_ge(prod, job[1] + 1)
                    if x >= 2:
                        if order[x - 2][0] == "g":
                            act.wait_ge(acted, sum(o[0] == "g" for o in order[:x - 1]))
                        else:
                            act.wait_ge(sdone, order[x - 2][1] + 1)
                    n = 0
                    act.activation(conv[:, x % 2, :], source(job), ACT.Identity, scale=tap(job, 0)).then_inc(last_tap, 1)
                    if x:
                        finish(x - 1)
                    x += 1
                if c == 4:
                    finish(x - 1)

        @block.vector
        def _(dve):
            step = in_turn(m, dve, "dve")
            for i in range(2):
                dve.wait_ge(evac, 16)
                dve.tensor_tensor(sc[:, 2 + i, :], sc[:, 2 + i, :], sc[:, 4 + i, :], ALU.mult).then_inc(prod, 1)
            dve.wait_ge(prod, 2)
            for x, job in enumerate(order):
                dve.wait_ge(last_tap, x + 1)
                taps = 2 if job[0] == "s" else 3
                for n in range(1, taps + 1):
                    y = conv[:, x % 2, n:S]
                    ins = dve.scalar_tensor_tensor(y, source(job)[:, 0:S - n], tap(job, n), y, ALU.mult, ALU.add)
                    if n < taps:
                        step(ins)
                ins.then_inc(older, 1)
                if job[0] == "s":
                    dve.wait_ge(older, x + 1)
                    y = sc[:, job[1], :]
                    dve.tensor_tensor(y, y, conv[:, x % 2, :], ALU.mult).then_inc(sdone, 1)
    m.slices += 8 * NC
    m.chunks += NC


SBD = 64


def program_order(first, slots, level, ends):
    events = [(0, n) for key in SLOT_KEYS for n, ahead in slots.get(key, ()) if ahead]
    events += [(0, n) for n in first]
    for h in range(HG):
        for key in SLOT_KEYS:
            events += level(h, *key)
            events += [(h + ahead, n) for n, ahead in slots.get(key, ()) if h + ahead < HG]
        events += [(h + ahead, n) for n, ahead in ends if h + ahead < HG]
    return events


LEVELS = range(1, 7)
SLOT_KEYS = [(j, g) for j in LEVELS for g in (0, 1)]


def delta_stage(m, q_, k_, v_, ab, t_at):
    nc, a = m.nc, m.a
    at = m.at
    a_t, kd, elast = t_at["a_t"], t_at["kd"], t_at["elast"]
    X, XT, LT, T1, ke = (at(n, [P, NT, P], 64 + 4 * i) for i, n in enumerate(("X", "XT", "LT", "T1", "ke")))
    q_sq, k_sq = at("q_sq", [P, S], 184), at("k_sq", [P, S], 188)
    LM = [at("LM0", [P, NT, P], 88), at("LM1", [P, NT, P], 92)]
    Gb, GBb, Qb, Kb = (at(n, [P, NT, P], 96 + 4 * i) for i, n in enumerate(("Gb", "GBb", "Qb", "Kb")))
    masks = at("masks", [P, 3, P], 112)
    lev = at("levels", [P, 7, P], 113.5)
    ones = at("ones", [P, P], 117)
    small = at("small", [P, 12, NT], 117.5)
    eps128 = at("eps128", [P, 1], 118)
    col8 = at("col8", [8, 4], 118.0625)
    beta = at("beta", [P, NT, 4], 84)
    gct, gbt = at("gct", [P, NT, 8], 118.125), at("gbt", [P, NT, 8], 118.375)
    gc, gcb = at("gc", [8, S], 196), ab
    r1, r2, r3 = (at(n, [8, S], 64 + 4 * i) for i, n in enumerate(("r1", "r2", "r3")))
    made, rows_in, rows, turned = m.sem("delta_masks"), m.sem("delta_in"), m.sem("delta_rows"), m.sem("delta_cols")
    pe_s, dve_s, act_s, pool_s = m.sem("delta_pe"), m.sem("delta_dve"), m.sem("delta_act"), m.sem("delta_pool")
    LEV = LEVELS
    MADE = 30
    PE_SLOTS = {(2, 0): [("ssc", 1)], (2, 1): [("g", 1)], (3, 0): [("gb", 1)], (3, 1): [("ssq", 1)],
                (4, 0): [("ssk", 1)], (4, 1): [("kt", 1)], (5, 0): [("vt", 1)]}
    ACT_SLOTS = {(1, 0): [("sqk", 1)], (1, 1): [("sqq", 1)], (2, 0): [("lns", 1)], (2, 1): [("gcopy", 1)],
                 (3, 0): [("gbcopy", 1)], (3, 1): [("lnq", 1)], (4, 0): [("lnk", 1)], (4, 1): [("ktcopy", 1)],
                 (5, 0): [("er1", 1), ("ex", 1)], (5, 1): [("elt", 1)], (6, 0): [("el", 1)], (6, 1): [("ea", 1)]}
    DVE_SLOTS = {(1, 0): [("a_t", 0)], (1, 1): [("qe", 0)], (3, 1): [("gsum", 1)], (4, 0): [("rq", 1)],
                 (4, 1): [("b", 1), ("rk", 1)], (5, 0): [("vb", 1), ("elt", 1)], (5, 1): [("el", 1)], (6, 0): [("ea", 1)]}
    PE_END = [("w0", 0), ("kk", 1), ("w1", 0), ("u0", 0), ("u1", 0), ("kq", 1)]
    ACT_END = [("w0", 0), ("w1", 0), ("u0", 0), ("u1", 0)]
    DVE_END = [("LT", 1), ("X", 1), ("XT", 1)]

    def pe_order():
        events = [(0, n) for key in SLOT_KEYS for n, ahead in PE_SLOTS.get(key, ()) if ahead] + [(0, "kk"), (0, "kq")]
        for h in range(HG):
            for j in LEV:
                kinds = ("x", "xt") if j < 6 else ("xt",)
                events += [(h, f"t{j}0"), (h, f"t{j}1")]
                events += [(h + 1, n) for n, _ in PE_SLOTS.get((j, 0), ()) if h + 1 < HG]
                events += [(h, f"{n}{j}0") for n in kinds]
                events += [(h + 1, n) for n, _ in PE_SLOTS.get((j, 1), ()) if h + 1 < HG]
                events += [(h, f"{n}{j}1") for n in kinds]
            events += [(h + ahead, n) for n, ahead in PE_END if h + ahead < HG]
        return events

    PE_EV = pe_order()
    ACT_EV = program_order([], ACT_SLOTS, lambda h, j, g: [(h, f"t{j}0"), (h, f"t{j}1")] if g == 0 else [], ACT_END)
    DVE_EV = program_order(["LT", "X", "XT"], DVE_SLOTS,
                           lambda h, j, g: [(h, f"{n}{j}{g}") for n in (("x", "xt") if j < 6 else ("xt",))], DVE_END)
    POOL_EV = [(h, n) for h in range(HG) for n in ("m1", "m2", "ke", "m3", "kd", "m4", "m5", "m6")]

    def pe_at(e, h, n):
        e.wait_ge(pe_s, PE_EV.index((h, n)) + 1)

    def dve_at(e, h, n):
        e.wait_ge(dve_s, DVE_EV.index((h, n)) + 1)

    def act_at(e, h, n):
        e.wait_ge(act_s, ACT_EV.index((h, n)) + 1)

    def pool_at(e, h, n):
        e.wait_ge(pool_s, POOL_EV.index((h, n)) + 1)

    def tiles(bank):
        return bank[:, :].rearrange("p (c n) -> p c n", n=P)

    def half(t, g):
        return t[:, 4 * g:4 * g + 4, :]

    def flat(t, c):
        return t[:, :, :].rearrange("p c n -> p (c n)")[:, c * HALF:(c + 1) * HALF]

    with nc.Block() as block:
        @block.sync
        def _(sp):
            sp.wait_ge(made, 1)
            sp.dma_start(col8[0:4, 0:1], a["gdn_dt_bias_2"].rearrange("a h -> h a")).then_inc(rows_in, 16)
            sp.dma_start(col8[0:4, 1:2], a["gdn_a_log_2"].rearrange("a h -> h a")).then_inc(rows_in, 16)
            sp.wait_ge(rows_in, 32)

        @block.gpsimd
        def _(pool):
            pool.memset(col8[:, :], 0.0).then_inc(made, 1)
            pool.memset(masks[:, :, :], 0.0).then_inc(made, 1)
            pool.memset(lev[:, :, :], 0.0).then_inc(made, 1)
            pool.memset(ones[:, :], 1.0).then_inc(made, 1)
            pool.memset(eps128[:, :], EPS * P).then_inc(made, 1)
            pool.wait_ge(made, 5)
            n = 5
            for i, b in ((0, 0), (1, -1)):
                pool.affine_select(out=masks[:, i, :], in_=masks[:, i, :], compare_op=ALU.is_ge, fill=NEG,
                                   base=b, pattern=[[1, P]], channel_multiplier=-1).then_inc(made, 1)
                n += 1
            pool.memset(masks[:, 2, :], NEG).then_inc(made, 1)
            n += 1
            pool.wait_ge(made, n)
            v = masks[:, 2, :].rearrange("p (b e) -> p b e", e=2)
            pool.affine_select(out=v[:, :, 0], in_=v[:, :, 0], compare_op=ALU.not_equal, fill=0.0,
                               base=-1, pattern=[[-2, 64]], channel_multiplier=1).then_inc(made, 1)
            n += 1
            for j in range(7):
                b = 1 << j
                v = lev[:, j, :].rearrange("p (k e r) -> p k e r", e=2, r=b)[:, :, 1, :]
                pool.memset(v, 1.0).then_inc(made, 1)
                n += 1
                pool.wait_ge(made, n)
                pool.affine_select(out=v, in_=v, compare_op=ALU.is_ge, fill=0.0, base=0,
                                   pattern=[[-2 * b, 64 // b], [0, b]], channel_multiplier=1).then_inc(made, 1)
                n += 1
                pool.wait_ge(made, n)
                pool.affine_select(out=v, in_=v, compare_op=ALU.is_ge, fill=0.0, base=b - 1,
                                   pattern=[[2 * b, 64 // b], [0, b]], channel_multiplier=-1).then_inc(made, 1)
                n += 1
            pool.wait_ge(made, n)
            assert n == MADE
            for h in range(HG):
                dve_at(pool, h, "LT")
                for j in LEV:
                    if j > 2:
                        pe_at(pool, h, f"t{j - 2}1")
                    elif h:
                        pe_at(pool, h - 1, f"t{j + 4}1")
                    pool.tensor_tensor(LM[j % 2][:, :, :], LT[:, :, :],
                                       lev[:, j, :].unsqueeze(1).to_broadcast([P, NT, P]), ALU.mult).then_inc(pool_s, 1)
                    if j == 2:
                        act_at(pool, h, "ktcopy")
                        act_at(pool, h, "ex")
                        if h:
                            pe_at(pool, h - 1, "w1")
                        pool.tensor_tensor(ke[:, :, :], kd[:, h, :, :],
                                           small[:, 8, :].unsqueeze(2).to_broadcast([P, NT, P]), ALU.mult).then_inc(pool_s, 1)
                    elif j == 3:
                        pool_at(pool, h, "ke")
                        pool.tensor_tensor(kd[:, h, :, :], kd[:, h, :, :],
                                           small[:, 9, :].unsqueeze(2).to_broadcast([P, NT, P]), ALU.mult).then_inc(pool_s, 1)

        @block.scalar
        def _(act):
            step = in_turn(m, act, "act")
            act.wait_ge(rows_in, 32)
            act.wait_ge(made, MADE)
            step(act.activation(r1[:, :], ab[:, :], ACT.Identity, bias=col8[:, 0:1]))
            step(act.activation(r2[:, :], r1[:, :], ACT.Abs))
            step(act.activation(r2[:, :], r2[:, :], ACT.Exp, scale=-1.0))
            act.activation(r2[:, :], r2[:, :], ACT.Ln, bias=1.0).then_inc(rows, 1)
            act.activation(col8[:, 2:3], col8[:, 1:2], ACT.Exp).then_inc(rows, 1)
            def pair(dst, ev, h, func, **kw):
                pe_at(act, h, ev)
                for c in range(2):
                    ins = act.activation(dst(c), m.psum[6 + c][:, :], func, **kw)
                ins.then_inc(act_s, 1)

            def prepare(h, n):
                if n == "sqk":
                    act.activation(k_sq[:, :], k_[:, h, :], ACT.Square).then_inc(act_s, 1)
                elif n == "sqq":
                    act.activation(q_sq[:, :], q_[:, h, :], ACT.Square).then_inc(act_s, 1)
                elif n == "lns":
                    pe_at(act, h, "ssc")
                    act.activation(small[:, 1, :], m.psum[6][:, 0:NT], ACT.Ln, bias=m.eps[:, 0:1]).then_inc(act_s, 1)
                elif n == "gcopy":
                    if h:
                        dve_at(act, h - 1, "qe")
                    pair(lambda c: flat(Gb, c), "g", h, ACT.Copy)
                elif n == "gbcopy":
                    pair(lambda c: flat(GBb, c), "gb", h, ACT.Copy)
                elif n == "lnq":
                    pair(lambda c: flat(Qb, c), "ssq", h, ACT.Ln, scale=float(P), bias=eps128[:, 0:1])
                elif n == "lnk":
                    pair(lambda c: flat(Kb, c), "ssk", h, ACT.Ln, bias=m.eps[:, 0:1])
                elif n == "ktcopy":
                    pair(lambda c: kd[:, h, 4 * c:4 * c + 4, :].rearrange("p c n -> p (c n)"), "kt", h, ACT.Copy)
                elif n == "er1":
                    dve_at(act, h, "rk")
                    act.activation(Gb[:, :, :], Qb[:, :, :], ACT.Exp).then_inc(act_s, 1)
                elif n == "ex":
                    dve_at(act, h, "b")
                    if h:
                        pool_at(act, h - 1, "kd")
                    act.activation(small[:, 8:12, :], small[:, 4:8, :], ACT.Exp).then_inc(act_s, 1)
                else:
                    t = {"ea": Qb, "elt": GBb, "el": Kb}[n]
                    dve_at(act, h, n)
                    act.activation(t[:, :, :], t[:, :, :], ACT.Exp).then_inc(act_s, 1)

            act.wait_ge(turned, 2)
            act.activation(beta[:, :, :], gbt[:, :, 4:8], ACT.Exp).then_inc(turned, 1)
            for key in SLOT_KEYS:
                for n, _ in ACT_SLOTS.get(key, ()):
                    prepare(0, n)
            for h in range(HG):
                for j, g in SLOT_KEYS:
                    if g == 0:
                        for half_ in (0, 1):
                            pe_at(act, h, f"t{j}{half_}")
                            act.activation(half(T1, half_), tiles(m.psum[half_]), ACT.Copy).then_inc(act_s, 1)
                    for n, _ in ACT_SLOTS.get((j, g), ()):
                        if h + 1 < HG:
                            prepare(h + 1, n)
                for i, (dst, w) in enumerate(((k_, "w"), (v_, "u"))):
                    for g in (0, 1):
                        pe_at(act, h, f"{w}{g}")
                        act.activation(dst[:, h, g * HALF:(g + 1) * HALF], m.psum[2 * i + g][:, :],
                                       ACT.Copy).then_inc(act_s, 1)

        @block.vector
        def _(dve):
            step = in_turn(m, dve, "dve")
            dve.wait_ge(rows, 2)
            step(dve.tensor_scalar(r3[:, :], r1[:, :], 0.0, None, ALU.max))
            step(dve.tensor_tensor(r3[:, :], r3[:, :], r2[:, :], ALU.add))
            step(dve.tensor_scalar(r3[:, :], r3[:, :], col8[:, 2:3], -1.0, ALU.mult, ALU.mult))
            step(dve.tensor_scalar(r1[:, :], r1[:, :], -1.0, 0.0, ALU.mult, ALU.max))
            step(dve.tensor_tensor(r1[:, :], r1[:, :], r2[:, :], ALU.add))
            step(dve.tensor_scalar(gcb[:, :], r1[:, :], -1.0, None, ALU.mult))
            step(dve.memset(r2[:, :], 1.0))
            step(dve.memset(r2[:, :].rearrange("p (c n) -> p c n", n=P)[:, :, 0:1], 0.0))
            dve.tensor_tensor_scan(gc[:, :], r2[:, :], r3[:, :], 0.0, ALU.mult, ALU.add).then_inc(rows, 1)
            dve.wait_ge(turned, 1)
            step(dve.tensor_copy(gct[:, :, :], m.psum[0][:, 0:64].rearrange("p (c n) -> p c n", n=8)))
            step(dve.tensor_copy(gbt[:, :, 4:8], m.psum[0][:, 64:128].rearrange("p (c n) -> p c n", n=8)[:, :, 4:8]))
            m.dve_steps_cols = m.dve_steps
            dve.tensor_tensor(gbt[:, :, 0:4], gbt[:, :, 4:8], gct[:, :, 0:4], ALU.add).then_inc(turned, 1)
            dve.wait_ge(turned, 3)
            dve.wait_ge(made, MADE)
            eye = m.ident[:, :].unsqueeze(1).to_broadcast([P, NT, P])

            def masked(h, t, bias, i, ev):
                for c in range(NT):
                    ins = dve.scalar_tensor_tensor(t[:, c, :], t[:, c, :], small[:, bias, c:c + 1], masks[:, i, :],
                                                   ALU.add, ALU.add)
                ins.then_inc(dve_s, 1)

            def prepare(h, n):
                if n == "gsum":
                    act_at(dve, h, "gbcopy")
                    step(dve.tensor_copy(small[:, 7, :], Gb[:, :, P - 1]))
                    dve.tensor_tensor(GBb[:, :, :], GBb[:, :, :], Gb[:, :, :], ALU.add).then_inc(dve_s, 1)
                elif n == "rq":
                    act_at(dve, h, "lnq")
                    dve.scalar_tensor_tensor(Qb[:, :, :], Qb[:, :, :], -0.5, Gb[:, :, :], ALU.mult, ALU.add).then_inc(dve_s, 1)
                elif n == "b":
                    step(dve.scalar_tensor_tensor(small[:, 2, :], small[:, 1, :], -0.5, gct[:, :, h], ALU.mult, ALU.subtract))
                    step(dve.scalar_tensor_tensor(small[:, 4, :], small[:, 1, :], -0.5, gbt[:, :, h], ALU.mult, ALU.add))
                    step(dve.tensor_tensor(small[:, 5, :], small[:, 2, :], small[:, 7, :], ALU.add))
                    dve.tensor_copy(small[:, 6, :], gbt[:, :, 4 + h]).then_inc(dve_s, 1)
                elif n == "rk":
                    act_at(dve, h, "lnk")
                    dve_at(dve, h, "gsum")
                    step(dve.scalar_tensor_tensor(GBb[:, :, :], Kb[:, :, :], -0.5, GBb[:, :, :], ALU.mult, ALU.add))
                    dve.scalar_tensor_tensor(Kb[:, :, :], Kb[:, :, :], -0.5, Gb[:, :, :], ALU.mult, ALU.subtract).then_inc(dve_s, 1)
                elif n == "vb":
                    pe_at(dve, h, "vt")
                    for c in range(2):
                        ins = dve.tensor_tensor(v_[:, h, c * HALF:(c + 1) * HALF].rearrange("p (c n) -> p c n", n=P),
                                                tiles(m.psum[6 + c]),
                                                beta[:, 4 * c:4 * c + 4, h].unsqueeze(2).to_broadcast([P, 4, P]), ALU.mult)
                    ins.then_inc(dve_s, 1)
                elif n == "elt":
                    dve_at(dve, h, "rk")
                    masked(h, GBb, 2, 1, n)
                elif n == "el":
                    masked(h, Kb, 4, 2, n)
                elif n == "ea":
                    act_at(dve, h, "er1")
                    masked(h, Qb, 2, 0, n)
                elif n == "a_t":
                    pe_at(dve, h, "kq")
                    act_at(dve, h, "ea")
                    for c in range(2):
                        ins = dve.tensor_tensor(a_t[:, h, 4 * c:4 * c + 4, :], tiles(m.psum[6 + c]), half(Qb, c), ALU.mult)
                    ins.then_inc(dve_s, 1)
                else:
                    step(dve.tensor_copy(elast[:, h, :], small[:, 11, :]))
                    dve.tensor_tensor(q_[:, h, :], q_[:, h, :], Gb[:, :, :].rearrange("p c n -> p (c n)"),
                                      ALU.mult).then_inc(dve_s, 1)

            def start(h):
                pe_at(dve, h, "kk")
                act_at(dve, h, "elt")
                if h:
                    pool_at(dve, h - 1, "m6")
                for c in range(2):
                    ins = dve.tensor_tensor(half(LT, c), tiles(m.psum[4 + c]), half(GBb, c), ALU.mult)
                ins.then_inc(dve_s, 1)
                act_at(dve, h, "el")
                for c in range(2):
                    step(dve.tensor_tensor(half(X, c), tiles(m.psum[4 + c]), half(Kb, c), ALU.mult))
                dve.tensor_tensor(X[:, :, :], eye, X[:, :, :], ALU.subtract).then_inc(dve_s, 1)
                if h:
                    pe_at(dve, h - 1, "u1")
                dve_at(dve, h, "LT")
                step(dve.tensor_tensor(XT[:, :, :], LT[:, :, :], lev[:, 0, :].unsqueeze(1).to_broadcast([P, NT, P]), ALU.mult))
                dve.tensor_tensor(XT[:, :, :], eye, XT[:, :, :], ALU.subtract).then_inc(dve_s, 1)

            for key in SLOT_KEYS:
                for n, ahead in DVE_SLOTS.get(key, ()):
                    if ahead:
                        prepare(0, n)
            start(0)
            for h in range(HG):
                dve_at(dve, h, "XT")
                for j, g in SLOT_KEYS:
                    if j < 6:
                        pe_at(dve, h, f"x{j}{g}")
                        dve.tensor_tensor(half(X, g), half(X, g), tiles(m.psum[2 + g]), ALU.subtract).then_inc(dve_s, 1)
                    pe_at(dve, h, f"xt{j}{g}")
                    dve.tensor_tensor(half(XT, g), half(XT, g), tiles(m.psum[4 + g]), ALU.subtract).then_inc(dve_s, 1)
                    for n, ahead in DVE_SLOTS.get((j, g), ()):
                        if h + ahead < HG:
                            prepare(h + ahead, n)
                if h + 1 < HG:
                    start(h + 1)

        @block.tensor
        def _(pe):
            pe.wait_ge(made, MADE)
            pe.wait_ge(rows, 3)
            for c in range(NT):
                pe.transpose(m.psum[0][:, 8 * c:8 * c + 8], gc[:, c * P:(c + 1) * P], m.ident[0:8, 0:8])
            for c in range(NT):
                mm = pe.transpose(m.psum[0][:, 64 + 8 * c:72 + 8 * c], gcb[:, c * P:(c + 1) * P], m.ident[0:8, 0:8])
            mm.then_inc(turned, 1)
            pe.wait_ge(m.dve_step, m.dve_steps_cols)
            def broadcast(lhs, row, ev):
                for c in range(2):
                    mm = pe.matmul(m.psum[6 + c][:, :], lhs, row(c), start=True, stop=True)
                mm.then_inc(pe_s, 1)

            def by_chunk(bank, product):
                for c in range(NT):
                    mm = product(m.psum[bank + c // 4][:, (c % 4) * P:(c % 4 + 1) * P], slice(c * P, (c + 1) * P))
                mm.then_inc(pe_s, 1)

            def products(bank, g, lhs, rhs):
                for c in range(4 * g, 4 * g + 4):
                    mm = pe.matmul(m.psum[bank][:, (c % 4) * P:(c % 4 + 1) * P], lhs(c), rhs(c), start=True, stop=True)
                mm.then_inc(pe_s, 1)

            def prepare(h, n):
                if n == "ssc":
                    act_at(pe, h, "sqk")
                    if h:
                        dve_at(pe, h - 1, "a_t")
                    for c in range(NT):
                        mm = pe.matmul(m.psum[6][:, c:c + 1], k_sq[:, c * P:(c + 1) * P], ones[:, 0:1], start=True, stop=True)
                    mm.then_inc(pe_s, 1)
                elif n == "g":
                    act_at(pe, h, "lns")
                    broadcast(m.sel[0:8, h, :], lambda c: gc[:, c * HALF:(c + 1) * HALF], n)
                elif n == "gb":
                    act_at(pe, h, "gcopy")
                    broadcast(m.sel[0:8, 4 + h, :], lambda c: gcb[:, c * HALF:(c + 1) * HALF], n)
                elif n == "ssq":
                    act_at(pe, h, "gbcopy")
                    broadcast(ones[:, :], lambda c: q_sq[:, c * HALF:(c + 1) * HALF], n)
                elif n == "ssk":
                    act_at(pe, h, "lnq")
                    broadcast(ones[:, :], lambda c: k_sq[:, c * HALF:(c + 1) * HALF], n)
                elif n == "kt":
                    act_at(pe, h, "lnk")
                    by_chunk(6, lambda out, tok: pe.transpose(out, k_[:, h, tok], m.ident[:, :]))
                elif n == "vt":
                    act_at(pe, h, "ktcopy")
                    by_chunk(6, lambda out, tok: pe.transpose(out, v_[:, h, tok], m.ident[:, :]))
                elif n == "kk":
                    if h:
                        dve_at(pe, h - 1, "xt61")
                    by_chunk(4, lambda out, tok: pe.matmul(out, k_[:, h, tok], k_[:, h, tok], start=True, stop=True))
                else:
                    dve_at(pe, h, "vb")
                    by_chunk(6, lambda out, tok: pe.matmul(out, k_[:, h, tok], q_[:, h, tok], start=True, stop=True))

            for key in SLOT_KEYS:
                for n, _ in PE_SLOTS.get(key, ()):
                    prepare(0, n)
            prepare(0, "kk")
            prepare(0, "kq")
            for h in range(HG):
                dve_at(pe, h, "X")
                for j in LEV:
                    pool_at(pe, h, f"m{j}")
                    for g in (0, 1):
                        if j > 1:
                            dve_at(pe, h, f"xt{j - 1}{g}")
                        elif h:
                            act_at(pe, h - 1, f"w{g}")
                        products(g, g, lambda c: LM[j % 2][:, c, :], lambda c: X[:, c, :])
                    for g in (0, 1):
                        for n, _ in PE_SLOTS.get((j, g), ()):
                            if h + 1 < HG:
                                prepare(h + 1, n)
                        if j == 1:
                            dve_at(pe, h, "XT")
                            if h:
                                act_at(pe, h - 1, f"u{g}")
                        act_at(pe, h, f"t{j}{g}")
                        if j < 6:
                            products(2 + g, g, lambda c: XT[:, c, :], lambda c: T1[:, c, :])
                        products(4 + g, g, lambda c: T1[:, c, :], lambda c: XT[:, c, :])

                def decayed(g):
                    dve_at(pe, h, f"xt6{g}")
                    products(g, g, lambda c: ke[:, c, :], lambda c: XT[:, c, :])

                pool_at(pe, h, "ke")
                decayed(0)
                if h + 1 < HG:
                    prepare(h + 1, "kk")
                decayed(1)
                for g in (0, 1):
                    products(2 + g, g, lambda c: XT[:, c, :], lambda c: v_[:, h, c * P:(c + 1) * P])
                if h + 1 < HG:
                    prepare(h + 1, "kq")


def scan_stage(m, q_, k_, v_, t_at, gz):
    nc = m.nc
    a_t, kd, elast = t_at["a_t"], t_at["kd"], t_at["elast"]
    state, vn = m.at("state", [P, HG, P], 64), m.at("v_new", [P, HG, P], 66)
    o = m.at("delta_out", [P, NT, HG, P], 68)
    sq = m.at("delta_sq", [P, NT, HG, P], 84)
    ss, rs = m.at("delta_ss", [P, NT * HG], 100), m.at("delta_rs", [P, NT * HG], 100.25)
    pe_s, dve_s, act_s = m.sem("scan_pe"), m.sem("scan_dve"), m.sem("scan_out")
    gate = m.sem("scan_gate")
    with nc.Block() as block:
        @block.tensor
        def _(pe):
            for c in range(NT):
                tok = slice(c * P, (c + 1) * P)
                for h in range(HG):
                    if c:
                        pe.wait_ge(dve_s, 8 * c - 4 + h + 1)
                    else:
                        pe.wait_ge(gate, 1)
                    pe.matmul(m.psum[h][:, 0:P], k_[:, h, tok], state[:, h, :], start=True, stop=True).then_inc(pe_s, 1)
                for h in range(HG):
                    if c:
                        pe.wait_ge(act_s, 4 * (c - 1) + h + 1)
                    pe.matmul(m.psum[4 + h][:, 0:P], q_[:, h, tok], state[:, h, :], start=True, stop=False)
                    pe.wait_ge(dve_s, 8 * c + h + 1)
                    pe.matmul(m.psum[4 + h][:, 0:P], a_t[:, h, c, :], vn[:, h, :], start=False, stop=True).then_inc(pe_s, 1)
                for h in range(HG):
                    pe.matmul(m.psum[h][:, 0:P], kd[:, h, c, :], vn[:, h, :], start=True, stop=True).then_inc(pe_s, 1)

        @block.vector
        def _(dve):
            step = in_turn(m, dve, "dve")
            dve.memset(state[:, :, :], 0.0).then_inc(gate, 1)
            dve.wait_ge(gate, 1)
            for c in range(NT):
                for h in range(HG):
                    dve.wait_ge(pe_s, 12 * c + h + 1)
                    dve.tensor_tensor(vn[:, h, :], v_[:, h, c * P:(c + 1) * P], m.psum[h][:, 0:P],
                                      ALU.subtract).then_inc(dve_s, 1)
                for h in range(HG):
                    dve.wait_ge(pe_s, 12 * c + 8 + h + 1)
                    if c:
                        dve.wait_ge(dve_s, 8 * c - 4 + h + 1)
                    dve.scalar_tensor_tensor(state[:, h, :], state[:, h, :], elast[:, h, c:c + 1], m.psum[h][:, 0:P],
                                             ALU.mult, ALU.add).then_inc(dve_s, 1)
            dve.wait_ge(gate, 2)
            dve.tensor_reduce(ss[:, :], sq[:, :, :, :].rearrange("p c h n -> p (c h) n"), AX, ALU.add).then_inc(gate, 1)
            dve.wait_ge(gate, 5)
            of = o[:, :, :, :].rearrange("p c h n -> p (c h) n")
            step(dve.tensor_tensor(of, of, rs[:, :].unsqueeze(2).to_broadcast([P, NT * HG, P]), ALU.mult))
            step(dve.tensor_tensor(gz[:, :, :], gz[:, :, :], o[:, :, :, :].rearrange("p c h n -> p c (h n)"), ALU.mult))

        @block.scalar
        def _(act):
            for c in range(NT):
                for h in range(HG):
                    act.wait_ge(pe_s, 12 * c + 4 + h + 1)
                    act.activation(o[:, c, h, :], m.psum[4 + h][:, 0:P], ACT.Copy).then_inc(act_s, 1)
            act.wait_ge(act_s, 32)
            act.wait_ge(gate, 1)
            act.activation(sq[:, :, :, :], o[:, :, :, :], ACT.Square).then_inc(gate, 1)
            act.wait_ge(gate, 3)
            act.activation(rs[:, :], ss[:, :], ACT.Ln, scale=1.0 / P, bias=m.eps[:, 0:1]).then_inc(gate, 1)
            act.wait_ge(gate, 4)
            act.activation(gz[:, :, :], gz[:, :, :], ACT.Silu).then_inc(m.act_step, 1)
            m.act_steps += 1
            act.wait_ge(m.act_step, m.act_steps)
            act.activation(rs[:, :], rs[:, :], ACT.Exp, scale=-0.5).then_inc(gate, 1)


def stick_stage(m, sqk, sv, y):
    nc = m.nc
    svt = m.at("sv_t", [P, NT, 4, SBD], 64)
    tri, allm, keep, mneg = (m.at(n, [P, P], 72 + i / 2) for i, n in enumerate(("tri", "minus_ones", "keep", "not_before")))
    zc, sp, acc, A = (m.at(n, [P, 4, HALF], 76 + 8 * i) for i, n in enumerate(("z_capped", "softplus", "later", "weights")))
    made, turned, values_in = m.sem("sb_made"), m.sem("sb_t"), m.sem("sb_values")
    z_made, summed, added = m.sem("sb_z"), m.sem("sb_summed"), m.sem("sb_added")
    capped, raw, soft, later, extra, evo = (m.sem(f"sb_{n}") for n in ("capped", "raw", "soft", "later", "extra", "out"))
    exped, logged, weighed = m.sem("sb_exp"), m.sem("sb_ln"), m.sem("sb_weights")
    steps = [(g, b, q) for g in range(2) for b in range(4 * g + 3, -1, -1) for q in range(2)]
    LAG = 4

    def units(p):
        g, b, q = steps[p]
        return [(2 * p + i, 2 * q + i, 2 * (p % 3) + i, g, b) for i in range(2)]

    def cols(g, b):
        return max(0, b - 4 * g) * P

    with nc.Block() as block:
        @block.gpsimd
        def _(pool):
            pool.memset(tri[:, :], -1.0).then_inc(made, 1)
            pool.memset(allm[:, :], -1.0).then_inc(made, 1)
            pool.memset(keep[:, :], 1.0).then_inc(made, 1)
            pool.memset(mneg[:, :], 0.0).then_inc(made, 1)
            pool.wait_ge(made, 4)
            pool.affine_select(out=tri[:, :], in_=tri[:, :], compare_op=ALU.is_ge, fill=0.0, base=0,
                               pattern=[[-1, P]], channel_multiplier=1).then_inc(made, 1)
            pool.affine_select(out=keep[:, :], in_=keep[:, :], compare_op=ALU.is_gt, fill=0.0, base=0,
                               pattern=[[1, P]], channel_multiplier=-1).then_inc(made, 1)
            pool.affine_select(out=mneg[:, :], in_=mneg[:, :], compare_op=ALU.is_gt, fill=NEG, base=0,
                               pattern=[[1, P]], channel_multiplier=-1).then_inc(made, 1)
            pool.wait_ge(made, 7)

        @block.tensor
        def _(pe):
            for n in range(2):
                for t in range(NT):
                    mm = pe.transpose(m.psum[2 * n + t // 4][:, (t % 4) * P:(t % 4 + 1) * P],
                                      sv[:, n, t * P:(t + 1) * P], m.ident[:, :])
                mm.then_inc(turned, 1)
            pe.wait_ge(made, 7)
            pe.wait_ge(values_in, 2)

            def scores(p):
                for u, h, bank, g, b in units(p):
                    p0, c0 = 64 * (h % 2), cols(g, b)
                    if p > 2:
                        pe.wait_ge(weighed, u - 6 + 1)
                    pe.matmul(m.psum[bank][:, c0:HALF], sqk[p0:p0 + 64, 2 + h // 2, b * P:(b + 1) * P],
                              sqk[p0:p0 + 64, h // 2, g * HALF + c0:(g + 1) * HALF], start=True, stop=True).then_inc(z_made, 1)

            def sums(p):
                for u, h, bank, g, b in units(p):
                    c0 = cols(g, b)
                    pe.wait_ge(soft, u + 1)
                    mm = pe.matmul(m.psum[bank][:, c0:HALF], tri[:, :], sp[:, h, c0:HALF], start=False, stop=False,
                                   skip_group_check=True)
                    if b >= 4 * g:
                        mm = pe.matmul(m.psum[bank][:, c0:c0 + P], m.ident[:, :], mneg[:, :], start=False, stop=False,
                                       skip_group_check=True)
                    if b != 4 * g + 3:
                        c1 = c0 + P if b >= 4 * g else c0
                        pe.wait_ge(later, u - LAG + 1)
                        mm = pe.matmul(m.psum[bank][:, c1:HALF], allm[:, :], acc[:, h, c1:HALF], start=False, stop=True,
                                       skip_group_check=True)
                    mm.then_inc(summed, 1)

            def values(p):
                for u, h, bank, g, b in units(p):
                    p0, c0 = 64 * (h % 2), cols(g, b)
                    pe.wait_ge(weighed, u + 1)
                    if b == 4 * g + 3 and g:
                        pe.wait_ge(evo, 2 * (h // 2 + 1))
                    pe.matmul(m.psum[6 + h // 2][p0:p0 + 64, c0:HALF], svt[:, b, h, :], A[:, h, c0:HALF],
                              start=b == 4 * g + 3, stop=b == 0, skip_group_check=True).then_inc(added, 1)

            scores(0)
            scores(1)
            for p in range(len(steps)):
                sums(p)
                if p + 2 < len(steps):
                    scores(p + 2)
                if p:
                    values(p - 1)
            values(len(steps) - 1)

        @block.vector
        def _(dve):
            for n in range(2):
                dve.wait_ge(turned, n + 1)
                for c in range(2):
                    ins = dve.tensor_copy(svt[:, 4 * c:4 * c + 4, 2 * n:2 * n + 2, :],
                                          m.psum[2 * n + c][:, :].rearrange("p (t h d) -> p t h d", t=4, h=2))
                ins.then_inc(values_in, 1)
            dve.wait_ge(made, 7)
            diagonals = [0]

            def cap(p):
                for u, h, bank, g, b in units(p):
                    c0 = cols(g, b)
                    dve.wait_ge(z_made, u + 1)
                    if p > 1:
                        dve.wait_ge(logged, u - LAG + 1)
                    dve.tensor_scalar(zc[:, h, c0:HALF], m.psum[bank][:, c0:HALF], 40.0, None, ALU.min).then_inc(capped, 1)

            def softplus(p):
                for u, h, bank, g, b in units(p):
                    c0 = cols(g, b)
                    dve.wait_ge(logged, u + 1)
                    ins = dve.tensor_tensor(sp[:, h, c0:HALF], sp[:, h, c0:HALF], m.psum[bank][:, c0:HALF], ALU.max)
                    if b >= 4 * g:
                        ins.then_inc(raw, 1)
                        diagonals[0] += 1
                        dve.wait_ge(raw, diagonals[0])
                        dve.tensor_tensor(sp[:, h, c0:c0 + P], sp[:, h, c0:c0 + P], keep[:, :], ALU.mult).then_inc(soft, 1)
                    else:
                        ins.then_inc(soft, 1)

            def add_later(p):
                for u, h, bank, g, b in units(p):
                    c0 = cols(g, b)
                    dve.wait_ge(summed, u + 1)
                    dve.wait_ge(soft, u + 1)
                    if p > 1:
                        dve.wait_ge(later, u - LAG + 1)
                    if b == 4 * g + 3:
                        dve.tensor_copy(acc[:, h, c0:HALF], sp[:, h, c0:HALF]).then_inc(later, 1)
                    elif b >= 4 * g:
                        dve.tensor_tensor(acc[:, h, c0 + P:HALF], acc[:, h, c0 + P:HALF], sp[:, h, c0 + P:HALF], ALU.add)\
                           .then_inc(extra, 1)
                        dve.tensor_copy(acc[:, h, c0:c0 + P], sp[:, h, c0:c0 + P]).then_inc(later, 1)
                    else:
                        dve.tensor_tensor(acc[:, h, :], acc[:, h, :], sp[:, h, :], ALU.add).then_inc(later, 1)

            def outputs(p):
                for u, h, bank, g, b in units(p):
                    if b == 0:
                        p0 = 64 * (h % 2)
                        dve.wait_ge(added, 2 * p + 2)
                        dve.tensor_copy(y[p0:p0 + 64, h // 2, g * HALF:(g + 1) * HALF],
                                        m.psum[6 + h // 2][p0:p0 + 64, :]).then_inc(evo, 1)

            for p in (0, 1):
                cap(p)
                softplus(p)
            for p in range(len(steps)):
                add_later(p)
                if p + 2 < len(steps):
                    cap(p + 2)
                if p > 0:
                    outputs(p - 1)
                if p + 2 < len(steps):
                    softplus(p + 2)
            outputs(len(steps) - 1)

        @block.scalar
        def _(act):
            def logs(p):
                for u, h, bank, g, b in units(p):
                    c0 = cols(g, b)
                    act.wait_ge(capped, u + 1)
                    act.activation(zc[:, h, c0:HALF], zc[:, h, c0:HALF], ACT.Exp).then_inc(exped, 1)
                for u, h, bank, g, b in units(p):
                    c0 = cols(g, b)
                    act.wait_ge(exped, u + 1)
                    if p > 1:
                        act.wait_ge(later, u - LAG + 1)
                    act.activation(sp[:, h, c0:HALF], zc[:, h, c0:HALF], ACT.Ln, bias=1.0).then_inc(logged, 1)

            def weights(p):
                for u, h, bank, g, b in units(p):
                    c0 = cols(g, b)
                    act.wait_ge(summed, u + 1)
                    if p > 1:
                        act.wait_ge(added, u - LAG + 1)
                    act.activation(A[:, h, c0:HALF], m.psum[bank][:, c0:HALF], ACT.Exp).then_inc(weighed, 1)

            logs(0)
            logs(1)
            for p in range(len(steps)):
                weights(p)
                if p + 2 < len(steps):
                    logs(p + 2)


def gather_stage(m, sc, gz, y_sb, first):
    nc = m.nc
    hi, lo, turned = m.sem("gather_hi"), m.sem("gather_lo"), m.sem("gather_turned")
    gn = ROW["w_gdn_norm_2"]
    direct = [(0, sc[:, 0, :]), (1, sc[:, 1, :]), (6, y_sb[:, 0, :]), (7, y_sb[:, 1, :])]
    with nc.Block() as block:
        @block.sync
        def _(sp):
            load_first(m, sp, m.slices, first)

        @block.gpsimd
        def _(pool):
            split_first(m, pool, m.slices)

        @block.tensor
        def _(pe):
            for i in range(8):
                h, k = i // 4, i % 4
                for j in range(4):
                    mm = pe.transpose(m.psum[i][:, j * P:(j + 1) * P], gz[:, 4 * h + j, k * P:(k + 1) * P], m.ident[:, :])
                mm.then_inc(turned, 1)

        @block.scalar
        def _(act):
            for k, src in direct:
                act.activation(m.xt_hi[:, k, :], src, ACT.Copy).then_inc(hi, 1)
            for i in range(8):
                h, k = i // 4, i % 4
                act.wait_ge(turned, i + 1)
                act.activation(m.xt_hi[:, 2 + k, h * HALF:(h + 1) * HALF], m.psum[i][:, :], ACT.Identity,
                               scale=m.cols[:, gn:gn + 1]).then_inc(hi, 1)

        @block.vector
        def _(dve):
            for n, (k, src) in enumerate(direct):
                dve.wait_ge(hi, n + 1)
                dve.tensor_tensor(m.xt_lo[:, k, :], src, m.xt_hi[:, k, :].bitcast(F32), ALU.subtract).then_inc(lo, 1)
            for i in range(8):
                h, k = i // 4, i % 4
                tok = slice(h * HALF, (h + 1) * HALF)
                dve.wait_ge(hi, 4 + i + 1)
                dve.scalar_tensor_tensor(m.xt_lo[:, 2 + k, tok], m.psum[i][:, :], m.cols[:, gn:gn + 1],
                                         m.xt_hi[:, 2 + k, tok].bitcast(F32), ALU.mult, ALU.subtract).then_inc(lo, 1)


def whole_norm_stage(m, x_sb, gain, out):
    nc = m.nc
    r = m.norms
    ss, rstd = m.at(f"ss_whole{r}", [P, 16], 60), m.at(f"rstd_whole{r}", [P, 16], 60.125)
    junk_a, junk_d = m.at(f"junk_whole_a{r}", [P, D], 48), m.at(f"junk_whole_d{r}", [P, D], 52)
    g = m.at(f"gain_whole{r}", [P, D], 56)
    sq_d = m.squares["dve"]
    in_g, done, stored = (m.sem(f"{n}{r}") for n in ("in_gain", "normed", "stored"))
    with nc.Block() as block:
        @block.sync
        def _(sp):
            sp.dma_start(g[:, :], gain.rearrange("(a n) -> a n", a=1).to_broadcast([P, D])).then_inc(in_g, 16)
            for t in range(NT):
                sp.wait_ge(done, t + 1)
                sp.dma_start(out[t * P:(t + 1) * P, :], x_sb[:, t, :]).then_inc(stored, 16)
            sp.wait_ge(stored, 16 * NT)

        @block.scalar
        def _(act):
            for half in range(2):
                square_sums(m, act, "act", whole(x_sb), 1, ss, junk_a, norm_tiles(half, "act"))
                inverse_rms(m, act, 1, ss, rstd, half, sq_d + 2 * (half + 1))

        @block.vector
        def _(dve):
            for half in range(2):
                square_sums(m, dve, "dve", whole(x_sb), 1, ss, junk_d, norm_tiles(half, "dve"))
            dve.wait_ge(in_g, 16)
            for t in range(NT):
                if t % 4 == 0:
                    dve.wait_ge(m.norm_rstd, 2 * r + t // 4 + 1)
                dve.scalar_tensor_tensor(x_sb[:, t, :], x_sb[:, t, :], rstd[:, t:t + 1], g[:, :],
                                         ALU.mult, ALU.mult).then_inc(done, 1)
    m.norms += 1


def by_tile(ap):
    return ap.rearrange("(t p) n -> p t n", p=P)


def whole(tile):
    return lambda t, c0, c1: tile[:, t, c0:c1]


def program(m, out):
    a = m.a
    x_sb = m.at("x_sb", [P, NT, D], 120)
    spare = m.at("spare", [P, NT, D], 0)
    w_s_raw = m.at("w_s_raw", [P, 8, P], 184)
    w_sT = m.at("w_sT", [P, 8, P], 16)
    start_stage(m, x_sb, w_s_raw, w_sT)
    spare1 = m.at("x_scaled", [P, NT, D], 152)
    norm_stage(m, whole(x_sb), whole(spare1), 1, ROW["mix_norm_g"], 6,
               columns_of(m, a["w_in"][0], 1544))
    zu, zv = m.at("zu", [P, NT, 512], 120), m.at("zv", [P, NT, 512], 136)
    v = m.at("v", [P, NT, 512], 152)
    q, k_ = m.at("q", [P, 4, S], 168), m.at("k", [P, 4, S], 184)
    sp_f, csum = m.at("sp_f", [8, 3, S], 20), m.at("csum", [8, S], 4)
    proj1_stage(m, zu, zv, v, q, k_, sp_f, csum)
    mix1_stage(m, zv, zu, zu, zv, v, q, k_, csum, w_sT)

    def merged(t, c0, c1):
        return zv[:, t, c0:c1] if c1 <= 512 else zu[:, t, c0 - 512:c1 - 512]

    norm_stage(m, merged, merged, 2, ROW["out_norm_g"], 6, columns_of(m, a["w_out"][0], 0))
    out_proj_stage(m, a["w_out"][0], x_sb, a["x"][0])
    norm_stage(m, whole(x_sb), whole(spare), 1, ROW["ffn_norm_g"], 152, up_first(m, a["w_gate_up"][0]))
    ffn_stage(m, a["w_gate_up"][0], a["w_down"][0], x_sb, False)

    x_dram = m.nc.dram_tensor("x_between", [S, D], F32, kind="Internal").ap()
    whole_norm_stage(m, x_sb, a["final_norm_g"], x_dram)
    norm_stage(m, whole(x_sb), whole(spare), 1, ROW["w_norm_mix_2"], 152,
               columns_of(m, a["w_mix_in_2"][0], 0))
    sc = m.at("sc", [P, 6, S], 0)
    qkv = m.at("qkv", [P, 12, S], 120)
    gz = m.at("gz", [P, NT, 512], 168)
    sqk, sv = m.at("sqk", [P, 4, S], 8), m.at("sv", [P, 2, S], 24)
    ab = m.at("ab", [8, S], 192)
    proj2_stage(m, sc, qkv, gz, sqk, sv, ab)
    t_at = {"a_t": m.at("a_t", [P, HG, NT, P], 32), "kd": m.at("kd", [P, HG, NT, P], 48),
            "elast": m.at("elast", [P, HG, NT], 118.75)}
    heads = [qkv[:, 4 * i:4 * i + 4, :] for i in range(3)]
    delta_stage(m, *heads, ab, t_at)
    scan_stage(m, *heads, t_at, gz)
    y_sb = m.at("y_sb", [P, 2, S], 184)
    stick_stage(m, sqk, sv, y_sb)
    gather_stage(m, sc, gz, y_sb, columns_of(m, a["w_mix_out_2"][0], 0))
    out_proj_stage(m, a["w_mix_out_2"][0], x_sb, x_dram)
    norm_stage(m, whole(x_sb), whole(spare), 1, ROW["w_norm_ffn_2"], 152, up_first(m, a["w_ffn_up_2"][0]))
    ffn_stage(m, a["w_ffn_up_2"][0], a["w_ffn_down_2"][0], x_sb, True)
    whole_norm_stage(m, x_sb, a["w_norm_final_2"], out)


def build(nc, out, **arrays):
    with ExitStack() as ctx:
        program(setup(nc, ctx, arrays), out.rearrange("a t n -> (a t) n"))


_INS = ["x", "mix_norm_g", "w_in", "b_f", "sgu_ln_g", "sgu_ln_b", "w_s", "b_s", "out_norm_g", "w_out", "ffn_norm_g",
        "w_gate_up", "w_down", "final_norm_g", "w_norm_mix_2", "w_mix_in_2", "w_sconv_2", "w_gdn_conv_2",
        "gdn_a_log_2", "gdn_dt_bias_2", "w_gdn_norm_2", "w_mix_out_2", "w_norm_ffn_2", "w_ffn_up_2",
        "w_ffn_conv_2", "w_ffn_down_2", "w_norm_final_2"]


def kernel(**inputs):
    import numpy as _np
    import concourse.bacc as _bacc
    from concourse import mybir as _mybir
    from concourse.bass_utils import run_bass_kernel_spmd as _run

    nc = _bacc.Bacc("TRN2", target_bir_lowering=False, num_devices=1)
    arrays, args = {}, {}
    for name in _INS:
        arr = _np.ascontiguousarray(inputs[name])
        arrays[f"in_{name}_dram"] = arr
        args[name] = nc.dram_tensor(f"in_{name}_dram", arr.shape, _mybir.dt.from_np(arr.dtype), kind="ExternalInput").ap()
    out = nc.dram_tensor("out_0_dram", (1, S, D), _mybir.dt.float32, kind="ExternalOutput").ap()
    build(nc, out, **args)
    r = _run(nc, [arrays], core_ids=[0])
    return r.results[0]["out_0_dram"]
```
